# Optimizing a Trainium2 kernel written in Bass

```python
import math
import jax, jax.numpy as jnp
from jax import lax
import numpy as np
import jax
import jax.numpy as jnp

D_MODEL = 1024
BATCH = 1
SEQ = 512
DEPTH = 2

GRID_W = 64
CTX_LEN = 256
N_MIXERS = 3
HEAD_DIM = 64
ROPE_BASE = 10000.0
ROPE_PAIRS_PER_AXIS = HEAD_DIM // 4
Q_BLOCK = 128
NORM_EPS = 1e-6
NEG_INF = -1e30
DIFF_HEADS = D_MODEL // (2 * HEAD_DIM)
NA_HEADS = D_MODEL // HEAD_DIM
NA_KH_MAX = 8
NA_KW = 16
SWA_HEADS = D_MODEL // HEAD_DIM
SWA_KV_HEADS = SWA_HEADS // 4
SWA_WINDOW = 128
D_FF = 2816
CONV_W = 3
N_LAYERS_A = (DEPTH + N_MIXERS - 1) // N_MIXERS
N_LAYERS_B = (DEPTH + N_MIXERS - 2) // N_MIXERS
N_LAYERS_C = (DEPTH + N_MIXERS - 3) // N_MIXERS


def rmsnorm(t, g):
    tf = t.astype(jnp.float32)
    tf = tf * lax.rsqrt(jnp.mean(tf * tf, axis=-1, keepdims=True) + NORM_EPS)
    return tf.astype(t.dtype) * g

def rope_tables(n_tokens, dtype):
    t = jnp.arange(n_tokens, dtype=jnp.int32)
    row = (t // GRID_W).astype(jnp.float32)
    col = (t % GRID_W).astype(jnp.float32)
    inv = ROPE_BASE ** (-jnp.arange(ROPE_PAIRS_PER_AXIS, dtype=jnp.float32) / ROPE_PAIRS_PER_AXIS)
    ar = row[:, None] * inv[None, :]
    ac = col[:, None] * inv[None, :]
    return tuple(a.astype(dtype) for a in (jnp.cos(ar), jnp.sin(ar), jnp.cos(ac), jnp.sin(ac)))

def _rotate(t, cos, sin):
    t1, t2 = jnp.split(t, 2, axis=-1)
    return jnp.concatenate([t1 * cos - t2 * sin, t2 * cos + t1 * sin], axis=-1)

def rope_2d(t, tables):
    cr, sr, cc, sc = (a[None, :, None, :] for a in tables)
    half = HEAD_DIM // 2
    return jnp.concatenate([_rotate(t[..., :half], cr, sr), _rotate(t[..., half:], cc, sc)], axis=-1)

def _to_blocks(t, blk):
    b, s = t.shape[:2]
    return jnp.moveaxis(t.reshape(b, s // blk, blk, *t.shape[2:]), 1, 0)

def _from_blocks(t):
    t = jnp.moveaxis(t, 0, 1)
    return t.reshape(t.shape[0], t.shape[1] * t.shape[2], *t.shape[3:])

def _diff_attend(q, k, v, lam, subln, lam_init):
    s = jnp.einsum('bqhjd,bkhjd->bhjqk', q, k).astype(jnp.float32) * (HEAD_DIM ** -0.5)
    p = jax.nn.softmax(s, axis=-1)
    a = (p[:, :, 0] - lam * p[:, :, 1]).astype(v.dtype)
    o = jnp.einsum('bhqk,bkhe->bqhe', a, v)
    o = rmsnorm(o, subln) * (1.0 - lam_init)
    return o.reshape(o.shape[0], o.shape[1], -1)

def diff_attention(h, hc, wqkv, wo, lam_vecs, subln, layer_idx, tables, need_ctx):
    B, S, _ = h.shape
    H, dh = DIFF_HEADS, HEAD_DIM
    lam_init = 0.8 - 0.6 * math.exp(-0.3 * layer_idx)
    lv = lam_vecs.astype(jnp.float32)
    lam = jnp.exp(jnp.sum(lv[0] * lv[1])) - jnp.exp(jnp.sum(lv[2] * lv[3])) + lam_init

    def proj(t):
        n = t.shape[1]
        q, k, v = jnp.split(t @ wqkv, 3, axis=-1)
        return q.reshape(B, n, 2 * H, dh), k.reshape(B, n, 2 * H, dh), v.reshape(B, n, H, 2 * dh)

    q, k, v = proj(h)
    q, k = rope_2d(q, tables), rope_2d(k, tables)
    qc, kc, vc = proj(hc)
    q = q.reshape(B, S, H, 2, dh)
    k = k.reshape(B, S, H, 2, dh)
    n_ctx = hc.shape[1]
    qc = qc.reshape(B, n_ctx, H, 2, dh)
    kc = kc.reshape(B, n_ctx, H, 2, dh)
    k_all = jnp.concatenate([k, kc], axis=1)
    v_all = jnp.concatenate([v, vc], axis=1)
    y = _from_blocks(lax.map(lambda qb: _diff_attend(qb, k_all, v_all, lam, subln, lam_init),
                             _to_blocks(q, Q_BLOCK))) @ wo
    yc = (_diff_attend(qc, kc, vc, lam, subln, lam_init) @ wo) if need_ctx else None
    return y, yc

def _mha(q, k, v, mask=None, bias=None):
    s = jnp.einsum('bqhd,bkhd->bhqk', q, k).astype(jnp.float32) * (q.shape[-1] ** -0.5)
    if bias is not None:
        s = s + bias
    if mask is not None:
        s = jnp.where(mask, s, NEG_INF)
    p = jax.nn.softmax(s, axis=-1).astype(v.dtype)
    return jnp.einsum('bhqk,bkhd->bqhd', p, v)

def neighbourhood_attention(h, hc, wqkv, wo, rpb, need_ctx):
    B, S, _ = h.shape
    H, dh = NA_HEADS, HEAD_DIM
    rows = S // GRID_W
    kh = min(NA_KH_MAX, rows)
    kw = NA_KW

    def proj(t):
        n = t.shape[1]
        q, k, v = jnp.split(t @ wqkv, 3, axis=-1)
        return q.reshape(B, n, H, dh), k.reshape(B, n, H, dh), v.reshape(B, n, H, dh)

    q, k, v = proj(h)
    qc, kc, vc = proj(hc)
    n_ctx = hc.shape[1]
    kg = k.reshape(B, rows, GRID_W, H, dh)
    vg = v.reshape(B, rows, GRID_W, H, dh)
    col = jnp.arange(GRID_W, dtype=jnp.int32)
    col_start = jnp.clip(col - kw // 2, 0, GRID_W - kw)
    col_ok = (col[None, :] >= col_start[:, None]) & (col[None, :] < col_start[:, None] + kw)
    dx_idx = jnp.clip(col[None, :] - col[:, None], -(kw - 1), kw - 1) + (kw - 1)
    mask = jnp.concatenate(
        [jnp.broadcast_to(col_ok[:, None, :], (GRID_W, kh, GRID_W)).reshape(GRID_W, kh * GRID_W),
         jnp.ones((GRID_W, n_ctx), dtype=bool)], axis=-1)
    rpb32 = rpb.astype(jnp.float32)
    ctx_bias = jnp.zeros((H, GRID_W, n_ctx), jnp.float32)

    def row_block(args):
        r, q_row = args
        rs = jnp.clip(r - kh // 2, 0, rows - kh)
        k_win = lax.dynamic_slice_in_dim(kg, rs, kh, axis=1).reshape(B, kh * GRID_W, H, dh)
        v_win = lax.dynamic_slice_in_dim(vg, rs, kh, axis=1).reshape(B, kh * GRID_W, H, dh)
        dy_idx = rs + jnp.arange(kh, dtype=jnp.int32) - r + (NA_KH_MAX - 1)
        bias = rpb32[:, dy_idx[None, :, None], dx_idx[:, None, :]].reshape(H, GRID_W, kh * GRID_W)
        bias = jnp.concatenate([bias, ctx_bias], axis=-1)
        o = _mha(q_row, jnp.concatenate([k_win, kc], axis=1), jnp.concatenate([v_win, vc], axis=1),
                 mask, bias)
        return o.reshape(B, GRID_W, H * dh)

    q_rows = jnp.moveaxis(q.reshape(B, rows, GRID_W, H, dh), 1, 0)
    y = _from_blocks(lax.map(row_block, (jnp.arange(rows, dtype=jnp.int32), q_rows))) @ wo
    yc = (_mha(qc, kc, vc).reshape(B, n_ctx, H * dh) @ wo) if need_ctx else None
    return y, yc

def _gqa_sink(q, k, v, sink, mask=None):
    s = jnp.einsum('bqkgd,bmkd->bkgqm', q, k).astype(jnp.float32) * (HEAD_DIM ** -0.5)
    if mask is not None:
        s = jnp.where(mask, s, NEG_INF)
    b, kv, g, n, _ = s.shape
    s = jnp.concatenate([s, jnp.broadcast_to(sink[None, :, :, None, None], (b, kv, g, n, 1))], axis=-1)
    p = jax.nn.softmax(s, axis=-1)[..., :-1].astype(v.dtype)
    o = jnp.einsum('bkgqm,bmkd->bqkgd', p, v)
    return o.reshape(b, n, -1)

def window_gqa_sink(h, hc, wqkv, wo, sinks, tables, need_ctx):
    B, S, _ = h.shape
    H, KV, dh = SWA_HEADS, SWA_KV_HEADS, HEAD_DIM
    G = H // KV
    n_ctx = hc.shape[1]

    def proj(t):
        n = t.shape[1]
        q, k, v = jnp.split(t @ wqkv, [H * dh, (H + KV) * dh], axis=-1)
        return q.reshape(B, n, H, dh), k.reshape(B, n, KV, dh), v.reshape(B, n, KV, dh)

    q, k, v = proj(h)
    q, k = rope_2d(q, tables), rope_2d(k, tables)
    q = q.reshape(B, S, KV, G, dh)
    qc, kc, vc = proj(hc)
    qc = qc.reshape(B, n_ctx, KV, G, dh)
    sink = sinks.astype(jnp.float32).reshape(KV, G)

    pad = SWA_WINDOW
    kp = jnp.pad(k, ((0, 0), (pad, pad), (0, 0), (0, 0)))
    vp = jnp.pad(v, ((0, 0), (pad, pad), (0, 0), (0, 0)))
    span = Q_BLOCK + 2 * pad
    qi = jnp.arange(Q_BLOCK, dtype=jnp.int32)
    kj = jnp.arange(span, dtype=jnp.int32)
    band = (kj[None, :] >= qi[:, None]) & (kj[None, :] <= qi[:, None] + 2 * SWA_WINDOW)
    ctx_ok = jnp.ones((Q_BLOCK, n_ctx), dtype=bool)

    def block(args):
        n, q_blk = args
        start = n * Q_BLOCK
        k_loc = lax.dynamic_slice_in_dim(kp, start, span, axis=1)
        v_loc = lax.dynamic_slice_in_dim(vp, start, span, axis=1)
        kpos = start - pad + kj
        valid = band & ((kpos >= 0) & (kpos < S))[None, :]
        mask = jnp.concatenate([valid, ctx_ok], axis=-1)
        return _gqa_sink(q_blk, jnp.concatenate([k_loc, kc], axis=1),
                         jnp.concatenate([v_loc, vc], axis=1), sink, mask)

    nb = S // Q_BLOCK
    y = _from_blocks(lax.map(block, (jnp.arange(nb, dtype=jnp.int32), _to_blocks(q, Q_BLOCK)))) @ wo
    yc = (_gqa_sink(qc, kc, vc, sink) @ wo) if need_ctx else None
    return y, yc

def conv_ffn(t, w_up, w_conv, b_conv, w_down):
    n = t.shape[1]
    u = t @ w_up
    half = CONV_W // 2
    up = jnp.pad(u, ((0, 0), (half, half), (0, 0)))
    acc = b_conv
    for tap in range(CONV_W):
        acc = acc + up[:, tap:tap + n] * w_conv[tap]
    a, g = jnp.split(acc, 2, axis=-1)
    return (jax.nn.silu(g) * a) @ w_down

def first_inputs(seed: int = 0) -> dict:
    key = jax.random.key(seed)
    ks = iter(jax.random.split(key, 32))

    def nrm(shape, scale):
        return jax.random.normal(next(ks), shape, jnp.float32) * scale

    D = D_MODEL
    s = D ** -0.5
    return {
        "x": nrm((BATCH, SEQ, D), 1.0),
        "c": nrm((BATCH, D), 1.0),
        "ctx": nrm((BATCH, CTX_LEN, D), 1.0),
        "c_ctx": nrm((D,), 1.0),
        "ada_w": nrm((DEPTH, D, 6 * D), s),
        "ada_b": nrm((DEPTH, 6 * D), 0.02),
        "norm_mix": 1.0 + nrm((DEPTH, D), 0.05),
        "norm_ffn": 1.0 + nrm((DEPTH, D), 0.05),
        "norm_out": 1.0 + nrm((D,), 0.05),
        "ffn_up": nrm((DEPTH, D, 2 * D_FF), s),
        "ffn_conv": nrm((DEPTH, CONV_W, 2 * D_FF), CONV_W ** -0.5),
        "ffn_conv_b": nrm((DEPTH, 2 * D_FF), 0.02),
        "ffn_down": nrm((DEPTH, D_FF, D), D_FF ** -0.5),
        "a_wqkv": nrm((N_LAYERS_A, D, 3 * D), s),
        "a_wo": nrm((N_LAYERS_A, D, D), s),
        "a_lambda": nrm((N_LAYERS_A, 4, HEAD_DIM), 0.1),
        "a_subln": 1.0 + nrm((N_LAYERS_A, 2 * HEAD_DIM), 0.05),
        "b_wqkv": nrm((N_LAYERS_B, D, 3 * D), s),
        "b_wo": nrm((N_LAYERS_B, D, D), s),
        "b_rpb": nrm((N_LAYERS_B, NA_HEADS, 2 * NA_KH_MAX - 1, 2 * NA_KW - 1), 0.5),
        "c_wqkv": nrm((N_LAYERS_C, D, (SWA_HEADS + 2 * SWA_KV_HEADS) * HEAD_DIM), s),
        "c_wo": nrm((N_LAYERS_C, D, D), s),
        "c_sinks": nrm((N_LAYERS_C, SWA_HEADS), 0.5),
    }

def first_block(x, c, ctx, c_ctx, ada_w, ada_b, norm_mix, norm_ffn, norm_out,
              ffn_up, ffn_conv, ffn_conv_b, ffn_down,
              a_wqkv, a_wo, a_lambda, a_subln,
              b_wqkv, b_wo, b_rpb,
              c_wqkv, c_wo, c_sinks):
    S = x.shape[1]
    tables = rope_tables(S, x.dtype)
    xc = ctx
    silu_c = jax.nn.silu(c)
    silu_cc = jax.nn.silu(c_ctx)
    for i in range(DEPTH):
        need_ctx = i < DEPTH - 1
        kind, j = i % N_MIXERS, i // N_MIXERS
        sh1, sc1, g1, sh2, sc2, g2 = jnp.split((silu_c @ ada_w[i] + ada_b[i])[:, None, :], 6, axis=-1)
        csh1, csc1, cg1, csh2, csc2, cg2 = jnp.split(silu_cc @ ada_w[i] + ada_b[i], 6, axis=-1)
        h = rmsnorm(x, norm_mix[i]) * (1.0 + sc1) + sh1
        hc = rmsnorm(xc, norm_mix[i]) * (1.0 + csc1) + csh1
        if kind == 0:
            y, yc = diff_attention(h, hc, a_wqkv[j], a_wo[j], a_lambda[j], a_subln[j], i, tables, need_ctx)
        elif kind == 1:
            y, yc = neighbourhood_attention(h, hc, b_wqkv[j], b_wo[j], b_rpb[j], need_ctx)
        else:
            y, yc = window_gqa_sink(h, hc, c_wqkv[j], c_wo[j], c_sinks[j], tables, need_ctx)
        x = x + g1 * y
        h2 = rmsnorm(x, norm_ffn[i]) * (1.0 + sc2) + sh2
        x = x + g2 * conv_ffn(h2, ffn_up[i], ffn_conv[i], ffn_conv_b[i], ffn_down[i])
        if need_ctx:
            xc = xc + cg1 * yc
            hc2 = rmsnorm(xc, norm_ffn[i]) * (1.0 + csc2) + csh2
            xc = xc + cg2 * conv_ffn(hc2, ffn_up[i], ffn_conv[i], ffn_conv_b[i], ffn_down[i])
    return rmsnorm(x, norm_out)


DEPTH_2 = 1

CHUNK = 64
F_TINY = 1e-30

DN_HEADS = 4
DN_DK = 128
DN_DV = 128
DN_QK = DN_HEADS * DN_DK
DN_V = DN_HEADS * DN_DV
CONV_K = 3

HG_HEADS = 4
HG_DK = 128
HG_DV = 128
HG_K = HG_HEADS * HG_DK
HG_V = HG_HEADS * HG_DV

N_GROUPS = 4
EXPERTS_PER_GROUP = 8
N_EXPERTS = N_GROUPS * EXPERTS_PER_GROUP
TOP_K_IN_GROUP = 2
D_EXPERT = D_MODEL // 2
MOE_BLOCK = 128

IN_SIZES = (2 * DN_QK + DN_V, DN_V, 2 * DN_HEADS, 2 * DN_HEADS, HG_K, 2 * HG_K, HG_V, HG_V, 2 * D_MODEL)
IN_SPLITS = tuple(sum(IN_SIZES[:i + 1]) for i in range(len(IN_SIZES) - 1))
N_IN = sum(IN_SIZES)


F32 = jnp.float32

def _rmsnorm(x, g):
    xf = x.astype(F32)
    y = xf * lax.rsqrt(jnp.mean(xf * xf, axis=-1, keepdims=True) + NORM_EPS)
    return (y * g.astype(F32)).astype(x.dtype)

def _l2norm(x):
    xf = x.astype(F32)
    return xf * lax.rsqrt(jnp.sum(xf * xf, axis=-1, keepdims=True) + NORM_EPS)

def _masked_exp(diff, mask):
    return jnp.where(mask, jnp.exp(jnp.where(mask, diff, 0.0)), 0.0)

def _gated_rmsnorm(o, z, g):
    bsz, n, h, dv = o.shape
    y = o * lax.rsqrt(jnp.mean(o * o, axis=-1, keepdims=True) + NORM_EPS) * g.astype(F32)
    y = y * jax.nn.silu(z.astype(F32).reshape(bsz, n, h, dv))
    return y.reshape(bsz, n, h * dv).astype(z.dtype)

def _short_conv(x, w):
    pad = CONV_K // 2
    return lax.conv_general_dilated(x, w[:, None, :].astype(x.dtype), window_strides=(1,),
                                    padding=[(pad, pad)], dimension_numbers=('NWC', 'WIO', 'NWC'),
                                    feature_group_count=x.shape[-1])

def _to_col_major(t):
    bsz, n, f = t.shape
    rows = n // GRID_W
    return t.reshape(bsz, rows, GRID_W, f).transpose(0, 2, 1, 3).reshape(bsz, n, f)

def _from_col_major(t):
    bsz, n, f = t.shape
    rows = n // GRID_W
    return t.reshape(bsz, GRID_W, rows, f).transpose(0, 2, 1, 3).reshape(bsz, n, f)

def _rev(t, direction):
    return jnp.flip(t, axis=1) if direction == 1 else t

def _to_chunks(t):
    bsz, n, h = t.shape[:3]
    t = t.reshape(bsz, n // CHUNK, CHUNK, h, *t.shape[3:])
    return jnp.moveaxis(t, (1, 3), (0, 2))

def _from_chunks(t):
    t = jnp.moveaxis(t, (0, 2), (1, 3))
    return t.reshape(t.shape[0], t.shape[1] * t.shape[2], *t.shape[3:])

def gated_delta_chunked(q, k, v, g, beta, s0, return_out):
    q, k, v, g, beta = (_to_chunks(t.astype(F32)) for t in (q, k, v, g, beta))
    dv = v.shape[-1]
    incl = jnp.tril(jnp.ones((CHUNK, CHUNK), bool))
    strict = jnp.tril(jnp.ones((CHUNK, CHUNK), bool), -1)
    gcum = jnp.cumsum(g, axis=-1)
    decay = _masked_exp(gcum[..., :, None] - gcum[..., None, :], incl)
    kb = k * beta[..., None]
    a = jnp.where(strict, jnp.einsum('nbhik,nbhjk->nbhij', kb, k) * decay, 0.0)
    rhs = jnp.concatenate([v * beta[..., None], kb * jnp.exp(gcum)[..., None]], axis=-1)
    sol = lax.linalg.triangular_solve(a, rhs, left_side=True, lower=True, unit_diagonal=True)
    u, w = sol[..., :dv], sol[..., dv:]

    def step(s, inp):
        qc, kc, uc, wc, gc, dc = inp
        v_new = uc - jnp.einsum('bhck,bhkv->bhcv', wc, s)
        g_last = gc[..., -1]
        s_new = s * jnp.exp(g_last)[..., None, None] + jnp.einsum(
            'bhck,bhcv->bhkv', kc * jnp.exp(g_last[..., None] - gc)[..., None], v_new)
        if not return_out:
            return s_new, None
        o = jnp.einsum('bhck,bhkv->bhcv', qc * jnp.exp(gc)[..., None], s) + jnp.einsum(
            'bhij,bhjv->bhiv', jnp.einsum('bhik,bhjk->bhij', qc, kc) * dc, v_new)
        return s_new, o

    s_fin, o = lax.scan(step, s0.astype(F32), (q, k, u, w, gcum, decay))
    return (_from_chunks(o) if return_out else None), s_fin

def gla_chunked(q, k, v, log_f, s0, return_out):
    q, k, v, log_f = (_to_chunks(t.astype(F32)) for t in (q, k, v, log_f))
    gcum = jnp.cumsum(log_f, axis=3)
    incl = jnp.tril(jnp.ones((CHUNK, CHUNK), bool))[..., None]

    def step(s, inp):
        qc, kc, vc, gc = inp
        g_last = gc[:, :, -1]
        s_new = s * jnp.exp(g_last)[..., None] + jnp.einsum(
            'bhck,bhcv->bhkv', kc * jnp.exp(g_last[:, :, None] - gc), vc)
        if not return_out:
            return s_new, None
        rel = _masked_exp(gc[:, :, :, None] - gc[:, :, None], incl)
        att = jnp.einsum('bhik,bhjk,bhijk->bhij', qc, kc, rel)
        o = jnp.einsum('bhck,bhkv->bhcv', qc * jnp.exp(gc), s) + jnp.einsum('bhij,bhjv->bhiv', att, vc)
        return s_new, o

    s_fin, o = lax.scan(step, s0.astype(F32), (q, k, v, gcum))
    return (_from_chunks(o) if return_out else None), s_fin

def _dn_inputs(qkv, b, a, conv_w, a_log, dt_bias):
    bsz, n = qkv.shape[:2]
    qkv = jax.nn.silu(_short_conv(qkv, conv_w))
    q, k, v = jnp.split(qkv, [DN_QK, 2 * DN_QK], axis=-1)
    q = _l2norm(q.reshape(bsz, n, DN_HEADS, DN_DK)) * (DN_DK ** -0.5)
    k = _l2norm(k.reshape(bsz, n, DN_HEADS, DN_DK))
    v = v.reshape(bsz, n, DN_HEADS, DN_DV)
    beta = jax.nn.sigmoid(b.astype(F32).reshape(bsz, n, 2, DN_HEADS))
    g = -jnp.exp(a_log.astype(F32)) * jax.nn.softplus(
        a.astype(F32).reshape(bsz, n, 2, DN_HEADS) + dt_bias.astype(F32))
    return q, k, v, beta, g

def _deltanet_scans(lat, ctx, ctx_out):
    xq, xk, xv, xb, xg = lat
    cq, ck, cv, cb, cg = ctx
    o_x, o_c = 0.0, 0.0
    for d in range(2):
        s0 = jnp.zeros((xq.shape[0], DN_HEADS, DN_DK, DN_DV), F32)
        oc, s_ctx = gated_delta_chunked(*(_rev(t, d) for t in (cq, ck, cv, cg[:, :, d], cb[:, :, d])), s0, ctx_out)
        ox, _ = gated_delta_chunked(*(_rev(t, d) for t in (xq, xk, xv, xg[:, :, d], xb[:, :, d])), s_ctx, True)
        o_x = o_x + _rev(ox, d)
        if ctx_out:
            o_c = o_c + _rev(oc, d)
    return o_x, (o_c if ctx_out else None)

def _hg_inputs(q, f2, i, lb):
    bsz, n = q.shape[:2]
    q = jax.nn.silu(q.astype(F32)).reshape(bsz, n, HG_HEADS, HG_DK)
    z = f2.astype(F32).reshape(bsz, n, 2, HG_HEADS, HG_DK)
    f = lb + (1.0 - lb) * jax.nn.sigmoid(z)
    log_f = jnp.log(jnp.maximum(f, F_TINY))
    k = (1.0 - lb) * jax.nn.sigmoid(-z)
    v = i.astype(F32).reshape(bsz, n, HG_HEADS, HG_DV)
    return q, k, log_f, v

def _hgrn2_scans(lat, ctx, ctx_out):
    xq, xk, xlf, xv = lat
    cq, ck, clf, cv = ctx
    o_x, o_c = 0.0, 0.0
    for d in range(2):
        s0 = jnp.zeros((xq.shape[0], HG_HEADS, HG_DK, HG_DV), F32)
        oc, s_ctx = gla_chunked(*(_rev(t, d) for t in (cq, ck[:, :, d], cv, clf[:, :, d])), s0, ctx_out)
        ox, _ = gla_chunked(*(_rev(t, d) for t in (xq, xk[:, :, d], xv, xlf[:, :, d])), s_ctx, True)
        o_x = o_x + _rev(ox, d)
        if ctx_out:
            o_c = o_c + _rev(oc, d)
    return o_x, (o_c if ctx_out else None)

def hybrid_mixer(hx, hc, w_in, dn_conv, dn_a_log, dn_dt_bias, dn_norm_g, lb, hg_norm_g,
                 w_br_dn, w_br_hg, w_out, ctx_out):
    bsz, n_lat = hx.shape[:2]
    n_ctx = hc.shape[1]
    proj = jnp.concatenate([hc, hx], axis=1) @ w_in
    pc = jnp.split(proj[:, :n_ctx], IN_SPLITS, axis=-1)
    px = jnp.split(proj[:, n_ctx:], IN_SPLITS, axis=-1)
    odn_x, odn_c = _deltanet_scans(_dn_inputs(px[0], px[2], px[3], dn_conv, dn_a_log, dn_dt_bias),
                                   _dn_inputs(pc[0], pc[2], pc[3], dn_conv, dn_a_log, dn_dt_bias), ctx_out)
    ohg_x, ohg_c = _hgrn2_scans(_hg_inputs(*(_to_col_major(t) for t in (px[4], px[5], px[6])), lb),
                                _hg_inputs(pc[4], pc[5], pc[6], lb), ctx_out)
    ohg_x = _from_col_major(ohg_x.reshape(bsz, n_lat, HG_V)).reshape(bsz, n_lat, HG_HEADS, HG_DV)

    def merge(parts, odn, ohg):
        br_dn = _gated_rmsnorm(odn, parts[1], dn_norm_g) @ w_br_dn
        br_hg = _gated_rmsnorm(ohg, parts[7], hg_norm_g) @ w_br_hg
        gate_dn, gate_hg = jnp.split(parts[8], 2, axis=-1)
        return (jax.nn.sigmoid(gate_dn) * br_dn + jax.nn.sigmoid(gate_hg) * br_hg) @ w_out

    y_x = merge(px, odn_x, ohg_x)
    y_c = merge(pc, odn_c, ohg_c) if ctx_out else None
    return y_x, y_c

def hier_moe(h, w_rg, b_rg, w_re, b_re, w_gate, w_up, w_down):
    n_tok, d = h.shape
    grp_logits = (h @ w_rg + b_rg).astype(F32)
    grp_sel = jnp.argmax(grp_logits, axis=-1)
    grp_p = jnp.take_along_axis(jax.nn.softmax(grp_logits, axis=-1), grp_sel[:, None], axis=-1)
    exp_logits = (h @ w_re + b_re).astype(F32).reshape(n_tok, N_GROUPS, EXPERTS_PER_GROUP)
    in_logits = jnp.take_along_axis(exp_logits, grp_sel[:, None, None], axis=1)[:, 0]
    top_p, top_j = lax.top_k(jax.nn.softmax(in_logits, axis=-1), TOP_K_IN_GROUP)
    gate = grp_p * top_p / jnp.sum(top_p, axis=-1, keepdims=True)
    expert = grp_sel[:, None] * EXPERTS_PER_GROUP + top_j
    n_asg = n_tok * TOP_K_IN_GROUP
    e_flat = expert.reshape(n_asg)
    order = jnp.argsort(e_flat)
    e_sorted = e_flat[order]
    tok_sorted = order // TOP_K_IN_GROUP
    gate_sorted = gate.reshape(n_asg)[order]
    counts = jnp.bincount(e_flat, length=N_EXPERTS)
    padded = (counts + MOE_BLOCK - 1) // MOE_BLOCK * MOE_BLOCK
    pad_end = jnp.cumsum(padded)
    pad_start = pad_end - padded
    start = jnp.cumsum(counts) - counts
    dest = pad_start[e_sorted] + jnp.arange(n_asg) - start[e_sorted]
    n_blocks = (n_asg + N_EXPERTS * (MOE_BLOCK - 1) + MOE_BLOCK - 1) // MOE_BLOCK
    rows = jnp.zeros((n_blocks * MOE_BLOCK, d), h.dtype).at[dest].set(h[tok_sorted])
    block_expert = jnp.minimum(jnp.searchsorted(pad_end, jnp.arange(n_blocks) * MOE_BLOCK, side='right'),
                               N_EXPERTS - 1)

    def expert_block(args):
        xb, e = args
        return (jax.nn.silu(xb @ w_gate[e]) * (xb @ w_up[e])) @ w_down[e]

    out = lax.map(expert_block, (rows.reshape(n_blocks, MOE_BLOCK, d), block_expert)).reshape(-1, d)
    contrib = (out[dest] * gate_sorted[:, None]).astype(h.dtype)
    return jnp.zeros((n_tok, d), h.dtype).at[tok_sorted].add(contrib)

def second_inputs(seed: int = 0) -> dict:
    key = jax.random.key(seed)
    ks = iter(jax.random.split(key, 26))
    D, L = D_MODEL, DEPTH_2

    def nrm(shape, scale):
        return jax.random.normal(next(ks), shape, F32) * scale

    x = nrm((BATCH, SEQ, D), 1.0)
    c = nrm((BATCH, D), 1.0)
    ctx = nrm((BATCH, CTX_LEN, D), 1.0)
    c_ctx = nrm((D,), 1.0)
    w_ada = nrm((L, D, 6 * D), 0.5 * D ** -0.5)
    b_ada = nrm((L, 6 * D), 0.02)
    g_mix = 1.0 + nrm((L, D), 0.02)
    g_ffn = 1.0 + nrm((L, D), 0.02)
    g_final = 1.0 + nrm((D,), 0.02)
    w_in = nrm((L, D, N_IN), D ** -0.5)
    dn_conv = nrm((L, CONV_K, 2 * DN_QK + DN_V), CONV_K ** -0.5)
    dn_a_log = jnp.log(jax.random.uniform(next(ks), (L, 2, DN_HEADS), F32, 1.0, 16.0))
    dt = jnp.exp(jax.random.uniform(next(ks), (L, 2, DN_HEADS), F32, math.log(1e-3), math.log(1e-1)))
    dn_dt_bias = dt + jnp.log(-jnp.expm1(-dt))
    dn_norm_g = 1.0 + nrm((L, DN_DV), 0.02)
    hg_lb_logits = nrm((L, HG_K), 0.5)
    hg_norm_g = 1.0 + nrm((L, HG_DV), 0.02)
    w_br_dn = nrm((L, DN_V, D), DN_V ** -0.5)
    w_br_hg = nrm((L, HG_V, D), HG_V ** -0.5)
    w_out = nrm((L, D, D), D ** -0.5)
    w_router_grp = nrm((L, D, N_GROUPS), D ** -0.5)
    b_router_grp = nrm((L, N_GROUPS), 0.01)
    w_router_exp = nrm((L, D, N_EXPERTS), D ** -0.5)
    b_router_exp = nrm((L, N_EXPERTS), 0.01)
    w_exp_gate = nrm((L, N_EXPERTS, D, D_EXPERT), D ** -0.5)
    w_exp_up = nrm((L, N_EXPERTS, D, D_EXPERT), D ** -0.5)
    w_exp_down = nrm((L, N_EXPERTS, D_EXPERT, D), D_EXPERT ** -0.5)
    return {'x': x, 'c': c, 'ctx': ctx, 'c_ctx': c_ctx, 'w_ada': w_ada, 'b_ada': b_ada,
            'g_mix': g_mix, 'g_ffn': g_ffn, 'g_final': g_final, 'w_in': w_in, 'dn_conv': dn_conv,
            'dn_a_log': dn_a_log, 'dn_dt_bias': dn_dt_bias, 'dn_norm_g': dn_norm_g,
            'hg_lb_logits': hg_lb_logits, 'hg_norm_g': hg_norm_g, 'w_br_dn': w_br_dn,
            'w_br_hg': w_br_hg, 'w_out': w_out, 'w_router_grp': w_router_grp,
            'b_router_grp': b_router_grp, 'w_router_exp': w_router_exp, 'b_router_exp': b_router_exp,
            'w_exp_gate': w_exp_gate, 'w_exp_up': w_exp_up, 'w_exp_down': w_exp_down}

def second_block(x, c, ctx, c_ctx, w_ada, b_ada, g_mix, g_ffn, g_final, w_in, dn_conv, dn_a_log,
              dn_dt_bias, dn_norm_g, hg_lb_logits, hg_norm_g, w_br_dn, w_br_hg, w_out,
              w_router_grp, b_router_grp, w_router_exp, b_router_exp, w_exp_gate, w_exp_up,
              w_exp_down):
    bsz, n_lat, d = x.shape
    n_ctx = ctx.shape[1]
    lb_w = jax.nn.softmax(hg_lb_logits.astype(F32), axis=0)
    lower_bounds = jnp.cumsum(lb_w, axis=0) - lb_w[0]
    s_c = jax.nn.silu(c)
    s_cc = jax.nn.silu(c_ctx)
    h_ctx = ctx
    for layer in range(DEPTH_2):
        last = layer == DEPTH_2 - 1
        mod_x = jnp.split((s_c @ w_ada[layer] + b_ada[layer])[:, None, :], 6, axis=-1)
        mod_c = jnp.split(s_cc @ w_ada[layer] + b_ada[layer], 6, axis=-1)
        hx = _rmsnorm(x, g_mix[layer]) * (1.0 + mod_x[1]) + mod_x[0]
        hc = _rmsnorm(h_ctx, g_mix[layer]) * (1.0 + mod_c[1]) + mod_c[0]
        y_x, y_c = hybrid_mixer(hx, hc, w_in[layer], dn_conv[layer], dn_a_log[layer], dn_dt_bias[layer],
                                dn_norm_g[layer], lower_bounds[layer].reshape(HG_HEADS, HG_DK),
                                hg_norm_g[layer], w_br_dn[layer], w_br_hg[layer], w_out[layer],
                                not last)
        x = x + mod_x[2] * y_x
        hx = (_rmsnorm(x, g_ffn[layer]) * (1.0 + mod_x[4]) + mod_x[3]).reshape(-1, d)
        moe_args = (w_router_grp[layer], b_router_grp[layer], w_router_exp[layer], b_router_exp[layer],
                    w_exp_gate[layer], w_exp_up[layer], w_exp_down[layer])
        if last:
            f_x = hier_moe(hx, *moe_args)
        else:
            h_ctx = h_ctx + mod_c[2] * y_c
            hc = (_rmsnorm(h_ctx, g_ffn[layer]) * (1.0 + mod_c[4]) + mod_c[3]).reshape(-1, d)
            f_all = hier_moe(jnp.concatenate([hc, hx], axis=0), *moe_args)
            h_ctx = h_ctx + mod_c[5] * f_all[:bsz * n_ctx].reshape(bsz, n_ctx, d)
            f_x = f_all[bsz * n_ctx:]
        x = x + mod_x[5] * f_x.reshape(bsz, n_lat, d)
    return _rmsnorm(x, g_final)


def setup_inputs(seed=0):
    out = dict(first_inputs(seed))
    for name, value in second_inputs(seed + 1).items():
        if name != "x":
            out[name + "_2"] = value
    return out


def reference(
    x, c, ctx, c_ctx, ada_w, ada_b, norm_mix, norm_ffn, norm_out, ffn_up, ffn_conv, ffn_conv_b,
    ffn_down, a_wqkv, a_wo, a_lambda, a_subln, b_wqkv, b_wo, b_rpb, c_wqkv, c_wo, c_sinks, c_2,
    ctx_2, c_ctx_2, w_ada_2, b_ada_2, g_mix_2, g_ffn_2, g_final_2, w_in_2, dn_conv_2,
    dn_a_log_2, dn_dt_bias_2, dn_norm_g_2, hg_lb_logits_2, hg_norm_g_2, w_br_dn_2, w_br_hg_2,
    w_out_2, w_router_grp_2, b_router_grp_2, w_router_exp_2, b_router_exp_2, w_exp_gate_2,
    w_exp_up_2, w_exp_down_2,
):
    x = first_block(
        x, c, ctx, c_ctx, ada_w, ada_b, norm_mix, norm_ffn, norm_out, ffn_up, ffn_conv,
        ffn_conv_b, ffn_down, a_wqkv, a_wo, a_lambda, a_subln, b_wqkv, b_wo, b_rpb, c_wqkv,
        c_wo, c_sinks,
    )
    return second_block(
        x, c_2, ctx_2, c_ctx_2, w_ada_2, b_ada_2, g_mix_2, g_ffn_2, g_final_2, w_in_2,
        dn_conv_2, dn_a_log_2, dn_dt_bias_2, dn_norm_g_2, hg_lb_logits_2, hg_norm_g_2,
        w_br_dn_2, w_br_hg_2, w_out_2, w_router_grp_2, b_router_grp_2, w_router_exp_2,
        b_router_exp_2, w_exp_gate_2, w_exp_up_2, w_exp_down_2,
    )


_drawn_inputs = setup_inputs


def setup_inputs(seed=0):
    import zlib

    import numpy as np

    out = dict(_drawn_inputs(seed))
    spreads = {}
    factors = {'ffn_conv_b': 2.927,
     'ctx_2': 6.583,
     'c_ctx_2': 8.0,
     'b_ada_2': 2.958,
     'g_mix_2': 7.435,
     'g_ffn_2': 4.584,
     'g_final_2': 7.38,
     'dn_norm_g_2': 8.0,
     'hg_norm_g_2': 8.0,
     'b_router_grp_2': 37.717,
     'b_router_exp_2': 43.872}
    for name, (base, spread) in spreads.items():
        noise = np.random.default_rng([zlib.crc32(name.encode()), seed]).standard_normal(out[name].shape)
        drawn = base * np.exp(spread * noise) if base else spread * noise
        out[name] = jnp.asarray(drawn.astype(out[name].dtype))
    for name, factor in factors.items():
        out[name] = (out[name] * factor).astype(out[name].dtype)
    return out
```

```python
from contextlib import ExitStack, contextmanager

import concourse.bass as bass
import numpy as np
from concourse import mybir
from concourse.alu_op_type import AluOpType as ALU

ACT = mybir.ActivationFunctionType
F32 = mybir.dt.float32
U32 = mybir.dt.uint32
I32 = mybir.dt.int32
AX_X = mybir.AxisListType.X

P = 128
D = 1024
KD = D // P
TX, TC = 512, 256
TT = TX + TC
NTX, NTC = TX // P, TC // P
NT = NTX + NTC
GRID_W = 64
GRID_H = TX // GRID_W
HD = 64
FF = 2816
NF = FF // P
EPS = 1e-6
NEG = -1e30
LAM_INIT = 0.8 - 0.6 * float(np.exp(-0.3 * 0))
KW = 16
KH = 8
NSLOT = 14
HEADS = 4
DNQKV = 3 * HEADS * P
C_Z_DN = DNQKV
C_BA = C_Z_DN + HEADS * P
C_HQ = C_BA + 16
C_HF = C_HQ + HEADS * P
C_HI = C_HF + 2 * HEADS * P
C_Z_HG = C_HI + HEADS * P
C_GATE = C_Z_HG + HEADS * P
N_IN = C_GATE + 2 * D
LEVELS = 7
NG, EPG = 4, 8
NE = NG * EPG
DE = D // 2
KE = DE // P
TOPK = 2
MB = 128
NBLK = (TX * TOPK + NE * (MB - 1) + MB - 1) // MB
F_TINY = 1e-30
LN_SHIFT = 60

VECS = {}
_at = 0
for _n, _k in (
    ("c", KD), ("c_ctx", KD), ("c2", KD), ("c_ctx2", KD),
    ("ada_b0", 48), ("ada_b1", 48), ("ada_b2", 48),
    ("norm_mix0", KD), ("norm_mix1", KD), ("norm_mix2", KD),
    ("norm_ffn0", KD), ("norm_ffn1", KD), ("norm_ffn2", KD), ("norm_out", KD), ("g_final", KD),
    ("conv0", 6 * NF), ("conv1", 6 * NF), ("conv_b0", 2 * NF), ("conv_b1", 2 * NF), ("dn_conv", 3 * 12),
    ("subln", 1), ("dn_norm", 1), ("hg_norm", 1),
):
    VECS[_n] = (_at, _k)
    _at += _k
N_VEC = _at
ROWS = {}
_at = 0
for _n, _k in (("lam", 4 * HD), ("a_log", 8), ("dt_bias", 8), ("b_router", NG + NE), ("lb", HEADS * P)):
    ROWS[_n] = (_at, _k)
    _at += _k
N_ROW = _at
CONST = {}
_at = 0
for _n, _k in (
    ("ident", P), ("ones", P), ("rot", P), ("incl", 2 * P), ("strict", 2 * P), ("level", 2 * LEVELS * P),
    ("cos", TX), ("sin", TX), ("window", GRID_W), ("group_rank", NG), ("expert_rank", EPG),
    ("blk", 1), ("tokid", NTX),
):
    CONST[_n] = (_at, _k)
    _at += _k
N_CONST = _at


def constants():
    out = np.zeros((P, N_CONST), np.float32)

    def put(name, a):
        at, k = CONST[name]
        out[:, at:at + k] = np.asarray(a, np.float32).reshape(P, k)

    i, j = np.arange(P)[None, :], np.arange(P)[:, None]
    put("ident", i == j)
    put("ones", np.ones((P, P)))
    rot = np.zeros((P, P))
    for b in range(0, P, 32):
        for e in range(16):
            rot[b + 16 + e, b + e] = -1
            rot[b + e, b + 16 + e] = 1
    put("rot", rot)
    put("incl", np.stack([j <= i, j >= i], 1))
    put("strict", np.stack([j < i, j > i], 1))
    level = np.zeros((P, 2, LEVELS, P))
    for n in range(LEVELS):
        s = 1 << n
        m = (j // (2 * s) == i // (2 * s)) & (j % (2 * s) < s) & (i % (2 * s) >= s)
        level[:, 0, n], level[:, 1, n] = m, m.T
    put("level", level)
    inv = np.float32(10000.0) ** (-np.arange(16, dtype=np.float32) / np.float32(16))
    t = np.arange(TX)
    row = (t // GRID_W).astype(np.float32)[:, None] * inv[None]
    col = (t % GRID_W).astype(np.float32)[:, None] * inv[None]
    ang = np.concatenate([row, row, col, col], 1).T
    ang = np.concatenate([ang, ang], 0)
    put("cos", np.cos(ang))
    put("sin", np.sin(ang))
    c = np.arange(GRID_W)
    start = np.clip(c - KW // 2, 0, GRID_W - KW)
    ok = (c[None] >= start[:, None]) & (c[None] < start[:, None] + KW)
    window = np.where(ok, 0.0, NEG)
    put("window", np.concatenate([window, window], 0))
    put("group_rank", np.tile(NG - np.arange(NG), (P, 1)))
    put("expert_rank", np.tile(EPG - np.arange(EPG), (P, 1)))
    put("blk", np.arange(P))
    put("tokid", np.arange(P)[:, None] + P * np.arange(NTX)[None])
    return out


class Core:

    def __init__(self, nc):
        self.nc, self.n, self.fresh, self.spent = nc, 0, [], []

    def sem(self, name):
        self.n += 1
        self.fresh.append(self.nc.alloc_semaphore(f"{name}_{self.n}"))
        return self.fresh[-1]

    def sb(self, ctx, name, shape, dt=F32):
        self.n += 1
        return ctx.enter_context(self.nc.sbuf_tensor(f"{name}_{self.n}", shape, dt))

    def ps(self, ctx, name, shape, dt=F32):
        self.n += 1
        return ctx.enter_context(self.nc.psum_tensor(f"{name}_{self.n}", shape, dt))

    def const(self, name):
        at, k = CONST[name]
        return self.consts[:, at:at + k]

    def vec(self, name, i=0, k=None):
        at, n = VECS[name]
        return self.vecs[:, at + i:at + i + (n if k is None else k)]

    def row(self, name):
        at, k = ROWS[name]
        return self.rows[:, at:at + k]

    @contextmanager
    def block(self):
        mine, self.fresh = self.fresh, []
        for spent in self.spent:
            self.nc.gpsimd.sem_clear(spent)
        with self.nc.Block() as block:
            yield block
        for spent in self.spent:
            self.nc.release_semaphore(spent)
        self.spent = mine


def at(i, k=1):
    return bass.ds(i, k)


def load_all(K, consts, vecs, rows, xT):
    nc = K.nc
    loaded, siluc = K.sem("loaded"), K.sem("siluc")
    with K.block() as block:
        @block.sync
        def _(sp):
            sp.dma_start(K.x[:], xT.rearrange("(c p) t -> p c t", p=P)).then_inc(loaded, 16)
            sp.dma_start(K.consts[:], consts).then_inc(loaded, 16)
            sp.dma_start(K.vecs[:], vecs).then_inc(loaded, 16)
            sp.dma_start(K.rows[:], rows).then_inc(loaded, 16)
            sp.wait_ge(loaded, 64)

        @block.scalar
        def _(act):
            act.wait_ge(loaded, 64)
            nc.scalar.activation(K.cond[:], K.vec("c", 0, 4 * KD), ACT.Silu).then_inc(siluc, 1)
            act.wait_ge(siluc, 1)


def ada(K, w, bias, pair):
    nc = K.nc
    G = 512
    C = G // P
    n_groups = 6 * D // G
    wv = w.rearrange("(c p) n -> p c n", p=P)
    cond = K.cond[:].rearrange("p (b s c) -> p b c s", b=2, s=2)[:, pair]
    with ExitStack() as ctx:
        wt = [K.sb(ctx, f"ada_w{u}", [P, KD, G]) for u in range(2)]
        acc = K.ps(ctx, "ada_acc", [P, 2, C * P])
        w_full = [K.sem("ada_w_full") for _ in range(2)]
        acc_full = [K.sem("ada_acc_full") for _ in range(2)]
        acc_free = [K.sem("ada_acc_free") for _ in range(2)]
        block = ctx.enter_context(K.block())

        @block.sync
        def _(sp):
            with sp.Fori(0, n_groups // 2) as it:
                for u in range(2):
                    sp.wait_ge(acc_full[u], it + 1)
                    sp.dma_start(wt[u][:], wv[:, :, at((it * 2 + u) * G, G)]).then_inc(w_full[u], 16)

        @block.tensor
        def _(pe):
            for u in range(2):
                pe.sem_inc(acc_full[u], 1)
            with pe.Fori(0, n_groups // 2) as it:
                for u in range(2):
                    pe.wait_ge(w_full[u], it * 16 + 16)
                    pe.wait_ge(acc_free[u], it + 1)
                    for n in range(C):
                        for c in range(KD):
                            last = nc.tensor.matmul(acc[:, u, 2 * n:2 * n + 2], wt[u][:, c, n * P:(n + 1) * P],
                                                    cond[:, c, :], start=(c == 0), stop=(c == KD - 1))
                    last.then_inc(acc_full[u], 1)

        @block.vector
        def _(dve):
            for u in range(2):
                dve.sem_inc(acc_free[u], 1)
            with dve.Fori(0, n_groups // 2) as it:
                for u in range(2):
                    dve.wait_ge(acc_full[u], it + 2)
                    for s in range(2):
                        last = nc.vector.tensor_tensor(
                            K.mod[:, s, at((it * 2 + u) * C, C)],
                            acc[:, u, 0:2 * C].rearrange("p (n s) -> p s n", s=2)[:, s],
                            K.vecs[:, at((it * 2 + u) * C + VECS[bias][0], C)], ALU.add)
                    last.then_inc(acc_free[u], 1)


def norm(K, src, dst, weight, scale_at, shift_at, ctx_tokens, mod=True):
    nc = K.nc
    T = TT if ctx_tokens else TX
    parts = ((0, 0, TX), (1, TX, TT)) if ctx_tokens else ((0, 0, TX),)
    ones = K.const("ones")
    with ExitStack() as ctx:
        rstd = K.sb(ctx, "rstd", [P, T])
        gain = K.sb(ctx, "gain", [P, 2, KD])
        squares = K.sb(ctx, "squares", [P, KD, T]) if dst is src else dst
        ss = K.ps(ctx, "ss", [P, 1024])
        sq, summed, inv, root, scaled, gained, done = (
            K.sem("norm_" + n) for n in ("sq", "summed", "inv", "root", "scaled", "gained", "done"))
        block = ctx.enter_context(K.block())

        @block.scalar
        def _(act):
            for c in range(KD):
                nc.scalar.activation(squares[:, c, 0:T], src[:, c, 0:T], ACT.Square).then_inc(sq, 1)
            act.wait_ge(inv, 1)
            nc.scalar.activation(rstd[:], rstd[:], ACT.Sqrt).then_inc(root, 1)
            act.wait_ge(gained, 1)
            for c in range(KD):
                act.wait_ge(scaled, c + 1)
                for s, a, b in parts:
                    bias = K.mod[:, s, shift_at + c:shift_at + c + 1] if mod else 0.0
                    last = nc.scalar.activation(dst[:, c, a:b], dst[:, c, a:b], ACT.Identity,
                                                bias=bias, scale=gain[:, s, c:c + 1])
            last.then_inc(done, 1)
            act.wait_ge(done, 1)

        @block.tensor
        def _(pe):
            for c in range(KD):
                pe.wait_ge(sq, c + 1)
                for s, a, b in parts:
                    last = nc.tensor.matmul(ss[:, a:b], ones, squares[:, c, a:b], start=(c == 0), stop=(c == KD - 1))
            last.then_inc(summed, 1)

        @block.vector
        def _(dve):
            for s, a, b in parts:
                if mod:
                    nc.vector.scalar_tensor_tensor(gain[:, s, :], K.mod[:, s, scale_at:scale_at + KD], 1.0,
                                                   K.vec(weight), ALU.add, ALU.mult)
                else:
                    nc.vector.tensor_copy(gain[:, s, :], K.vec(weight))
            dve.drain()
            dve.sem_inc(gained, 1)
            dve.wait_ge(summed, 1)
            nc.vector.tensor_scalar(rstd[:], ss[:, 0:T], 1.0 / D, EPS, ALU.mult, ALU.add)
            dve.drain()
            nc.vector.reciprocal(rstd[:], rstd[:]).then_inc(inv, 1)
            dve.wait_ge(root, 1)
            for c in range(KD):
                nc.vector.tensor_tensor(dst[:, c, 0:T], src[:, c, 0:T], rstd[:], ALU.mult).then_inc(scaled, 1)


def features(K, h, w, col0, n_chunks, tok, evac):
    nc = K.nc
    wv = w.rearrange("(c p) n -> p c n", p=P)
    parts = ((0, TX), (TX, TT)) if tok == TT else ((0, tok),)
    with ExitStack() as ctx:
        wt = [K.sb(ctx, f"feat_w{u}", [P, KD, P]) for u in range(2)]
        acc = K.ps(ctx, "feat_acc", [P, 2, 1024])
        w_full = [K.sem("feat_w_full") for _ in range(2)]
        acc_full = [K.sem("feat_acc_full") for _ in range(2)]
        acc_free = [K.sem("feat_acc_free") for _ in range(2)]
        block = ctx.enter_context(K.block())

        @block.sync
        def _(sp):
            with sp.Fori(0, n_chunks // 2) as it:
                for u in range(2):
                    sp.wait_ge(acc_full[u], it + 1)
                    sp.dma_start(wt[u][:], wv[:, :, at((it * 2 + u) * P + col0, P)]).then_inc(w_full[u], 16)

        @block.tensor
        def _(pe):
            for u in range(2):
                pe.sem_inc(acc_full[u], 1)
            with pe.Fori(0, n_chunks // 2) as it:
                for u in range(2):
                    pe.wait_ge(w_full[u], it * 16 + 16)
                    pe.wait_ge(acc_free[u], it + 1)
                    for c in range(KD):
                        for a, b in parts:
                            last = nc.tensor.matmul(acc[:, u, a:b], wt[u][:, c, :], h[:, c, a:b],
                                                    start=(c == 0), stop=(c == KD - 1))
                    last.then_inc(acc_full[u], 1)

        @block.scalar
        def _(act):
            for u in range(2):
                act.sem_inc(acc_free[u], 1)
            with act.Fori(0, n_chunks // 2) as it:
                for u in range(2):
                    act.wait_ge(acc_full[u], it + 2)
                    evac(it * 2 + u, acc[:, u:u + 1, 0:tok]).then_inc(acc_free[u], 1)


def token_rows(K, h, w, col0, n_cols, tiles, dst):
    nc = K.nc
    G = 256
    wv = w.rearrange("(c p) n -> p c n", p=P)
    with ExitStack() as ctx:
        wt = [K.sb(ctx, f"tok_w{u}", [P, KD, G]) for u in range(2)]
        acc = K.ps(ctx, "tok_acc", [P, tiles, 512])
        w_full = [K.sem("tok_w_full") for _ in range(2)]
        acc_full = [K.sem("tok_acc_full") for _ in range(tiles)]
        acc_free = [K.sem("tok_acc_free") for _ in range(tiles)]
        block = ctx.enter_context(K.block())

        @block.sync
        def _(sp):
            with sp.Fori(0, n_cols // G // 2) as it:
                for u in range(2):
                    sp.wait_ge(acc_full[tiles - 1], it * 2 + u + 1)
                    sp.dma_start(wt[u][:], wv[:, :, at((it * 2 + u) * G + col0, G)]).then_inc(w_full[u], 16)

        @block.tensor
        def _(pe):
            pe.sem_inc(acc_full[tiles - 1], 2)
            with pe.Fori(0, n_cols // G // 2) as it:
                for u in range(2):
                    pe.wait_ge(w_full[u], it * 16 + 16)
                    for t in range(tiles):
                        pe.wait_ge(acc_free[t], it * 2 + u + 1)
                        for c in range(KD):
                            last = nc.tensor.matmul(acc[:, t, 0:G], h[:, c, t * P:(t + 1) * P], wt[u][:, c, :],
                                                    start=(c == 0), stop=(c == KD - 1))
                        last.then_inc(acc_full[t], 1)

        @block.scalar
        def _(act):
            for t in range(tiles):
                act.sem_inc(acc_free[t], 1)
            with act.Fori(0, n_cols // G // 2) as it:
                for u in range(2):
                    for t in range(tiles):
                        act.wait_ge(acc_full[t], it * 2 + u + (1 if t < tiles - 1 else 3))
                        nc.scalar.copy(dst[:, t, at((it * 2 + u) * G, G)], acc[:, t, 0:G]).then_inc(acc_free[t], 1)


def rope(K, qk, n_chunks):
    nc = K.nc
    with ExitStack() as ctx:
        turned = [K.sb(ctx, f"turned{u}", [P, 1, TX]) for u in range(2)]
        acc = K.ps(ctx, "rope_acc", [P, 2, TX])
        acc_full = [K.sem("rope_full") for _ in range(2)]
        acc_free = [K.sem("rope_free") for _ in range(2)]
        sin = K.const("sin").unsqueeze(1)
        cos = K.const("cos").unsqueeze(1)
        block = ctx.enter_context(K.block())

        @block.tensor
        def _(pe):
            with pe.Fori(0, n_chunks // 2) as it:
                for u in range(2):
                    pe.wait_ge(acc_free[u], it + 1)
                    nc.tensor.matmul(acc[:, u, :], K.const("rot"), qk[:, at(it * 2 + u), 0:TX],
                                     start=True, stop=True).then_inc(acc_full[u], 1)

        @block.vector
        def _(dve):
            for u in range(2):
                dve.sem_inc(acc_free[u], 1)
            with dve.Fori(0, n_chunks // 2) as it:
                for u in range(2):
                    part = qk[:, at(it * 2 + u), 0:TX]
                    dve.wait_ge(acc_full[u], it + 1)
                    nc.vector.tensor_tensor(turned[u][:], acc[:, u:u + 1, :], sin, ALU.mult)
                    nc.vector.tensor_tensor(part, part, cos, ALU.mult)
                    dve.drain()
                    nc.vector.tensor_tensor(part, part, turned[u][:], ALU.add).then_inc(acc_free[u], 1)


def residual(K, src, w, kc, gate_at, tok):
    nc = K.nc
    wv = w.rearrange("(c p) n -> p c n", p=P)
    parts = ((0, 0, TX), (1, TX, TT)) if tok == TT else ((0, 0, tok),)
    with ExitStack() as ctx:
        wt = [K.sb(ctx, f"res_w{u}", [P, kc, P]) for u in range(2)]
        acc = K.ps(ctx, "res_acc", [P, 2, 1024])
        w_full = [K.sem("res_w_full") for _ in range(2)]
        acc_full = [K.sem("res_acc_full") for _ in range(2)]
        acc_free = [K.sem("res_acc_free") for _ in range(2)]
        block = ctx.enter_context(K.block())

        @block.sync
        def _(sp):
            with sp.Fori(0, KD // 2) as it:
                for u in range(2):
                    sp.wait_ge(acc_full[u], it + 1)
                    sp.dma_start(wt[u][:], wv[:, :, at((it * 2 + u) * P, P)]).then_inc(w_full[u], 16)

        @block.tensor
        def _(pe):
            for u in range(2):
                pe.sem_inc(acc_full[u], 1)
            with pe.Fori(0, KD // 2) as it:
                for u in range(2):
                    pe.wait_ge(w_full[u], it * 16 + 16)
                    pe.wait_ge(acc_free[u], it + 1)
                    for c in range(kc):
                        for _, a, b in parts:
                            last = nc.tensor.matmul(acc[:, u, a:b], wt[u][:, c, :], src[:, c, a:b],
                                                    start=(c == 0), stop=(c == kc - 1))
                    last.then_inc(acc_full[u], 1)

        @block.vector
        def _(dve):
            for u in range(2):
                dve.sem_inc(acc_free[u], 1)
            with dve.Fori(0, KD // 2) as it:
                for u in range(2):
                    n = it * 2 + u
                    dve.wait_ge(acc_full[u], it + 2)
                    for s, a, b in parts:
                        last = nc.vector.scalar_tensor_tensor(
                            K.x[:, at(n), a:b], acc[:, u:u + 1, a:b], K.mod[:, s, at(n + gate_at)],
                            K.x[:, at(n), a:b], ALU.mult, ALU.add)
                    last.then_inc(acc_free[u], 1)


def ffn_up(K, h, w, taps, bias, gated, tok):
    nc = K.nc
    wv = w.rearrange("(c p) (s n) -> p c s n", p=P, s=2)
    parts = ((0, TX), (TX, TT)) if tok == TT else ((0, tok),)
    tap0, b0 = VECS[taps][0], VECS[bias][0]
    with ExitStack() as ctx:
        wt = [K.sb(ctx, f"up_w{u}", [P, KD, 2, P]) for u in range(2)]
        conv = K.sb(ctx, "conv", [P, 2, 2, tok])
        acc = K.ps(ctx, "up_acc", [P, 2, 2, 1024])
        w_full = [K.sem("up_w_full") for _ in range(2)]
        acc_full = [K.sem("up_acc_full") for _ in range(2)]
        mid = [K.sem("up_mid") for _ in range(2)]
        acc_free = [K.sem("up_acc_free") for _ in range(2)]
        silu = [K.sem("up_silu") for _ in range(2)]
        out = [K.sem("up_out") for _ in range(2)]
        block = ctx.enter_context(K.block())

        @block.sync
        def _(sp):
            with sp.Fori(0, NF // 2) as it:
                for u in range(2):
                    sp.wait_ge(acc_full[u], it + 1)
                    sp.dma_start(wt[u][:, :, 0, :], wv[:, :, 0, at((it * 2 + u) * P, P)]).then_inc(w_full[u], 16)
                    sp.dma_start(wt[u][:, :, 1, :], wv[:, :, 1, at((it * 2 + u) * P, P)]).then_inc(w_full[u], 16)

        @block.tensor
        def _(pe):
            for u in range(2):
                pe.sem_inc(acc_full[u], 1)
            with pe.Fori(0, NF // 2) as it:
                for u in range(2):
                    pe.wait_ge(w_full[u], it * 32 + 32)
                    pe.wait_ge(acc_free[u], it + 1)
                    for s in range(2):
                        for c in range(KD):
                            for a, b in parts:
                                last = nc.tensor.matmul(acc[:, u, s, a:b], wt[u][:, c, s, :], h[:, c, a:b],
                                                        start=(c == 0), stop=(c == KD - 1))
                    last.then_inc(acc_full[u], 1)

        @block.scalar
        def _(act):
            for u in range(2):
                act.sem_inc(mid[u], 1)
            with act.Fori(0, NF // 2) as it:
                for u in range(2):
                    n = it * 2 + u
                    act.wait_ge(acc_full[u], it + 2)
                    act.wait_ge(out[u], it + 1)
                    for s in range(2):
                        last = nc.scalar.activation(conv[:, u, s, :], acc[:, u, s, 0:tok], ACT.Identity,
                                                    bias=K.vecs[:, at(n + (b0 + s * NF))],
                                                    scale=K.vecs[:, at(n + (tap0 + 2 * NF + s * NF))])
                    last.then_inc(mid[u], 1)
                    act.wait_ge(acc_free[u], it + 2)
                    nc.scalar.activation(conv[:, u, 1, :], conv[:, u, 1, :], ACT.Silu).then_inc(silu[u], 1)

        @block.vector
        def _(dve):
            for u in range(2):
                dve.sem_inc(acc_free[u], 1)
                dve.sem_inc(out[u], 1)
            with dve.Fori(0, NF // 2) as it:
                for u in range(2):
                    n = it * 2 + u
                    dve.wait_ge(mid[u], it + 2)
                    for s in range(2):
                        for a, b in parts:
                            nc.vector.scalar_tensor_tensor(
                                conv[:, u, s, a + 1:b], acc[:, u, s, a:b - 1], K.vecs[:, at(n + (tap0 + s * NF))],
                                conv[:, u, s, a + 1:b], ALU.mult, ALU.add)
                    dve.drain()
                    for s in range(2):
                        for a, b in parts:
                            last = nc.vector.scalar_tensor_tensor(
                                conv[:, u, s, a:b - 1], acc[:, u, s, a + 1:b],
                                K.vecs[:, at(n + (tap0 + 4 * NF + s * NF))],
                                conv[:, u, s, a:b - 1], ALU.mult, ALU.add)
                    last.then_inc(acc_free[u], 1)
                    dve.wait_ge(silu[u], it + 1)
                    nc.vector.tensor_tensor(gated[:, at(n), 0:tok], conv[:, u, 0:1, :], conv[:, u, 1:2, :],
                                            ALU.mult).then_inc(out[u], 1)


def head_norm(K, src, chunks, tok, dst, a, eps, gain):
    nc = K.nc
    parts = ((0, TX), (TX, TT)) if tok == TT else ((0, tok),)
    with ExitStack() as ctx:
        sq = [K.sb(ctx, f"hn_sq{u}", [P, 1, tok]) for u in range(2)]
        rstd = [K.sb(ctx, f"hn_rstd{u}", [P, 1, tok]) for u in range(2)]
        ss = K.ps(ctx, "hn_ss", [P, 2, 1024])
        sq_full = [K.sem("hn_sq") for _ in range(2)]
        ss_full = [K.sem("hn_ss") for _ in range(2)]
        inv = [K.sem("hn_inv") for _ in range(2)]
        root = [K.sem("hn_root") for _ in range(2)]
        done = [K.sem("hn_done") for _ in range(2)]
        block = ctx.enter_context(K.block())

        @block.scalar
        def _(act):
            with act.Fori(0, chunks // 2) as it:
                for u in range(2):
                    act.wait_ge(ss_full[u], it + 1)
                    nc.scalar.activation(sq[u][:], src[:, at(it * 2 + u), 0:tok], ACT.Square).then_inc(sq_full[u], 1)
                for u in range(2):
                    act.wait_ge(inv[u], it + 1)
                    nc.scalar.activation(rstd[u][:], rstd[u][:], ACT.Sqrt).then_inc(root[u], 1)

        @block.tensor
        def _(pe):
            for u in range(2):
                pe.sem_inc(ss_full[u], 1)
            with pe.Fori(0, chunks // 2) as it:
                for u in range(2):
                    pe.wait_ge(sq_full[u], it + 1)
                    pe.wait_ge(done[u], it + 1)
                    for p, q in parts:
                        last = nc.tensor.matmul(ss[:, u, p:q], K.const("ones"), sq[u][:, 0, p:q], start=True, stop=True)
                    last.then_inc(ss_full[u], 1)

        @block.vector
        def _(dve):
            for u in range(2):
                dve.sem_inc(done[u], 1)
            with dve.Fori(0, chunks // 2) as it:
                for u in range(2):
                    dve.wait_ge(ss_full[u], it + 2)
                    nc.vector.tensor_scalar(rstd[u][:], ss[:, u:u + 1, 0:tok], a, eps, ALU.mult, ALU.add)
                    dve.drain()
                    nc.vector.reciprocal(rstd[u][:], rstd[u][:]).then_inc(inv[u], 1)
                    dve.wait_ge(root[u], it + 1)
                    nc.vector.scalar_tensor_tensor(dst[:, at(it * 2 + u), 0:tok], src[:, at(it * 2 + u), 0:tok], gain,
                                                   rstd[u][:], ALU.mult, ALU.mult).then_inc(done[u], 1)


def attention(K, q, k, v, o, diff, bias_rows):
    nc = K.nc
    scale = HD ** -0.5
    NQ = NT if diff else NTX
    NA = 1 if diff else 2
    TQ = NQ * P
    ident = K.const("ident")
    with ExitStack() as ctx:
        qs = [K.sb(ctx, f"att_q{u}", [P, 1, TQ]) for u in range(2)]
        ks = [K.sb(ctx, f"att_k{u}", [P, 1, TT]) for u in range(2)]
        vs = [K.sb(ctx, f"att_v{u}", [P, NT, P]) for u in range(2)]
        prob = K.sb(ctx, "prob", [P, 2, 2, TT])
        pT = K.sb(ctx, "pT", [P, NA, NT, TX])
        if diff:
            pTc = K.sb(ctx, "pTc", [P, NTC, TC])
        mx = K.sb(ctx, "mx", [P, 2, 2, 2])
        nm = K.sb(ctx, "nm", [P, 2, 2])
        rs = K.sb(ctx, "rs", [P, 2, 2, 2])
        rr = K.sb(ctx, "rr", [P, 2, 2])
        lam = K.sb(ctx, "lam", [P, 1])
        S = K.ps(ctx, "scores", [P, 2, 3 * 512])
        tp = K.ps(ctx, "turned", [P, 2 * 512])
        if not diff:
            sb_ = K.sb(ctx, "biased", [P, 2, 2, TX])
            bias = [K.sb(ctx, f"bias{u}", [P, 2, NSLOT, GRID_W]) for u in range(2)]
            bias_full = [K.sem("bias_full") for _ in range(2)]
        staged = [K.sem("att_staged") for _ in range(2)]
        first_half = K.sem("att_first_half")
        s_ready, m_ready, e_done, a_ready, t_ready, t_out, pv, lam_ready = (
            K.sem("att_" + n) for n in ("scores", "max", "exp", "probs", "turned", "turned_out", "pv", "lam"))
        block = ctx.enter_context(K.block())

        @block.gpsimd
        def _(pool):
            with pool.Fori(0, 4) as it:
                for u in range(2):
                    hh = it * 2 + u
                    pool.wait_ge(pv, hh + 1)
                    nc.gpsimd.tensor_copy(qs[u][:], q[:, at(hh), :])
                    nc.gpsimd.tensor_copy(ks[u][:], k[:, at(hh), :])
                    nc.gpsimd.tensor_copy(vs[u][:], v[:, :, at(hh * P, P)])
                    pool.drain()
                    pool.sem_inc(staged[u], 1)

        if not diff:
            @block.sync
            def _(sp):
                with sp.Fori(0, 4) as it:
                    for u in range(2):
                        hh = it * 2 + u
                        sp.wait_ge(m_ready, hh * NQ + NQ)
                        for j in range(2):
                            head = (hh * 2 + j)
                            sp.dma_start(bias[u][0:64, j], bias_rows[at(head), :, 1:1 + NSLOT, :].rearrange(
                                "h c s k -> c (h s) k")).then_inc(bias_full[u], 16)
                            sp.dma_start(bias[u][64:128, j], bias_rows[at(head), :, 0:NSLOT, :].rearrange(
                                "h c s k -> c (h s) k")).then_inc(bias_full[u], 16)

        @block.tensor
        def _(pe):
            pe.sem_inc(pv, 2)
            pe.sem_inc(t_ready, 2 * NA)

            def scores(u, g, qt):
                b = qt % 2
                pe.wait_ge(e_done, g + 1)
                for j in range(2):
                    half = slice(64 * j, 64 * j + 64)
                    q_tile = qs[u][half, 0, qt * P:(qt + 1) * P]
                    image = S[:, b, j * TX:(j + 1) * TX]
                    context = S[:, b, 2 * TX + j * TC:2 * TX + (j + 1) * TC]
                    if j == 1 and qt < NTX:
                        nc.tensor.matmul(image, q_tile, ks[u][half, 0, 0:TX], start=True, stop=True)
                    if j == 1:
                        pe.wait_ge(first_half, g + 1)
                    nc.tensor.matmul(context, q_tile, ks[u][half, 0, TX:TT], start=True, stop=True).then_inc(
                        s_ready if j else first_half, 1)
                    if j == 0 and qt < NTX:
                        nc.tensor.matmul(image, q_tile, ks[u][half, 0, 0:TX], start=True, stop=True)

            def turn(hh, qt):
                b = qt % 2
                g = hh * NQ + qt
                pe.wait_ge(a_ready, g + 1)
                for j in range(NA):
                    pe.wait_ge(t_out, hh * (NQ * NA + 1) + (qt * NA + j + 1))
                    for kt in range(NT):
                        if qt < NTX or kt >= NTX:
                            last = nc.tensor.transpose(tp[:, kt * P:(kt + 1) * P], prob[:, b, j, kt * P:(kt + 1) * P], ident)
                    last.then_inc(t_ready, 1)

            with pe.Fori(0, 4) as it:
                for u in range(2):
                    hh = it * 2 + u
                    g0 = hh * NQ
                    pe.wait_ge(staged[u], it + 1)
                    scores(u, g0, 0)
                    for qt in range(NQ):
                        if qt + 1 < NQ:
                            scores(u, g0 + qt + 1, qt + 1)
                        turn(hh, qt)
                    pe.wait_ge(t_out, hh * (NQ * NA + 1) + (NQ * NA + 1))
                    for j in range(NA):
                        rows = slice(0, P) if diff else slice(64 * j, 64 * j + 64)
                        for kt in range(NT):
                            last = nc.tensor.matmul(tp[rows, 0:TX], vs[u][:, kt, rows], pT[:, j, kt, :],
                                                    start=(kt == 0), stop=(kt == NT - 1))
                    if diff:
                        for kt in range(NTC):
                            last = nc.tensor.matmul(tp[:, TX:TT], vs[u][:, NTX + kt, :], pTc[:, kt, :],
                                                    start=(kt == 0), stop=(kt == NTC - 1))
                    last.then_inc(pv, 1)

        @block.vector
        def _(dve):
            dve.sem_inc(m_ready, 2 * NQ)
            if diff:
                lv = K.row("lam").rearrange("p (a b d) -> p a b d", a=2, b=2)
                prod = prob[:, 0, 0, 0:2 * HD].rearrange("p (a d) -> p a d", a=2)
                nc.vector.tensor_tensor(prod, lv[:, :, 0], lv[:, :, 1], ALU.mult)
                dve.drain()
                nc.vector.tensor_reduce(mx[:, 0, 0, :], prod, AX_X, ALU.add)
                dve.drain()
                dve.sem_inc(lam_ready, 1)
                dve.wait_ge(lam_ready, 2)
                nc.vector.scalar_tensor_tensor(lam[:], nm[:, 0, 0:1], LAM_INIT, nm[:, 0, 1:2], ALU.add, ALU.subtract)
                dve.drain()
                dve.sem_inc(lam_ready, 1)

            def maxima(u, g, qt):
                b = qt % 2
                dve.wait_ge(s_ready, g + 1)
                if diff:
                    if qt < NTX:
                        nc.vector.tensor_reduce(mx[:, b, 0, :], S[:, b, 0:2 * TX].rearrange("p (j k) -> p j k", j=2),
                                                AX_X, ALU.max)
                else:
                    at_row = KH - 1 - 2 * qt
                    for j in range(2):
                        nc.vector.scalar_tensor_tensor(
                            sb_[:, b, j, :], S[:, b, j * TX:(j + 1) * TX], scale,
                            bias[u][:, j, at_row - 1:at_row - 1 + GRID_H, :].rearrange("p s k -> p (s k)"),
                            ALU.mult, ALU.add)
                    dve.drain()
                    nc.vector.tensor_reduce(mx[:, b, 0, :], sb_[:, b], AX_X, ALU.max)
                nc.vector.tensor_reduce(mx[:, b, 1, :], S[:, b, 2 * TX:3 * TX].rearrange("p (j k) -> p j k", j=2),
                                        AX_X, ALU.max)
                dve.drain()
                if qt >= NTX:
                    nc.vector.tensor_scalar(nm[:, b, :], mx[:, b, 1, :], -scale, None, ALU.mult).then_inc(m_ready, 1)
                    return
                if diff:
                    nc.vector.tensor_tensor(mx[:, b, 0, :], mx[:, b, 0, :], mx[:, b, 1, :], ALU.max)
                    dve.drain()
                    nc.vector.tensor_scalar(nm[:, b, :], mx[:, b, 0, :], -scale, None, ALU.mult).then_inc(m_ready, 1)
                else:
                    nc.vector.scalar_tensor_tensor(mx[:, b, 0, :], mx[:, b, 1, :], scale, mx[:, b, 0, :],
                                                   ALU.mult, ALU.max)
                    dve.drain()
                    nc.vector.tensor_scalar(nm[:, b, :], mx[:, b, 0, :], -1.0, None, ALU.mult).then_inc(m_ready, 1)

            def weigh(g, qt):
                b = qt % 2
                lo = 0 if qt < NTX else TX
                dve.wait_ge(e_done, g + 3)
                if qt < NTX:
                    nc.vector.tensor_tensor(rr[:, b, :], rs[:, b, 0, :], rs[:, b, 1, :], ALU.add)
                    dve.drain()
                    nc.vector.reciprocal(rr[:, b, :], rr[:, b, :])
                else:
                    nc.vector.reciprocal(rr[:, b, :], rs[:, b, 1, :])
                dve.drain()
                if diff:
                    nc.vector.tensor_scalar(prob[:, b, 1, lo:], prob[:, b, 1, lo:], rr[:, b, 1:2], lam[:], ALU.mult, ALU.mult)
                    dve.drain()
                    nc.vector.scalar_tensor_tensor(prob[:, b, 0, lo:], prob[:, b, 0, lo:], rr[:, b, 0:1],
                                                   prob[:, b, 1, lo:], ALU.mult, ALU.subtract).then_inc(a_ready, 1)
                else:
                    for j in range(2):
                        last = nc.vector.tensor_scalar(prob[:, b, j, :], prob[:, b, j, :], rr[:, b, j:j + 1], None, ALU.mult)
                    last.then_inc(a_ready, 1)

            with dve.Fori(0, 4) as it:
                for u in range(2):
                    hh = it * 2 + u
                    g0 = hh * NQ
                    if not diff:
                        dve.wait_ge(bias_full[u], it * 64 + 64)
                        for j in range(2):
                            nc.vector.tensor_tensor(bias[u][:, j], bias[u][:, j], K.const("window").unsqueeze(1).broadcast_to(
                                [P, NSLOT, GRID_W]), ALU.add)
                        dve.drain()
                    maxima(u, g0, 0)
                    for qt in range(NQ):
                        if qt + 1 < NQ:
                            maxima(u, g0 + qt + 1, qt + 1)
                        weigh(g0 + qt, qt)

        @block.scalar
        def _(act):
            act.sem_inc(e_done, 2)
            act.sem_inc(t_out, 1)
            if diff:
                act.wait_ge(lam_ready, 1)
                nc.scalar.activation(nm[:, 0, :], mx[:, 0, 0, :], ACT.Exp)
                act.drain()
                act.sem_inc(lam_ready, 1)
                act.wait_ge(lam_ready, 3)

            def exps(g, qt):
                b = qt % 2
                act.wait_ge(m_ready, g + 1 + 2 * NQ)
                act.wait_ge(t_ready, g * NA + NA)
                for j in range(2):
                    if qt < NTX:
                        src = S[:, b, j * TX:(j + 1) * TX] if diff else sb_[:, b, j, :]
                        nc.scalar.activation(prob[:, b, j, 0:TX], src, ACT.Exp, bias=nm[:, b, j:j + 1],
                                             scale=scale if diff else 1.0, accum_out=rs[:, b, 0, j:j + 1])
                    nc.scalar.activation(prob[:, b, j, TX:TT], S[:, b, 2 * TX + j * TC:2 * TX + (j + 1) * TC], ACT.Exp,
                                         bias=nm[:, b, j:j + 1], scale=scale, accum_out=rs[:, b, 1, j:j + 1])
                act.drain()
                act.sem_inc(e_done, 1)

            def take(hh, g, qt):
                for j in range(NA):
                    act.wait_ge(t_ready, g * NA + j + 1 + 2 * NA)
                    if qt == 0 and j == 0:
                        act.wait_ge(pv, hh + 2)
                    if qt < NTX:
                        last = nc.scalar.copy(pT[:, j, :, qt * P:(qt + 1) * P],
                                              tp[:, 0:TT].rearrange("p (k q) -> p k q", k=NT))
                    else:
                        last = nc.scalar.copy(pTc[:, :, (qt - NTX) * P:(qt - NTX + 1) * P],
                                              tp[:, TX:TT].rearrange("p (k q) -> p k q", k=NTC))
                    last.then_inc(t_out, 1)

            with act.Fori(0, 4) as it:
                for u in range(2):
                    hh = it * 2 + u
                    g0 = hh * NQ
                    exps(g0, 0)
                    for qt in range(NQ):
                        if qt + 1 < NQ:
                            exps(g0 + qt + 1, qt + 1)
                        take(hh, g0 + qt, qt)
                    act.wait_ge(pv, hh + 3)
                    nc.scalar.copy(o[:, at(hh), 0:TQ], tp[:, 0:TQ].unsqueeze(1)).then_inc(t_out, 1)


def first_block(K, io):
    nc = K.nc
    for i in range(2):
        kind = "a" if i == 0 else "b"
        tok = TT if i == 0 else TX
        ada(K, io["ada_w"][i], f"ada_b{i}", 0)
        with ExitStack() as ctx:
            q = K.sb(ctx, "q", [P, KD, tok])
            k = K.sb(ctx, "k", [P, KD, TT])
            v = K.sb(ctx, "v", [P, NT, D])
            h = K.sb(ctx, "h", [P, KD, TT])
            w = io[kind + "_wqkv"][0]
            norm(K, K.x, h, f"norm_mix{i}", 8, 0, True)
            features(K, h, w, 0, KD, tok, lambda n, sums: nc.scalar.copy(q[:, at(n), :], sums))
            features(K, h, w, D, KD, TT, lambda n, sums: nc.scalar.copy(k[:, at(n), :], sums))
            token_rows(K, h, w, 2 * D, D, NT, v)
            if i == 0:
                rope(K, q, KD)
                rope(K, k, KD)
            attention(K, q, k, v, h, i == 0, io["bias_rows"])
            if i == 0:
                head_norm(K, h, KD, tok, h, 1.0 / P, EPS, K.subln[:])
            residual(K, h, io[kind + "_wo"][0], KD, 16, tok)
        with ExitStack() as ctx:
            gated = K.sb(ctx, "gated", [P, NF, tok])
            with ExitStack() as up:
                h = K.sb(up, "h2", [P, KD, tok])
                norm(K, K.x, h, f"norm_ffn{i}", 32, 24, i == 0)
                ffn_up(K, h, io["ffn_up"][i], f"conv{i}", f"conv_b{i}", gated, tok)
            residual(K, gated, io["ffn_down"][i], NF, 40, tok)
    norm(K, K.x, K.x, "norm_out", 0, 0, False, mod=False)


def dn_inputs(K, h, w, dst):
    nc = K.nc
    wv = w.rearrange("(c p) n -> p c n", p=P)
    parts = ((0, TX), (TX, TT))
    tap0 = VECS["dn_conv"][0]
    n_chunks = DNQKV // P
    with ExitStack() as ctx:
        wt = [K.sb(ctx, f"dni_w{u}", [P, KD, P]) for u in range(2)]
        conv = K.sb(ctx, "dni_conv", [P, 2, TT])
        acc = K.ps(ctx, "dni_acc", [P, 2, 1024])
        w_full = [K.sem("dni_w_full") for _ in range(2)]
        acc_full = [K.sem("dni_acc_full") for _ in range(2)]
        mid = [K.sem("dni_mid") for _ in range(2)]
        acc_free = [K.sem("dni_acc_free") for _ in range(2)]
        out = [K.sem("dni_out") for _ in range(2)]
        block = ctx.enter_context(K.block())

        @block.sync
        def _(sp):
            with sp.Fori(0, n_chunks // 2) as it:
                for u in range(2):
                    sp.wait_ge(acc_full[u], it + 1)
                    sp.dma_start(wt[u][:], wv[:, :, at((it * 2 + u) * P, P)]).then_inc(w_full[u], 16)

        @block.tensor
        def _(pe):
            for u in range(2):
                pe.sem_inc(acc_full[u], 1)
            with pe.Fori(0, n_chunks // 2) as it:
                for u in range(2):
                    pe.wait_ge(w_full[u], it * 16 + 16)
                    pe.wait_ge(acc_free[u], it + 1)
                    for c in range(KD):
                        for a, b in parts:
                            last = nc.tensor.matmul(acc[:, u, a:b], wt[u][:, c, :], h[:, c, a:b],
                                                    start=(c == 0), stop=(c == KD - 1))
                    last.then_inc(acc_full[u], 1)

        @block.scalar
        def _(act):
            for u in range(2):
                act.sem_inc(out[u], 1)
            with act.Fori(0, n_chunks // 2) as it:
                for u in range(2):
                    n = it * 2 + u
                    act.wait_ge(acc_full[u], it + 2)
                    act.wait_ge(out[u], it + 1)
                    nc.scalar.activation(conv[:, u, :], acc[:, u, 0:TT], ACT.Identity,
                                         scale=K.vecs[:, at(n + (tap0 + n_chunks))]).then_inc(mid[u], 1)
                    act.wait_ge(acc_free[u], it + 2)
                    nc.scalar.activation(dst[:, at(n), :], conv[:, u:u + 1, :], ACT.Silu).then_inc(out[u], 1)

        @block.vector
        def _(dve):
            for u in range(2):
                dve.sem_inc(acc_free[u], 1)
            with dve.Fori(0, n_chunks // 2) as it:
                for u in range(2):
                    n = it * 2 + u
                    dve.wait_ge(mid[u], it + 1)
                    for a, b in parts:
                        nc.vector.scalar_tensor_tensor(conv[:, u, a + 1:b], acc[:, u, a:b - 1], K.vecs[:, at(n + tap0)],
                                                       conv[:, u, a + 1:b], ALU.mult, ALU.add)
                    dve.drain()
                    for a, b in parts:
                        last = nc.vector.scalar_tensor_tensor(
                            conv[:, u, a:b - 1], acc[:, u, a + 1:b], K.vecs[:, at(n + (tap0 + 2 * n_chunks))],
                            conv[:, u, a:b - 1], ALU.mult, ALU.add)
                    last.then_inc(acc_free[u], 1)


def dn_gates(K, h, w, beta, g):
    nc = K.nc
    with ExitStack() as ctx:
        wt = K.sb(ctx, "ba_w", [P, KD, 16])
        y, e, l = (K.sb(ctx, "ba_" + n, [P, NT, 8]) for n in "yel")
        rate = K.sb(ctx, "rate", [P, 8])
        acc = K.ps(ctx, "ba_acc", [P, NT, 16])
        w_full, summed, biased, exped, done = (K.sem("ba_" + n) for n in ("w", "summed", "biased", "exped", "done"))
        block = ctx.enter_context(K.block())

        @block.sync
        def _(sp):
            sp.dma_start(wt[:], w[:, C_BA:C_BA + 16].rearrange("(c p) n -> p c n", p=P)).then_inc(w_full, 16)

        @block.tensor
        def _(pe):
            pe.wait_ge(w_full, 16)
            for t in range(NT):
                for c in range(KD):
                    last = nc.tensor.matmul(acc[:, t, :], h[:, c, t * P:(t + 1) * P], wt[:, c, :],
                                            start=(c == 0), stop=(c == KD - 1))
            last.then_inc(summed, 1)

        @block.vector
        def _(dve):
            dve.wait_ge(summed, 1)
            nc.vector.tensor_copy(beta[:], acc[:, :, 0:8])
            nc.vector.tensor_tensor(y[:], acc[:, :, 8:16], K.row("dt_bias").unsqueeze(1).broadcast_to([P, NT, 8]), ALU.add)
            dve.drain()
            nc.vector.scalar_tensor_tensor(e[:], y[:], -1.0, y[:], ALU.mult, ALU.min).then_inc(biased, 1)
            dve.wait_ge(exped, 1)
            nc.vector.scalar_tensor_tensor(l[:], y[:], 0.0, l[:], ALU.max, ALU.add)
            dve.drain()
            nc.vector.scalar_tensor_tensor(g[:], l[:], -1.0, rate[:].unsqueeze(1).broadcast_to([P, NT, 8]),
                                           ALU.mult, ALU.mult)
            dve.drain()

        @block.scalar
        def _(act):
            act.wait_ge(biased, 1)
            nc.scalar.activation(e[:], e[:], ACT.Exp)
            nc.scalar.activation(rate[:], K.row("a_log"), ACT.Exp)
            act.drain()
            nc.scalar.activation(l[:], e[:], ACT.Ln, bias=1.0)
            act.drain()
            act.sem_inc(exped, 1)
            nc.scalar.activation(beta[:], beta[:], ACT.Sigmoid).then_inc(done, 1)
            act.wait_ge(done, 1)


def steps_of(d):
    c = list(range(NTX, NT)) + list(range(NTX)) if d == 0 else list(range(NT - 1, NTX - 1, -1)) + list(range(NTX - 1, -1, -1))
    return c


def last_of(d):
    return P - 1 if d == 0 else 0


def deltanet(K, qkv, beta, g, o):
    nc = K.nc
    NS = 2 * NT
    UNITS = LEVELS * 3
    ident = K.const("ident")
    incl = K.const("incl").rearrange("p (d i) -> p d i", d=2)
    level = K.const("level").rearrange("p (d n i) -> p d n i", d=2, n=LEVELS)

    def last_column(t, d):
        return t[:, d * NT:(d + 1) * NT, last_of(d)]

    with ExitStack() as ctx:
        qs = K.sb(ctx, "dn_q", [P, NTX, P])
        ks, vs, kt, vt = (K.sb(ctx, "dn_" + n, [P, NT, P]) for n in ("k", "v", "kt", "vt"))
        gh, bh, gcol, ecol, edl, bk = (K.sb(ctx, "dn_" + n, [P, NS]) for n in ("gh", "bh", "gcol", "ecol", "edl", "bk"))
        gx, bx, dt, egc, AT, T, U, Pm, Kb = (
            K.sb(ctx, "dn_" + n, [P, NS, P]) for n in ("gx", "bx", "dt", "egc", "AT", "T", "U", "Pm", "Kb"))
        Vb, Kd, wT = gx, bx, Pm
        AL = K.sb(ctx, "dn_AL", [P, 2, NS, P])
        qe, att = (K.sb(ctx, "dn_" + n, [P, 2, NTX, P]) for n in ("qe", "att"))
        S = K.sb(ctx, "dn_S", [P, 2, 2, P])
        vn = K.sb(ctx, "dn_vn", [P, 2, 2, P])
        B = K.ps(ctx, "dn_banks", [P, 8, 512])
        three = B[:, 0:3, :].rearrange("p b n -> p (b n)").rearrange("p (s i) -> p s i", s=NS)
        gram = B[:, 4:6, :].rearrange("p b n -> p (b n)")[:, 0:NT * P].rearrange("p (c i) -> p c i", c=NT)
        vturn = B[:, 6:8, :].rearrange("p b n -> p (b n)")[:, 0:NT * P].rearrange("p (c i) -> p c i", c=NT)
        qk = B[:, 6, :].rearrange("p (c i) -> p c i", c=NTX)
        staged, gc_ready, dt_ready, exps, tm_ready, tm_out, gram_ready, beta_ready, a_built = (
            K.sem("dn_" + n) for n in ("staged", "gc", "dt", "exps", "turned", "turned_out", "gram", "beta", "a_built"))
        al_ready, p_ready, p_out, xy_ready, t_done, kv_ready, w_ready, w_out, head_done = (
            K.sem("dn_" + n) for n in ("al", "p", "p_out", "xy", "t_done", "kv", "w", "w_out", "head_done"))
        vn_ready, vn_out, ds_ready, s_done, o_ready, o_out = (
            [K.sem(f"dn_{n}{d}") for d in range(2)] for n in ("vn", "vn_out", "ds", "s_done", "o", "o_out"))
        block = ctx.enter_context(K.block())

        @block.gpsimd
        def _(pool):
            with pool.Fori(0, HEADS) as it:
                pool.wait_ge(head_done, it + 1)
                nc.gpsimd.tensor_copy(ks[:], qkv[:, at(it + HEADS), :].rearrange("p o (c i) -> p (o c) i", i=P))
                nc.gpsimd.tensor_copy(vs[:], qkv[:, at(it + 2 * HEADS), :].rearrange("p o (c i) -> p (o c) i", i=P))
                nc.gpsimd.tensor_copy(qs[:], qkv[:, at(it), 0:TX].rearrange("p o (c i) -> p (o c) i", i=P))
                for d in range(2):
                    nc.gpsimd.tensor_copy(gh[:, d * NT:(d + 1) * NT].unsqueeze(2), g[:, :, at(it + d * HEADS)])
                    nc.gpsimd.tensor_copy(bh[:, d * NT:(d + 1) * NT].unsqueeze(2), beta[:, :, at(it + d * HEADS)])
                pool.drain()
                nc.gpsimd.tensor_copy(gx[:], gh[:].unsqueeze(2).broadcast_to([P, NS, P]))
                nc.gpsimd.tensor_copy(bx[:], bh[:].unsqueeze(2).broadcast_to([P, NS, P]))
                pool.drain()
                pool.sem_inc(staged, 1)
                pool.wait_ge(a_built, it + 1)
                for n in range(LEVELS):
                    for q in range(3):
                        if n >= 2:
                            pool.wait_ge(t_done, it * UNITS + (n - 2) * 3 + q + 1)
                        for lo, hi, d in ((4 * q, min(4 * q + 4, NT), 0), (max(4 * q, NT), 4 * q + 4, 1)):
                            if lo < hi:
                                nc.gpsimd.tensor_tensor(
                                    AL[:, n % 2, lo:hi, :], AT[:, lo:hi, :],
                                    level[:, d, n, :].unsqueeze(1).broadcast_to([P, hi - lo, P]), ALU.mult)
                        pool.drain()
                        pool.sem_inc(al_ready, 1)
                    if n == 1:
                        pool.wait_ge(exps, it + 1)
                        pool.wait_ge(tm_out, it + 1)
                        nc.gpsimd.tensor_tensor(bk[:], bh[:], ecol[:], ALU.mult)
                        for d in range(2):
                            own = slice(d * NT, (d + 1) * NT)
                            nc.gpsimd.tensor_tensor(Vb[:, own, :], vt[:], bh[:, own].unsqueeze(2).broadcast_to([P, NT, P]), ALU.mult)
                            nc.gpsimd.tensor_tensor(Kd[:, own, :], kt[:], edl[:, own].unsqueeze(2).broadcast_to([P, NT, P]), ALU.mult)
                            nc.gpsimd.tensor_tensor(qe[:, d], qs[:], egc[:, d * NT:d * NT + NTX, :], ALU.mult)
                        pool.drain()
                        for d in range(2):
                            own = slice(d * NT, (d + 1) * NT)
                            nc.gpsimd.tensor_tensor(Kb[:, own, :], kt[:], bk[:, own].unsqueeze(2).broadcast_to([P, NT, P]), ALU.mult)
                        pool.drain()
                        pool.sem_inc(kv_ready, 1)

        @block.tensor
        def _(pe):
            pe.sem_inc(head_done, 1)
            with pe.Fori(0, HEADS) as it:
                pe.wait_ge(staged, it + 1)
                for d in range(2):
                    pe.wait_ge(o_out[d], it * NTX + 1)
                    pe.wait_ge(vn_out[d], it * NT + 1)
                    pe.wait_ge(s_done[d], it * (NT - 1) + 1)
                for s in range(NS):
                    nc.tensor.matmul(three[:, s, :], gx[:, s, :], incl[:, s // NT, :], start=True, stop=True)
                for d in range(2):
                    last = nc.tensor.matmul(B[:, 3, d * NT:(d + 1) * NT], incl[:, d, :], gh[:, d * NT:(d + 1) * NT],
                                            start=True, stop=True)
                last.then_inc(gc_ready, 1)
                for c in range(NT):
                    nc.tensor.transpose(gram[:, c, :], ks[:, c, :], ident)
                for c in range(NT):
                    last = nc.tensor.transpose(vturn[:, c, :], vs[:, c, :], ident)
                last.then_inc(tm_ready, 1)
                pe.wait_ge(tm_out, it + 1)
                for c in range(NT):
                    nc.tensor.matmul(gram[:, c, :], ks[:, c, :], ks[:, c, :], start=True, stop=True)
                for c in range(NTX):
                    last = nc.tensor.matmul(qk[:, c, :], ks[:, c, :], qs[:, c, :], start=True, stop=True)
                last.then_inc(gram_ready, 1)
                pe.wait_ge(exps, it + 1)
                for s in range(NS):
                    last = nc.tensor.matmul(three[:, s, :], bx[:, s, :], ident, start=True, stop=True)
                last.then_inc(beta_ready, 1)
                pe.wait_ge(a_built, it + 1)

                def first_product(n):
                    lev, q = divmod(n, 3)
                    pe.wait_ge(al_ready, it * UNITS + n + 1)
                    if 2 <= n < 5:
                        pe.wait_ge(t_done, it * UNITS + n - 1)
                    elif n >= 5:
                        pe.wait_ge(t_done, it * UNITS + n - 2)
                    if n >= 5:
                        pe.wait_ge(p_out, it * (UNITS - 3) + n - 4)
                    for s in range(4 * q, 4 * q + 4):
                        rhs = ident if lev == 0 else T[:, s, :]
                        last = nc.tensor.matmul(B[:, n % 2, (s % 4) * P:(s % 4 + 1) * P], AL[:, lev % 2, s, :], rhs,
                                                start=True, stop=True)
                    last.then_inc(p_ready, 1)

                def second_products(n):
                    lev, q = divmod(n, 3)
                    if lev == 0:
                        return
                    pe.wait_ge(p_out, it * (UNITS - 3) + n - 2)
                    if n >= 5:
                        pe.wait_ge(t_done, it * UNITS + n - 1)
                    for s in range(4 * q, 4 * q + 4):
                        cols = slice((s % 4) * P, (s % 4 + 1) * P)
                        if lev < LEVELS - 1:
                            nc.tensor.matmul(B[:, 2 + n % 2, cols], U[:, s, :], Pm[:, s, :], start=True, stop=True)
                        last = nc.tensor.matmul(B[:, 4 + n % 2, cols], Pm[:, s, :], U[:, s, :], start=True, stop=True)
                    last.then_inc(xy_ready, 1)

                for n in range(UNITS + 1):
                    if n < UNITS:
                        first_product(n)
                    if n >= 1:
                        second_products(n - 1)
                pe.wait_ge(t_done, it * UNITS + UNITS)
                pe.wait_ge(kv_ready, it + 1)
                for s in range(NS):
                    last = nc.tensor.matmul(three[:, s, :], Kb[:, s, :], U[:, s, :], start=True, stop=True)
                last.then_inc(w_ready, 1)
                pe.wait_ge(w_out, it + 1)
                for st in range(NT):
                    for d in range(2):
                        c = steps_of(d)[st]
                        s = d * NT + c
                        pe.wait_ge(vn_out[d], it * NT + st + 1)
                        last = nc.tensor.matmul(B[:, 3 + d, 0:P], U[:, s, :], Vb[:, s, :], start=True, stop=(st == 0))
                        if st > 0:
                            pe.wait_ge(s_done[d], it * (NT - 1) + st + 1)
                            last = nc.tensor.matmul(B[:, 3 + d, 0:P], wT[:, s, :], S[:, d, st % 2, :], start=False, stop=True)
                        last.then_inc(vn_ready[d], 1)
                    for d in range(2):
                        c = steps_of(d)[st]
                        s = d * NT + c
                        pe.wait_ge(vn_out[d], it * NT + st + 2)
                        if st < NT - 1:
                            nc.tensor.matmul(B[:, 5 + d, 0:P], Kd[:, s, :], vn[:, d, st % 2, :],
                                             start=True, stop=True).then_inc(ds_ready[d], 1)
                        if c < NTX:
                            k = st - NTC
                            pe.wait_ge(o_out[d], it * NTX + k + 1)
                            nc.tensor.matmul(B[:, d, 0:P], S[:, d, st % 2, :], qe[:, d, c, :], start=True, stop=False)
                            last = nc.tensor.matmul(B[:, d, 0:P], vn[:, d, st % 2, :], att[:, d, c, :],
                                                    start=False, stop=True)
                            last.then_inc(o_ready[d], 1)
                nc.tensor.matmul(B[:, 7, 0:P], ident, ident, start=True, stop=True).then_inc(head_done, 1)

        @block.scalar
        def _(act):
            for d in range(2):
                act.sem_inc(vn_out[d], 1)
            with act.Fori(0, HEADS) as it:
                act.wait_ge(tm_ready, it + 1)
                nc.scalar.copy(kt[:], gram)
                nc.scalar.copy(vt[:], vturn)
                act.drain()
                act.sem_inc(tm_out, 1)
                act.wait_ge(dt_ready, it + 1)
                nc.scalar.activation(egc[:], three, ACT.Exp)
                nc.scalar.activation(dt[:], dt[:], ACT.Exp)
                nc.scalar.activation(ecol[:], gcol[:], ACT.Exp)
                nc.scalar.activation(edl[:], edl[:], ACT.Exp)
                act.drain()
                act.sem_inc(exps, 1)
                for n in range(3, UNITS):
                    q = n % 3
                    act.wait_ge(p_ready, it * UNITS + n + 1)
                    nc.scalar.copy(Pm[:, 4 * q:4 * q + 4, :], B[:, n % 2, :].rearrange("p (s i) -> p s i", s=4)).then_inc(p_out, 1)
                act.wait_ge(w_ready, it + 1)
                nc.scalar.mul(wT[:], three, -1.0).then_inc(w_out, 1)
                for st in range(NT):
                    for d in range(2):
                        act.wait_ge(vn_ready[d], it * NT + st + 1)
                        nc.scalar.copy(vn[:, d, st % 2, :], B[:, 3 + d, 0:P]).then_inc(vn_out[d], 1)

        @block.vector
        def _(dve):
            for d in range(2):
                dve.sem_inc(s_done[d], 1)
                dve.sem_inc(o_out[d], 1)
            with dve.Fori(0, HEADS) as it:
                dve.wait_ge(gc_ready, it + 1)
                nc.vector.tensor_copy(gcol[:], B[:, 3, 0:NS])
                dve.drain()
                for s in range(NS):
                    nc.vector.tensor_scalar(dt[:, s, :], three[:, s, :], gcol[:, s:s + 1], 0.0, ALU.subtract, ALU.min)
                for d in range(2):
                    nc.vector.tensor_tensor(edl[:, d * NT:(d + 1) * NT], last_column(three, d), gcol[:, d * NT:(d + 1) * NT], ALU.subtract)
                dve.drain()
                dve.sem_inc(dt_ready, 1)
                dve.wait_ge(exps, it + 1)
                dve.wait_ge(gram_ready, it + 1)
                for d in range(2):
                    own = slice(d * NT, (d + 1) * NT)
                    image = slice(d * NT, d * NT + NTX)
                    nc.vector.tensor_tensor(AT[:, own, :], dt[:, own, :], gram, ALU.mult)
                    nc.vector.tensor_tensor(att[:, d], dt[:, image, :], qk, ALU.mult)
                dve.drain()
                for d in range(2):
                    nc.vector.tensor_tensor(att[:, d], att[:, d], incl[:, d, :].unsqueeze(1).broadcast_to([P, NTX, P]), ALU.mult)
                dve.wait_ge(beta_ready, it + 1)
                nc.vector.tensor_tensor(AT[:], AT[:], three, ALU.mult)
                dve.drain()
                dve.sem_inc(a_built, 1)
                for n in range(UNITS):
                    lev, q = divmod(n, 3)
                    own = slice(4 * q, 4 * q + 4)
                    four = lambda b: B[:, b, :].rearrange("p (s i) -> p s i", s=4)
                    wide = ident.unsqueeze(1).broadcast_to([P, 4, P])
                    if lev == 0:
                        dve.wait_ge(p_ready, it * UNITS + n + 1)
                        nc.vector.tensor_tensor(T[:, own, :], wide, four(n % 2), ALU.subtract)
                        nc.vector.tensor_tensor(U[:, own, :], wide, AL[:, 0, own, :], ALU.subtract)
                    else:
                        dve.wait_ge(xy_ready, it * (UNITS - 3) + n - 2)
                        if lev < LEVELS - 1:
                            nc.vector.tensor_tensor(T[:, own, :], T[:, own, :], four(2 + n % 2), ALU.subtract)
                        nc.vector.tensor_tensor(U[:, own, :], U[:, own, :], four(4 + n % 2), ALU.subtract)
                    dve.drain()
                    dve.sem_inc(t_done, 1)
                for st in range(NT):
                    if st == NTC + NTX // 2:
                        dve.drain()
                    for d in range(2):
                        c = steps_of(d)[st]
                        s = d * NT + c
                        if st < NT - 1:
                            dve.wait_ge(ds_ready[d], it * (NT - 1) + st + 1)
                            if st == 0:
                                nc.vector.tensor_copy(S[:, d, 1, :], B[:, 5 + d, 0:P]).then_inc(s_done[d], 1)
                            else:
                                nc.vector.scalar_tensor_tensor(
                                    S[:, d, 1 - st % 2, :], S[:, d, st % 2, :], egc[:, s, last_of(d):last_of(d) + 1],
                                    B[:, 5 + d, 0:P], ALU.mult, ALU.add).then_inc(s_done[d], 1)
                        if c < NTX:
                            k = st - NTC
                            dve.wait_ge(o_ready[d], it * NTX + k + 1)
                            part = o[:, at(it), c * P:(c + 1) * P]
                            if st < NTC + NTX // 2:
                                nc.vector.tensor_copy(part, B[:, d:d + 1, 0:P]).then_inc(o_out[d], 1)
                            else:
                                nc.vector.tensor_tensor(part, part, B[:, d:d + 1, 0:P], ALU.add).then_inc(o_out[d], 1)


def column_order(K, h, hp):
    nc = K.nc
    with K.block() as block:
        @block.vector
        def _(dve):
            for c in range(KD):
                nc.vector.tensor_copy(hp[:, c, 0:TX].rearrange("p (c r) -> p c r", r=GRID_H),
                                      h[:, c, 0:TX].rearrange("p (r c) -> p c r", r=GRID_H))
            dve.drain()

        @block.gpsimd
        def _(pool):
            nc.gpsimd.tensor_copy(hp[:, :, TX:TT], h[:, :, TX:TT])
            pool.drain()


def hg_gates(K, z, k):
    nc = K.nc
    W = 2 * HEADS * P
    both = lambda t: t[:].unsqueeze(1).broadcast_to([P, 2, HEADS * P])
    halves = lambda t: t.rearrange("p (d n) -> p d n", d=2)
    unit = float(2.0 ** LN_SHIFT)
    with ExitStack() as ctx:
        lb, oml = K.sb(ctx, "lb", [P, HEADS * P]), K.sb(ctx, "oml", [P, HEADS * P])
        low = K.sb(ctx, "low", [P, NT, W])
        zeroed, ones, bound, sig, shifted, logs = (K.sem("hgg_" + n) for n in ("zeroed", "ones", "bound", "sig", "shifted", "logs"))
        block = ctx.enter_context(K.block())

        @block.scalar
        def _(act):
            act.wait_ge(zeroed, 1)
            nc.scalar.activation(lb[:], lb[:], ACT.Exp).then_inc(ones, 1)
            for t in range(NT):
                nc.scalar.activation(k[:, t, :], z[:, t, 0:W], ACT.Sigmoid, scale=-1.0)
                act.drain()
                nc.scalar.activation(z[:, t, 0:W], z[:, t, 0:W], ACT.Sigmoid)
                act.drain()
                act.sem_inc(sig, 1)
            for t in range(NT):
                act.wait_ge(shifted, t + 1)
                nc.scalar.activation(z[:, t, 0:W], z[:, t, 0:W], ACT.Ln).then_inc(logs, 1)

        @block.vector
        def _(dve):
            nc.vector.tensor_tensor(lb[:], K.row("lb"), K.row("lb"), ALU.subtract).then_inc(zeroed, 1)
            dve.wait_ge(ones, 1)
            nc.vector.reciprocal(oml[:], lb[:])
            dve.drain()
            nc.vector.tensor_tensor(lb[:], lb[:], oml[:], ALU.mult)
            dve.drain()
            nc.vector.tensor_tensor(lb[:], lb[:], lb[:], ALU.subtract)
            dve.drain()
            nc.vector.tensor_scalar(oml[:], lb[:], -1.0, 1.0, ALU.mult, ALU.add)
            dve.drain()
            for t in range(NT):
                f = z[:, t, 0:W]
                dve.wait_ge(sig, t + 1)
                nc.vector.tensor_tensor(halves(k[:, t, :]), halves(k[:, t, :]), both(oml), ALU.mult)
                nc.vector.tensor_tensor(halves(f), halves(f), both(oml), ALU.mult)
                dve.drain()
                nc.vector.tensor_tensor(halves(f), halves(f), both(lb), ALU.add)
                dve.drain()
                nc.vector.tensor_scalar(f, f, F_TINY, None, ALU.max)
                dve.drain()
                nc.vector.tensor_scalar(low[:, t, :], f, 2.0 ** -40, unit, ALU.is_lt, ALU.mult)
                dve.drain()
                nc.vector.scalar_tensor_tensor(f, low[:, t, :], 1.0, f, ALU.add, ALU.mult).then_inc(shifted, 1)
            for t in range(NT):
                dve.wait_ge(logs, t + 1)
                nc.vector.scalar_tensor_tensor(z[:, t, 0:W], low[:, t, :], -LN_SHIFT * float(np.log(2.0)) / unit,
                                               z[:, t, 0:W], ALU.mult, ALU.add)
            dve.drain()


def hgrn(K, q, fi, kk, o):
    nc = K.nc
    NS = 2 * NT
    UNITS = 2 * LEVELS
    ident = K.const("ident")
    incl = K.const("incl").rearrange("p (d i) -> p d i", d=2)
    strict = K.const("strict").rearrange("p (d i) -> p d i", d=2)
    level = K.const("level").bitcast(U32).rearrange("p (d n i) -> p d n i", d=2, n=LEVELS)
    with ExitStack() as ctx:
        qs = K.sb(ctx, "hg_q", [P, NTX, P])
        lf, ks, ekd, gc = (K.sb(ctx, "hg_" + n, [P, NS, P]) for n in ("lf", "k", "ekd", "gc"))
        kd = lf
        vs = K.sb(ctx, "hg_v", [P, NT, P])
        kT, egc, qe, att = (K.sb(ctx, "hg_" + n, [P, 2, NTX, P]) for n in ("kT", "egc", "qe", "att"))
        egl = K.sb(ctx, "hg_egl", [P, NS])
        S = ekd[:].rearrange("p (d t) i -> p d t i", d=2)
        E, ql = (K.sb(ctx, "hg_" + n, [P, 2, TX]) for n in ("E", "ql"))
        kl = ks[:, 0:2 * NTX, :].rearrange("p (u c) i -> p u (c i)", u=2)
        B = K.ps(ctx, "hg_banks", [P, 8, 512])
        span = lambda lo, n: B[:, lo:lo + n, :].rearrange("p b n -> p (b n)").rearrange("p (s i) -> p s i", i=P)
        staged, sums, taken, weighed, ds_ready, states, o_ready, o_out, head_done = (
            K.sem("hg_" + n) for n in ("staged", "sums", "taken", "weighed", "ds", "states", "o", "o_out", "head_done"))
        diff, e_ready, q_ready, k_ready, a_ready, seen, a_out = (
            K.sem("hg_" + n) for n in ("diff", "e", "ql", "kl", "att", "seen", "att_out"))
        block = ctx.enter_context(K.block())

        @block.gpsimd
        def _(pool):
            with pool.Fori(0, HEADS) as it:
                pool.wait_ge(head_done, it + 1)
                for d in range(2):
                    own = slice(d * NT, (d + 1) * NT)
                    nc.gpsimd.tensor_copy(lf[:, own, :], fi[:, :, at((it + d * HEADS) * P, P)])
                    nc.gpsimd.tensor_copy(ks[:, own, :], kk[:, :, at((it + d * HEADS) * P, P)])
                nc.gpsimd.tensor_copy(vs[:], fi[:, :, at((it + 2 * HEADS) * P, P)])
                nc.gpsimd.tensor_copy(qs[:], q[:, at(it), :].rearrange("p o (c i) -> p (o c) i", i=P))
                pool.drain()
                pool.sem_inc(staged, 1)
                pool.wait_ge(taken, it + 1)
                nc.gpsimd.tensor_tensor(kd[:], ks[:], ekd[:], ALU.mult)
                for d in range(2):
                    nc.gpsimd.tensor_tensor(qe[:, d], qs[:], egc[:, d], ALU.mult)
                pool.drain()
                pool.sem_inc(weighed, 1)
                for n in range(UNITS):
                    pool.wait_ge(e_ready, it * UNITS + n + 1)
                    if n >= 2:
                        pool.wait_ge(a_ready, it * (UNITS + 2) + n + 1)
                    nc.gpsimd.tensor_tensor(kl[:, n % 2, :], kT[:, n % 2].rearrange("p c i -> p (c i)"), E[:, n % 2, :],
                                            ALU.mult).then_inc(k_ready, 1)

        @block.tensor
        def _(pe):
            pe.sem_inc(head_done, 1)
            with pe.Fori(0, HEADS) as it:
                pe.wait_ge(staged, it + 1)
                pe.wait_ge(o_out, it + 1)
                for s in range(NS):
                    nc.tensor.matmul(span(0, 3)[:, s, :], lf[:, s, :], incl[:, s // NT, :], start=True, stop=True)
                for d in range(2):
                    for lo, hi in ((0, 4), (4, 6)) if d == 0 else ((6, 8), (8, 12)):
                        nc.tensor.matmul(span(3, 3)[:, lo:hi, :], strict[:, 1 - d, :], lf[:, lo:hi, :], start=True, stop=True)
                for d in range(2):
                    for c in range(NTX):
                        last = nc.tensor.transpose(span(6, 2)[:, d * NTX + c, :], ks[:, d * NT + c, :], ident)
                last.then_inc(sums, 1)
                pe.wait_ge(taken, it + 1)
                for d in range(2):
                    for c in range(NTX):
                        last = nc.tensor.matmul(B[:, 6 + d, c * P:(c + 1) * P], kT[:, d, c, :], qs[:, c, :], start=True, stop=True)
                    last.then_inc(a_ready, 1)
                pe.wait_ge(weighed, it + 1)
                for s in range(NS):
                    last = nc.tensor.matmul(span(0, 3)[:, s, :], kd[:, s, :], vs[:, s % NT, :], start=True, stop=True)
                last.then_inc(ds_ready, 1)
                for n in range(UNITS):
                    pe.wait_ge(q_ready, it * UNITS + n + 1)
                    pe.wait_ge(k_ready, it * UNITS + n + 1)
                    pe.wait_ge(a_out, it * (UNITS + 2) + n + 1)
                    for c in range(NTX):
                        cols = slice(c * P, (c + 1) * P)
                        last = nc.tensor.matmul(B[:, 6 + n % 2, cols], kl[:, n % 2, cols], ql[:, n % 2, cols], start=True, stop=True)
                    last.then_inc(a_ready, 1)
                pe.wait_ge(a_out, it * (UNITS + 2) + UNITS + 2)
                pe.wait_ge(states, it + 1)
                for c in range(NTX):
                    for d in range(2):
                        nc.tensor.matmul(B[:, 5, c * P:(c + 1) * P], vs[:, c, :], att[:, d, c, :], start=(d == 0), stop=False)
                        last = nc.tensor.matmul(B[:, 5, c * P:(c + 1) * P], S[:, d, steps_of(d).index(c), :], qe[:, d, c, :],
                                                start=False, stop=(d == 1))
                last.then_inc(o_ready, 1)
                nc.tensor.matmul(B[:, 4, 0:P], ident, ident, start=True, stop=True).then_inc(head_done, 1)

        @block.scalar
        def _(act):
            act.sem_inc(o_out, 1)
            with act.Fori(0, HEADS) as it:
                act.wait_ge(sums, it + 1)
                nc.scalar.copy(gc[:], span(0, 3))
                nc.scalar.copy(kT[:].rearrange("p d c i -> p (d c) i"), span(6, 2))
                act.drain()
                nc.scalar.activation(ekd[:], span(3, 3), ACT.Exp)
                for d in range(2):
                    nc.scalar.activation(egc[:, d], gc[:, d * NT:d * NT + NTX, :], ACT.Exp)
                    nc.scalar.activation(egl[:, d * NT:(d + 1) * NT], gc[:, d * NT:(d + 1) * NT, last_of(d)], ACT.Exp)
                act.drain()
                act.sem_inc(taken, 1)
                for n in range(UNITS):
                    act.wait_ge(diff, it * UNITS + n + 1)
                    nc.scalar.activation(E[:, n % 2, :], E[:, n % 2, :], ACT.Abs)
                    act.drain()
                    nc.scalar.activation(E[:, n % 2, :], E[:, n % 2, :], ACT.Exp, scale=-1.0).then_inc(e_ready, 1)
                act.wait_ge(o_ready, it + 1)
                nc.scalar.copy(o[:, at(it), :].rearrange("p o (r c) -> p (o c) r", r=GRID_H),
                               B[:, 5, :].rearrange("p (c r) -> p c r", r=GRID_H)).then_inc(o_out, 1)

        @block.vector
        def _(dve):
            def keep(it, n):
                lev, d = divmod(n, 2)
                dve.wait_ge(a_ready, it * (UNITS + 2) + n + 3)
                dve.sem_inc(seen, 1)
                nc.vector.copy_predicated(att[:, d], level[:, d, lev, :].unsqueeze(1).broadcast_to([P, NTX, P]),
                                          B[:, 6 + d, :].rearrange("p (c i) -> p c i", i=P)).then_inc(a_out, 1)

            with dve.Fori(0, HEADS) as it:
                dve.wait_ge(taken, it + 1)

                def distances(n):
                    lev, d = divmod(n, 2)
                    s = 1 << lev
                    if n >= 2:
                        dve.wait_ge(k_ready, it * UNITS + n - 1)
                        dve.wait_ge(q_ready, it * UNITS + n - 1)
                    x = gc[:, d * NT:d * NT + NTX, :].rearrange("p c i -> p (c i)").rearrange("p (b t) -> p b t", t=2 * s)
                    ref = x[:, :, s - 1:s] if d == 0 else x[:, :, s:s + 1]
                    nc.vector.tensor_tensor(E[:, n % 2, :].rearrange("p (b t) -> p b t", t=2 * s), x,
                                            ref.broadcast_to([P, TX // (2 * s), 2 * s]), ALU.subtract).then_inc(diff, 1)

                distances(0)
                for d in range(2):
                    dve.wait_ge(a_ready, it * (UNITS + 2) + d + 1)
                    nc.vector.tensor_tensor(att[:, d], B[:, 6 + d, :].rearrange("p (c i) -> p c i", i=P),
                                            ident.unsqueeze(1).broadcast_to([P, NTX, P]), ALU.mult).then_inc(a_out, 1)
                for n in range(UNITS):
                    d = n % 2
                    if n + 1 < UNITS:
                        distances(n + 1)
                    dve.wait_ge(e_ready, it * UNITS + n + 1)
                    if n >= 2:
                        dve.wait_ge(a_ready, it * (UNITS + 2) + n + 1)
                    nc.vector.tensor_tensor(ql[:, d, :], qs[:].rearrange("p c i -> p (c i)"), E[:, d, :], ALU.mult).then_inc(q_ready, 1)
                    if n == 1:
                        dve.wait_ge(ds_ready, it + 1)
                        for dd in range(2):
                            nc.vector.tensor_copy(S[:, dd, 1, :], span(0, 3)[:, dd * NT + steps_of(dd)[0], :])
                            nc.vector.memset(S[:, dd, 0, :], 0.0)
                        dve.drain()
                        for st in range(1, NT - 1):
                            for dd in range(2):
                                i = dd * NT + steps_of(dd)[st]
                                nc.vector.scalar_tensor_tensor(S[:, dd, st + 1, :], S[:, dd, st, :], egl[:, i:i + 1],
                                                               span(0, 3)[:, i, :], ALU.mult, ALU.add)
                            dve.drain()
                        dve.sem_inc(states, 1)
                    if n >= 1:
                        keep(it, n - 1)
                keep(it, UNITS - 1)


def times(K, a, b):
    nc = K.nc
    with K.block() as block:
        @block.vector
        def _(dve):
            nc.vector.tensor_tensor(a[:], a[:], b[:], ALU.mult)
            dve.drain()


def merge(K, h, w_in, odn, w_dn, ohg, w_hg, m):
    nc = K.nc
    gv = w_in[:, C_GATE:C_GATE + 2 * D].rearrange("(c p) (s n) -> p c s n", p=P, s=2)
    bv = [w.rearrange("(c p) n -> p c n", p=P) for w in (w_dn, w_hg)]
    src = (odn, ohg)
    with ExitStack() as ctx:
        wg = [K.sb(ctx, f"gate_w{u}", [P, KD, 2, P]) for u in range(2)]
        wb = [K.sb(ctx, f"branch_w{u}", [P, 2, HEADS, P]) for u in range(2)]
        sig = K.sb(ctx, "gate_sig", [P, 2, 2, TX])
        acc = K.ps(ctx, "merge_acc", [P, 2, 4, TX])
        w_full = [K.sem("mrg_w_full") for _ in range(2)]
        acc_full = [K.sem("mrg_acc_full") for _ in range(2)]
        sig_full = [K.sem("mrg_sig_full") for _ in range(2)]
        out = [K.sem("mrg_out") for _ in range(2)]
        block = ctx.enter_context(K.block())

        @block.sync
        def _(sp):
            with sp.Fori(0, KD // 2) as it:
                for u in range(2):
                    cols = at((it * 2 + u) * P, P)
                    sp.wait_ge(acc_full[u], it + 1)
                    for s in range(2):
                        sp.dma_start(wg[u][:, :, s, :], gv[:, :, s, cols]).then_inc(w_full[u], 16)
                        sp.dma_start(wb[u][:, s], bv[s][:, :, cols]).then_inc(w_full[u], 16)

        @block.tensor
        def _(pe):
            for u in range(2):
                pe.sem_inc(acc_full[u], 1)
            with pe.Fori(0, KD // 2) as it:
                for u in range(2):
                    pe.wait_ge(w_full[u], it * 64 + 64)
                    pe.wait_ge(out[u], it + 1)
                    for s in range(2):
                        for c in range(KD):
                            nc.tensor.matmul(acc[:, u, s, :], wg[u][:, c, s, :], h[:, c, 0:TX], start=(c == 0), stop=(c == KD - 1))
                        for c in range(HEADS):
                            last = nc.tensor.matmul(acc[:, u, 2 + s, :], wb[u][:, s, c, :], src[s][:, c, :],
                                                    start=(c == 0), stop=(c == HEADS - 1))
                    last.then_inc(acc_full[u], 1)

        @block.scalar
        def _(act):
            with act.Fori(0, KD // 2) as it:
                for u in range(2):
                    act.wait_ge(acc_full[u], it + 2)
                    act.wait_ge(out[u], it + 1)
                    nc.scalar.activation(sig[:, u], acc[:, u, 0:2, :], ACT.Sigmoid).then_inc(sig_full[u], 1)

        @block.vector
        def _(dve):
            for u in range(2):
                dve.sem_inc(out[u], 1)
            with dve.Fori(0, KD // 2) as it:
                for u in range(2):
                    dve.wait_ge(sig_full[u], it + 1)
                    nc.vector.tensor_tensor(sig[:, u], sig[:, u], acc[:, u, 2:4, :], ALU.mult)
                    dve.drain()
                    nc.vector.tensor_tensor(m[:, at(it * 2 + u), :], sig[:, u, 0:1, :], sig[:, u, 1:2, :], ALU.add).then_inc(out[u], 1)


def route(K, h, w_router, h_rows, table, gate, dest, slots, blocks):
    nc = K.nc
    NB = NE
    with ExitStack() as ctx:
        wr = K.sb(ctx, "router_w", [P, KD, NG + NE])
        rows = K.sb(ctx, "h_rows", [P, 2, D])
        L = K.sb(ctx, "logits", [P, NTX, NG + NE])
        g1, g2, eg, oh = (K.sb(ctx, "grp_" + n, [P, NTX, NG]) for n in ("a", "b", "e", "oh"))
        gm, gs = K.sb(ctx, "grp_max", [P, NTX]), K.sb(ctx, "grp_sum", [P, NTX])
        pick = K.sb(ctx, "pick", [P, NTX, EPG, NG])
        p, e1 = K.sb(ctx, "exp_p", [P, NTX, EPG]), K.sb(ctx, "exp_val", [P, NTX, EPG])
        chosen = K.sb(ctx, "chosen", [P, TOPK, NTX, EPG])
        top = K.sb(ctx, "top", [P, TOPK, NTX])
        m0, m1 = K.sb(ctx, "max_a", [P, NTX]), K.sb(ctx, "max_b", [P, NTX])
        M = K.sb(ctx, "assigned", [P, TOPK, NTX, NE])
        Ms = K.sb(ctx, "assigned_any", [P, NTX, NE])
        cnt, nb, ca, cb, start = (K.sb(ctx, "cnt_" + n, [P, NE]) for n in ("n", "blocks", "a", "b", "start"))
        where = K.sb(ctx, "where", [P, NTX, NE])
        picked = K.sb(ctx, "picked", [P, TOPK, NTX, NE])
        destf = K.sb(ctx, "destf", [P, TOPK, NTX])
        be = K.sb(ctx, "block_expert", [P, 1])
        zero = K.sb(ctx, "zero", [NBLK, P])
        tab = K.sb(ctx, "tab", [NBLK, P])
        lp = K.ps(ctx, "route_logits", [P, NTX, NG + NE])
        cp = K.ps(ctx, "route_counts", [P, NTX + 1, NE])
        bp = K.ps(ctx, "route_blocks", [P, P])
        tp = K.ps(ctx, "route_turned", [P, 2, D])
        names = ("w", "logits", "shifted", "exps", "shifted2", "exps2", "assigned", "counts", "be", "bp", "dest",
                 "zeroed", "cleared", "scattered", "tab", "tab_turned", "turned", "rows", "stored0", "stored1", "done")
        (w_full, logits, shifted, exps, shifted2, exps2, assigned, counts, be_ready, bp_ready, dest_ready,
         zeroed, cleared, scattered, tab_full, tab_turned, turned, rows_out, stored0, stored1, done) = (
            K.sem("rt_" + n) for n in names)
        stored = (stored0, stored1)
        block = ctx.enter_context(K.block())

        @block.sync
        def _(sp):
            sp.dma_start(wr[:], w_router.rearrange("(c p) n -> p c n", p=P)).then_inc(w_full, 16)
            sp.wait_ge(zeroed, 1)
            sp.dma_start(table.rearrange("(b p) o -> b (p o)", p=P), zero[:]).then_inc(cleared, 16)
            for t in range(NTX):
                sp.wait_ge(rows_out, t + 1)
                sp.dma_start(h_rows[t * P:(t + 1) * P, :], rows[:, t % 2, :]).then_inc(stored[t % 2], 16)
            sp.wait_ge(scattered, 16 * TOPK * NTX)
            sp.dma_start(tab[:], table.rearrange("(b p) o -> b (p o)", p=P)).then_inc(tab_full, 16)
            for u in range(2):
                sp.wait_ge(stored[u], 16 * NTX // 2)

        @block.gpsimd
        def _(pool):
            nc.gpsimd.memset(zero[:], 0.0)
            pool.drain()
            pool.sem_inc(zeroed, 1)
            pool.wait_ge(cleared, 16)
            pool.wait_ge(dest_ready, 1)
            for k in range(TOPK):
                for t in range(NTX):
                    nc.gpsimd.indirect_dma_start(
                        out=table, out_offset=bass.IndirectOffsetOnAxis(ap=dest[:, k, t:t + 1], axis=0),
                        in_=K.const("tokid")[:, t:t + 1], in_offset=None).then_inc(scattered, 16)

        @block.tensor
        def _(pe):
            ident = K.const("ident")
            ones = K.const("ones")
            before = K.const("strict")[:, 0:P]
            pe.wait_ge(w_full, 16)
            for t in range(NTX):
                for c in range(KD):
                    last = nc.tensor.matmul(lp[:, t, :], h[:, c, t * P:(t + 1) * P], wr[:, c, :], start=(c == 0), stop=(c == KD - 1))
            last.then_inc(logits, 1)
            for t in range(NTX):
                if t >= 2:
                    pe.wait_ge(rows_out, t - 1)
                for c in range(KD):
                    last = nc.tensor.transpose(tp[:, t % 2, c * P:(c + 1) * P], h[:, c, t * P:(t + 1) * P], ident)
                last.then_inc(turned, 1)
            pe.wait_ge(assigned, 1)
            for t in range(NTX):
                for b in range(t):
                    nc.tensor.matmul(cp[:, t, :], ones, Ms[:, b, :], start=(b == 0), stop=False)
                nc.tensor.matmul(cp[:, t, :], before, Ms[:, t, :], start=(t == 0), stop=True)
            for t in range(NTX):
                last = nc.tensor.matmul(cp[:, NTX, :], ones, Ms[:, t, :], start=(t == 0), stop=(t == NTX - 1))
            last.then_inc(counts, 1)
            pe.wait_ge(be_ready, 1)
            nc.tensor.matmul(bp[0:1, :], be[:], ident, start=True, stop=True).then_inc(bp_ready, 1)
            pe.wait_ge(tab_full, 16)
            pe.wait_ge(done, 1)
            nc.tensor.transpose(bp[:, 0:NBLK], tab[:], ident[0:NBLK, 0:NBLK]).then_inc(tab_turned, 1)

        @block.scalar
        def _(act):
            act.wait_ge(shifted, 1)
            nc.scalar.activation(eg[:], g1[:], ACT.Exp).then_inc(exps, 1)
            for t in range(NTX):
                act.wait_ge(turned, t + 1)
                if t >= 2:
                    act.wait_ge(stored[t % 2], 16)
                nc.scalar.copy(rows[:, t % 2, :], tp[:, t % 2, :]).then_inc(rows_out, 1)
            act.wait_ge(shifted2, 1)
            nc.scalar.activation(p[:], p[:], ACT.Exp).then_inc(exps2, 1)

        @block.vector
        def _(dve):
            tt, ts, rd = nc.vector.tensor_tensor, nc.vector.tensor_scalar, nc.vector.tensor_reduce
            over_g = lambda a: a[:].unsqueeze(2).broadcast_to([P, NTX, NG])
            over_e = lambda a: a[:].unsqueeze(2).broadcast_to([P, NTX, EPG])
            rank_g = K.const("group_rank").unsqueeze(1).broadcast_to([P, NTX, NG])
            rank_e = K.const("expert_rank").unsqueeze(1).broadcast_to([P, NTX, EPG])
            dve.wait_ge(logits, 1)
            tt(L[:], lp[:], K.row("b_router").unsqueeze(1).broadcast_to([P, NTX, NG + NE]), ALU.add)
            dve.drain()
            rd(gm[:], L[:, :, 0:NG], AX_X, ALU.max)
            dve.drain()
            tt(g1[:], L[:, :, 0:NG], over_g(gm), ALU.subtract).then_inc(shifted, 1)
            tt(g2[:], L[:, :, 0:NG], over_g(gm), ALU.is_equal)
            dve.drain()
            tt(g2[:], g2[:], rank_g, ALU.mult)
            dve.drain()
            rd(gm[:], g2[:], AX_X, ALU.max)
            dve.drain()
            tt(oh[:], g2[:], over_g(gm), ALU.is_equal)
            dve.drain()
            tt(pick[:], L[:, :, NG:].rearrange("p t (g j) -> p t j g", g=NG),
               oh[:].unsqueeze(2).broadcast_to([P, NTX, EPG, NG]), ALU.mult)
            dve.drain()
            rd(p[:], pick[:], AX_X, ALU.add)
            dve.drain()
            rd(m0[:], p[:], AX_X, ALU.max)
            dve.drain()
            tt(p[:], p[:], over_e(m0), ALU.subtract).then_inc(shifted2, 1)
            dve.wait_ge(exps, 1)
            rd(gs[:], eg[:], AX_X, ALU.add)
            dve.drain()
            nc.vector.reciprocal(gs[:], gs[:])
            dve.wait_ge(exps2, 1)
            rd(m0[:], p[:], AX_X, ALU.add)
            dve.drain()
            nc.vector.reciprocal(m0[:], m0[:])
            dve.drain()
            tt(p[:], p[:], over_e(m0), ALU.mult)
            dve.drain()
            for k in range(TOPK):
                rd(top[:, k, :], p[:], AX_X, ALU.max)
                dve.drain()
                tt(e1[:], p[:], top[:, k, :].unsqueeze(2).broadcast_to([P, NTX, EPG]), ALU.is_equal)
                dve.drain()
                tt(e1[:], e1[:], rank_e, ALU.mult)
                dve.drain()
                rd(m1[:], e1[:], AX_X, ALU.max)
                dve.drain()
                tt(chosen[:, k], e1[:], over_e(m1), ALU.is_equal)
                dve.drain()
                if k + 1 < TOPK:
                    nc.vector.scalar_tensor_tensor(p[:], chosen[:, k], -2.0, p[:], ALU.mult, ALU.add)
                    dve.drain()
            tt(m0[:], top[:, 0, :], top[:, 1, :], ALU.add)
            dve.drain()
            nc.vector.reciprocal(m0[:], m0[:])
            for k in range(TOPK):
                tt(gate[:, k, :], top[:, k, :], gs[:], ALU.mult)
                for t in range(NTX):
                    tt(M[:, k, t, :].rearrange("p (g j) -> p g j", g=NG),
                       oh[:, t, :].unsqueeze(2).broadcast_to([P, NG, EPG]),
                       chosen[:, k, t, :].unsqueeze(1).broadcast_to([P, NG, EPG]), ALU.mult)
            dve.drain()
            for k in range(TOPK):
                tt(gate[:, k, :], gate[:, k, :], m0[:], ALU.mult)
            tt(Ms[:], M[:, 0], M[:, 1], ALU.add)
            dve.drain()
            dve.sem_inc(assigned, 1)
            dve.wait_ge(counts, 1)
            nc.vector.tensor_copy(cnt[:], cp[:, NTX, :])
            dve.drain()
            ts(nb[:], cnt[:], 0.0, None, ALU.is_gt)
            for m in range(1, TX // MB):
                dve.drain()
                nc.vector.scalar_tensor_tensor(nb[:], cnt[:], float(MB * m), nb[:], ALU.is_gt, ALU.add)
            dve.drain()
            src, step, i = nb, 1, 0
            while step < NE:
                dst = (ca, cb)[i % 2]
                tt(dst[:, step:], src[:, step:], src[:, 0:NE - step], ALU.add)
                nc.vector.tensor_copy(dst[:, 0:step], src[:, 0:step])
                dve.drain()
                src, step, i = dst, 2 * step, i + 1
            spare = (ca, cb)[i % 2]
            tt(start[:], src[:], nb[:], ALU.subtract)
            ts(spare[:], src[:], K.const("blk"), None, ALU.is_le)
            dve.drain()
            rd(be[:], spare[:], AX_X, ALU.add)
            ts(start[:], start[:], float(MB), None, ALU.mult)
            dve.drain()
            ts(be[:], be[:], float(NE - 1), None, ALU.min).then_inc(be_ready, 1)
            tt(where[:], cp[:, 0:NTX, :], start[:].unsqueeze(1).broadcast_to([P, NTX, NE]), ALU.add)
            dve.drain()
            for k in range(TOPK):
                tt(picked[:, k], M[:, k], where[:], ALU.mult)
            dve.drain()
            for k in range(TOPK):
                rd(destf[:, k, :], picked[:, k], AX_X, ALU.add)
            dve.drain()
            nc.vector.tensor_copy(dest[:], destf[:])
            dve.drain()
            dve.sem_inc(dest_ready, 1)
            dve.wait_ge(bp_ready, 1)
            nc.vector.tensor_copy(blocks[0:1, :], bp[0:1, 0:NBLK])
            dve.drain()
            dve.sem_inc(done, 1)
            dve.wait_ge(tab_turned, 1)
            nc.vector.tensor_copy(slots[:], bp[:, 0:NBLK])
            dve.drain()


def experts(K, w_gate, w_up, w_down, h_rows, y_rows, slots, blocks):
    nc = K.nc
    ident = K.const("ident")
    with ExitStack() as ctx:
        wg, wu = ([K.sb(ctx, f"exp_{n}{u}", [P, KD, DE]) for u in range(2)] for n in ("gate", "up"))
        wd = [K.sb(ctx, f"exp_down{u}", [P, KE, D]) for u in range(2)]
        idx = [K.sb(ctx, f"exp_idx{u}", [P, 1], U32) for u in range(2)]
        xr = [K.sb(ctx, f"exp_x{u}", [P, D]) for u in range(2)]
        xT = K.sb(ctx, "exp_xT", [P, KD, P])
        act_ = K.sb(ctx, "exp_silu", [P, DE])
        hid = K.sb(ctx, "exp_hid", [P, KE, P])
        y = [K.sb(ctx, f"exp_y{u}", [P, D]) for u in range(2)]
        tp = K.ps(ctx, "exp_turned", [P, D])
        gp = K.ps(ctx, "exp_gate_acc", [P, DE])
        up = K.ps(ctx, "exp_up_acc", [P, DE])
        yp = K.ps(ctx, "exp_down_acc", [P, D])
        w_full, x_full, y_out, y_stored = ([K.sem(f"ex_{n}{u}") for u in range(2)] for n in ("w", "x", "y", "stored"))
        turned, xT_full, up_ready, silu, hid_full, y_ready = (
            K.sem("ex_" + n) for n in ("turned", "xT", "up", "silu", "hid", "y"))
        block = ctx.enter_context(K.block())

        @block.sync
        def _(sp):
            with sp.Fori(0, NBLK // 2) as it:
                for u in range(2):
                    e = sp.value_load(blocks[0:1, at(it * 2 + u)], min_val=0, max_val=NE - 1)
                    sp.wait_ge(y_ready, it * 2 + u + 1)
                    sp.dma_start(wg[u][:], w_gate[at(e)].rearrange("e (c p) n -> p (e c) n", p=P)).then_inc(w_full[u], 16)
                    sp.dma_start(wu[u][:], w_up[at(e)].rearrange("e (c p) n -> p (e c) n", p=P)).then_inc(w_full[u], 16)
                    sp.dma_start(wd[u][:], w_down[at(e)].rearrange("e (c p) n -> p (e c) n", p=P)).then_inc(w_full[u], 16)

        @block.gpsimd
        def _(pool):
            with pool.Fori(0, NBLK // 2) as it:
                for u in range(2):
                    b = it * 2 + u
                    pool.wait_ge(turned, b + 1)
                    nc.gpsimd.tensor_copy(idx[u][:], slots[:, at(b)])
                    pool.drain()
                    nc.gpsimd.indirect_dma_start(out=xr[u][:], out_offset=None, in_=h_rows,
                                                 in_offset=bass.IndirectOffsetOnAxis(ap=idx[u][:], axis=0)).then_inc(x_full[u], 16)

        @block.tensor
        def _(pe):
            pe.sem_inc(turned, 2)
            pe.sem_inc(y_ready, 2)

            def turn(u, b, visit):
                pe.wait_ge(x_full[u], visit * 16 + 16)
                pe.wait_ge(xT_full, b + 1)
                for c in range(KD):
                    last = nc.tensor.transpose(tp[:, c * P:(c + 1) * P], xr[u][:, c * P:(c + 1) * P], ident)
                last.then_inc(turned, 1)

            def pair(it, more):
                for u in range(2):
                    b = it * 2 + u
                    pe.wait_ge(w_full[u], it * 48 + 48)
                    pe.wait_ge(xT_full, b + 2)
                    pe.wait_ge(hid_full, b + 1)
                    for acc, w in ((gp, wg[u]), (up, wu[u])):
                        for n in range(KE):
                            for c in range(KD):
                                last = nc.tensor.matmul(acc[:, n * P:(n + 1) * P], w[:, c, n * P:(n + 1) * P], xT[:, c, :],
                                                        start=(c == 0), stop=(c == KD - 1))
                        last.then_inc(up_ready, 1)
                    if u == 0 or more:
                        turn(1 - u, b + 1, it + u)
                    pe.wait_ge(hid_full, b + 2)
                    pe.wait_ge(y_out[1 - u], it + 1)
                    for n in range(2):
                        for c in range(KE):
                            last = nc.tensor.matmul(yp[:, n * 512:(n + 1) * 512], hid[:, c, :], wd[u][:, c, n * 512:(n + 1) * 512],
                                                    start=(c == 0), stop=(c == KE - 1))
                    last.then_inc(y_ready, 1)

            turn(0, 0, 0)
            with pe.Fori(0, NBLK // 2 - 1) as it:
                pair(it, True)
            pair(NBLK // 2 - 1, False)

        @block.scalar
        def _(act):
            act.sem_inc(xT_full, 1)
            for u in range(2):
                act.sem_inc(y_stored[u], 16)

            def take(b):
                act.wait_ge(turned, b + 3)
                nc.scalar.copy(xT[:].rearrange("p c i -> p (c i)"), tp[:]).then_inc(xT_full, 1)

            def pair(it, more):
                for u in range(2):
                    b = it * 2 + u
                    act.wait_ge(up_ready, b * 2 + 1)
                    act.wait_ge(hid_full, b + 1)
                    nc.scalar.activation(act_[:], gp[:], ACT.Silu).then_inc(silu, 1)
                    if u == 0 or more:
                        take(b + 1)
                    act.wait_ge(y_out[u], it + 1 + u)
                    act.dma_start(y_rows[at(b * MB, MB), :], y[u][:]).then_inc(y_stored[u], 16)

            take(0)
            with act.Fori(0, NBLK // 2 - 1) as it:
                pair(it, True)
            pair(NBLK // 2 - 1, False)
            for u in range(2):
                act.wait_ge(y_stored[u], 16 * (NBLK // 2 + 1))

        @block.vector
        def _(dve):
            dve.sem_inc(hid_full, 1)
            dve.sem_inc(y_out[1], 1)
            with dve.Fori(0, NBLK // 2) as it:
                for u in range(2):
                    b = it * 2 + u
                    dve.wait_ge(silu, b + 1)
                    dve.wait_ge(up_ready, b * 2 + 2)
                    dve.wait_ge(y_ready, b + 2)
                    nc.vector.tensor_tensor(hid[:].rearrange("p c i -> p (c i)"), act_[:], up[:], ALU.mult).then_inc(hid_full, 1)
                    dve.wait_ge(y_ready, b + 3)
                    dve.wait_ge(y_stored[u], it * 16 + 16)
                    nc.vector.tensor_copy(y[u][:], yp[:]).then_inc(y_out[u], 1)


def combine(K, gate, dest, y_rows):
    nc = K.nc
    ident = K.const("ident")
    with ExitStack() as ctx:
        rows = K.sb(ctx, "cmb_rows", [P, TOPK, NTX, D])
        f = K.sb(ctx, "cmb_f", [P, NTX, D])
        tp = K.ps(ctx, "cmb_turned", [P, 2, 2, TX])
        got = [K.sem(f"cmb_got{t}") for t in range(NTX)]
        summed, turned, out = (K.sem("cmb_" + n) for n in ("summed", "turned", "out"))
        block = ctx.enter_context(K.block())

        @block.gpsimd
        def _(pool):
            for t in range(NTX):
                for k in range(TOPK):
                    nc.gpsimd.indirect_dma_start(out=rows[:, k, t, :], out_offset=None, in_=y_rows,
                                                 in_offset=bass.IndirectOffsetOnAxis(ap=dest[:, k, t:t + 1], axis=0)).then_inc(got[t], 16)

        @block.vector
        def _(dve):
            for t in range(NTX):
                dve.wait_ge(got[t], 16 * TOPK)
                nc.vector.tensor_scalar(f[:, t, :], rows[:, 0, t, :], gate[:, 0, t:t + 1], None, ALU.mult)
                dve.drain()
                nc.vector.scalar_tensor_tensor(f[:, t, :], rows[:, 1, t, :], gate[:, 1, t:t + 1], f[:, t, :],
                                               ALU.mult, ALU.add).then_inc(summed, 1)
            for n in range(KD):
                dve.wait_ge(turned, n + 1)
                nc.vector.scalar_tensor_tensor(K.x[:, n, 0:TX], tp[:, n % 2, 0, :], K.mod[:, 0, 40 + n:41 + n],
                                               K.x[:, n, 0:TX], ALU.mult, ALU.add).then_inc(out, 1)
            dve.drain()

        @block.tensor
        def _(pe):
            pe.wait_ge(summed, NTX)
            for n in range(KD):
                if n >= 2:
                    pe.wait_ge(out, n - 1)
                for t in range(NTX):
                    last = nc.tensor.transpose(tp[:, n % 2, 0, t * P:(t + 1) * P], f[:, t, n * P:(n + 1) * P], ident)
                last.then_inc(turned, 1)


def second_context(K, ctx2T):
    nc = K.nc
    loaded = K.sem("ctx2")
    with K.block() as block:
        @block.sync
        def _(sp):
            sp.dma_start(K.x[:, :, TX:TT], ctx2T.rearrange("(c p) t -> p c t", p=P)).then_inc(loaded, 16)
            sp.wait_ge(loaded, 16)


def second_block(K, io):
    nc = K.nc
    w_in = io["w_in_2"][0]
    second_context(K, io["ctx2T"])
    ada(K, io["w_ada_2"][0], "ada_b2", 1)
    with ExitStack() as ctx:
        h = K.sb(ctx, "mix_h", [P, KD, TT])
        odn = K.sb(ctx, "odn", [P, HEADS, TX])
        norm(K, K.x, h, "norm_mix2", 8, 0, True)
        with ExitStack() as dn:
            qkv = K.sb(dn, "dn_qkv", [P, 3 * HEADS, TT])
            beta, g = (K.sb(dn, n, [P, NT, 8]) for n in ("dn_beta", "dn_g"))
            dn_inputs(K, h, w_in, qkv)
            dn_gates(K, h, w_in, beta, g)
            head_norm(K, qkv[:, 0:HEADS, :], HEADS, TX, qkv[:, 0:HEADS, :], 1.0, EPS, P ** -0.5)
            head_norm(K, qkv[:, HEADS:2 * HEADS, :], HEADS, TT, qkv[:, HEADS:2 * HEADS, :], 1.0, EPS, 1.0)
            deltanet(K, qkv, beta, g, odn)
        ohg = K.sb(ctx, "ohg", [P, HEADS, TX])
        with ExitStack() as hg:
            fi = K.sb(hg, "hg_fi", [P, NT, 3 * HEADS * P])
            q = K.sb(hg, "hg_qs", [P, HEADS, TX])
            with ExitStack() as proj:
                hp = K.sb(proj, "hg_h", [P, KD, TT])
                column_order(K, h, hp)
                features(K, hp, w_in, C_HQ, HEADS, TX,
                         lambda n, sums: nc.scalar.activation(q[:, at(n), :], sums, ACT.Silu))
                token_rows(K, hp, w_in, C_HF, 3 * HEADS * P, NT, fi)
            kk = K.sb(hg, "hg_kk", [P, NT, 2 * HEADS * P])
            hg_gates(K, fi, kk)
            hgrn(K, q, fi, kk, ohg)
        z = K.sb(ctx, "z", [P, HEADS, TX])
        for col, o, gain in ((C_Z_DN, odn, "dn_norm"), (C_Z_HG, ohg, "hg_norm")):
            features(K, h, w_in, col, HEADS, TX, lambda n, sums: nc.scalar.activation(z[:, at(n), :], sums, ACT.Silu))
            head_norm(K, o, HEADS, TX, o, 1.0 / P, EPS, K.vec(gain))
            times(K, o, z)
        m = K.sb(ctx, "merged", [P, KD, TX])
        merge(K, h, w_in, odn, io["w_br_dn_2"][0], ohg, io["w_br_hg_2"][0], m)
        residual(K, m, io["w_out_2"][0], KD, 16, TX)
    h_rows = nc.dram_tensor("h_rows", (TX, D), F32, kind="Internal").ap()
    table = nc.dram_tensor("slot_table", (NBLK * MB, 1), F32, kind="Internal").ap()
    y_rows = nc.dram_tensor("y_rows", (NBLK * MB, D), F32, kind="Internal").ap()
    with ExitStack() as ctx:
        gate = K.sb(ctx, "gate", [P, TOPK, NTX])
        dest = K.sb(ctx, "dest", [P, TOPK, NTX], U32)
        slots = K.sb(ctx, "slots", [P, NBLK], U32)
        blocks = K.sb(ctx, "blocks", [P, NBLK], I32)
        with ExitStack() as rt:
            h = K.sb(rt, "ffn_h", [P, KD, TX])
            norm(K, K.x, h, "norm_ffn2", 32, 24, False)
            route(K, h, io["w_router"], h_rows, table, gate, dest, slots, blocks)
        experts(K, io["w_exp_gate_2"][0], io["w_exp_up_2"][0], io["w_exp_down_2"][0], h_rows, y_rows, slots, blocks)
        combine(K, gate, dest, y_rows)
    norm(K, K.x, K.x, "g_final", 0, 0, False, mod=False)


def store(K, out):
    nc = K.nc
    stored = K.sem("stored")
    with K.block() as block:
        @block.sync
        def _(sp):
            sp.dma_start(out.rearrange("(c p) t -> p c t", p=P), K.x[:, :, 0:TX]).then_inc(stored, 16)
            sp.wait_ge(stored, 16)


def program(nc, io, out):
    with ExitStack() as whole:
        K = Core(nc)
        K.x = K.sb(whole, "x", [P, KD, TT])
        K.consts = K.sb(whole, "consts", [P, N_CONST])
        K.vecs = K.sb(whole, "vecs", [P, N_VEC])
        K.rows = K.sb(whole, "rows", [P, N_ROW])
        K.cond = K.sb(whole, "cond", [P, 4 * KD])
        K.mod = K.sb(whole, "mod", [P, 2, 48])
        K.subln = K.sb(whole, "subln", [P, 1])
        load_all(K, io["consts"], io["vecs"], io["rows"], io["xT"])
        scaled_subln(K)
        first_block(K, io)
        second_block(K, io)
        store(K, out)


def scaled_subln(K):
    nc = K.nc
    with K.block() as block:
        @block.vector
        def _(dve):
            nc.vector.tensor_scalar(K.subln[:], K.vec("subln"), 1.0 - LAM_INIT, None, ALU.mult)
            dve.drain()


def layout(inputs):
    f = {k: np.asarray(v) for k, v in inputs.items()}
    rows = lambda a: np.ascontiguousarray(a).reshape(-1, P)
    taps = lambda a: rows(a)
    vec = {
        "c": f["c"], "c_ctx": f["c_ctx"], "c2": f["c_2"], "c_ctx2": f["c_ctx_2"],
        "ada_b0": f["ada_b"][0], "ada_b1": f["ada_b"][1], "ada_b2": f["b_ada_2"],
        "norm_mix0": f["norm_mix"][0], "norm_mix1": f["norm_mix"][1], "norm_mix2": f["g_mix_2"],
        "norm_ffn0": f["norm_ffn"][0], "norm_ffn1": f["norm_ffn"][1], "norm_ffn2": f["g_ffn_2"],
        "norm_out": f["norm_out"], "g_final": f["g_final_2"],
        "conv0": f["ffn_conv"][0], "conv1": f["ffn_conv"][1],
        "conv_b0": f["ffn_conv_b"][0], "conv_b1": f["ffn_conv_b"][1], "dn_conv": f["dn_conv_2"],
        "subln": f["a_subln"], "dn_norm": f["dn_norm_g_2"], "hg_norm": f["hg_norm_g_2"],
    }
    line = {
        "lam": f["a_lambda"], "a_log": f["dn_a_log_2"], "dt_bias": f["dn_dt_bias_2"],
        "b_router": np.concatenate([f["b_router_grp_2"], f["b_router_exp_2"]], 1), "lb": f["hg_lb_logits_2"],
    }
    c = np.arange(GRID_W)
    dx = c[None, :] - c[:, None] + KW - 1
    inside = (dx >= 0) & (dx < 2 * KW - 1)
    wide = np.concatenate([f["b_rpb"][0], np.zeros((D // HD, 2 * KH - 1, 1), np.float32)], 2)
    bias = wide[:, :, np.where(inside, dx, 2 * KW - 1)]
    out = {k: f[k] for k in ("ada_w", "ffn_up", "ffn_down", "a_wqkv", "a_wo", "b_wqkv", "b_wo",
                             "w_ada_2", "w_in_2", "w_br_dn_2", "w_br_hg_2", "w_out_2",
                             "w_exp_gate_2", "w_exp_up_2", "w_exp_down_2")}
    out["xT"] = np.concatenate([f["x"][0].T, f["ctx"][0].T], 1)
    out["ctx2T"] = f["ctx_2"][0].T
    out["vecs"] = np.concatenate([rows(vec[n]) for n in VECS], 0).T
    out["rows"] = np.tile(np.concatenate([line[n].reshape(-1) for n in ROWS])[None], (P, 1))
    out["bias_rows"] = bias.transpose(0, 2, 1, 3)
    out["w_router"] = np.concatenate([f["w_router_grp_2"][0], f["w_router_exp_2"][0]], 1)
    out["consts"] = constants()
    return {k: np.ascontiguousarray(a) for k, a in out.items()}


def kernel(**inputs):
    import concourse.bacc as bacc
    from concourse.bass_utils import run_bass_kernel_spmd

    nc = bacc.Bacc("TRN2", target_bir_lowering=False, num_devices=1)
    arrays = layout(inputs)
    io = {k: nc.dram_tensor(f"in_{k}", a.shape, mybir.dt.from_np(a.dtype), kind="ExternalInput").ap()
          for k, a in arrays.items()}
    out = nc.dram_tensor("out_x", (D, TX), F32, kind="ExternalOutput").ap()
    program(nc, io, out)
    r = run_bass_kernel_spmd(nc, [{f"in_{k}": a for k, a in arrays.items()}], core_ids=[0])
    return np.ascontiguousarray(r.results[0]["out_x"].T)[None]
```

```python
from contextlib import ExitStack, contextmanager

import concourse.bass as bass
import numpy as np
from concourse import mybir
from concourse.alu_op_type import AluOpType as ALU

ACT = mybir.ActivationFunctionType
F32 = mybir.dt.float32
FR = mybir.dt.float32r
U32 = mybir.dt.uint32
I32 = mybir.dt.int32
AX_X = mybir.AxisListType.X

P = 128
D = 1024
KD = D // P
TX, TC = 512, 256
TT = TX + TC
NTX, NTC = TX // P, TC // P
NT = NTX + NTC
GRID_W = 64
GRID_H = TX // GRID_W
HD = 64
FF = 2816
NF = FF // P
EPS = 1e-6
NEG = -1e30
LAM_INIT = 0.8 - 0.6 * float(np.exp(-0.3 * 0))
KW = 16
KH = 8
NSLOT = 14
HEADS = 4
DNQKV = 3 * HEADS * P
C_Z_DN = DNQKV
C_BA = C_Z_DN + HEADS * P
C_HQ = C_BA + 16
C_HF = C_HQ + HEADS * P
C_HI = C_HF + 2 * HEADS * P
C_Z_HG = C_HI + HEADS * P
C_GATE = C_Z_HG + HEADS * P
N_IN = C_GATE + 2 * D
LEVELS = 7
NG, EPG = 4, 8
NE = NG * EPG
DE = D // 2
KE = DE // P
TOPK = 2
MB = P
NBLK = (TX * TOPK + NE * (MB - 1) + MB - 1) // MB
NPAIR = NBLK // 2
F_TINY = 1e-30
LN_SHIFT = 60

VECS = {}
_at = 0
for _n, _k in (
    ("c", KD), ("c_ctx", KD), ("c2", KD), ("c_ctx2", KD),
    ("ada_b0", 48), ("ada_b1", 48), ("ada_b2", 48),
    ("norm_mix0", KD), ("norm_mix1", KD), ("norm_mix2", KD),
    ("norm_ffn0", KD), ("norm_ffn1", KD), ("norm_ffn2", KD), ("norm_out", KD), ("g_final", KD),
    ("conv0", 6 * NF), ("conv1", 6 * NF), ("conv_b0", 2 * NF), ("conv_b1", 2 * NF), ("dn_conv", 3 * 12),
    ("subln", 1), ("dn_norm", 1), ("hg_norm", 1),
):
    VECS[_n] = (_at, _k)
    _at += _k
N_VEC = _at
ROWS = {}
_at = 0
for _n, _k in (("lam", 4 * HD), ("a_log", 8), ("dt_bias", 8), ("b_router", NG + NE), ("lb", HEADS * P)):
    ROWS[_n] = (_at, _k)
    _at += _k
N_ROW = _at
CONST = {}
_at = 0
for _n, _k in (
    ("ident", P), ("ones", P), ("rot", P), ("incl", 2 * P), ("strict", 2 * P), ("level", 2 * LEVELS * P),
    ("cos", TX), ("sin", TX), ("window", GRID_W), ("group_rank", NG), ("expert_rank", EPG),
    ("blk", 1), ("tokid", NTX), ("pick", 2 * KD - 1),
):
    CONST[_n] = (_at, _k)
    _at += _k
N_CONST = _at


def constants():
    out = np.zeros((P, N_CONST), np.float32)

    def put(name, a):
        at, k = CONST[name]
        out[:, at:at + k] = np.asarray(a, np.float32).reshape(P, k)

    i, j = np.arange(P)[None, :], np.arange(P)[:, None]
    put("ident", i == j)
    put("ones", np.ones((P, P)))
    rot = np.zeros((P, P))
    for b in range(0, P, 32):
        for e in range(16):
            rot[b + 16 + e, b + e] = -1
            rot[b + e, b + 16 + e] = 1
    put("rot", rot)
    put("incl", np.stack([j <= i, j >= i], 1))
    put("strict", np.stack([j < i, j > i], 1))
    level = np.zeros((P, 2, LEVELS, P))
    for n in range(LEVELS):
        s = 1 << n
        m = (j // (2 * s) == i // (2 * s)) & (j % (2 * s) < s) & (i % (2 * s) >= s)
        level[:, 0, n], level[:, 1, n] = m, m.T
    put("level", level)
    inv = np.float32(10000.0) ** (-np.arange(16, dtype=np.float32) / np.float32(16))
    t = np.arange(TX)
    row = (t // GRID_W).astype(np.float32)[:, None] * inv[None]
    col = (t % GRID_W).astype(np.float32)[:, None] * inv[None]
    ang = np.concatenate([row, row, col, col], 1).T
    ang = np.concatenate([ang, ang], 0)
    put("cos", np.cos(ang))
    put("sin", np.sin(ang))
    c = np.arange(GRID_W)
    start = np.clip(c - KW // 2, 0, GRID_W - KW)
    ok = (c[None] >= start[:, None]) & (c[None] < start[:, None] + KW)
    window = np.where(ok, 0.0, NEG)
    put("window", np.concatenate([window, window], 0))
    put("group_rank", np.tile(NG - np.arange(NG), (P, 1)))
    put("expert_rank", np.tile(EPG - np.arange(EPG), (P, 1)))
    put("blk", np.arange(P))
    put("pick", np.tile(np.arange(2 * KD - 1) == KD - 1, (P, 1)))
    put("tokid", np.arange(P)[:, None] + P * np.arange(NTX)[None])
    return out


class Core:

    def __init__(self, nc):
        self.nc, self.n, self.fresh, self.spent, self.place = nc, 0, [], [], {}

    def sem(self, name):
        self.n += 1
        self.fresh.append(self.nc.alloc_semaphore(f"{name}_{self.n}"))
        return self.fresh[-1]

    def sb(self, ctx, name, shape, dt=F32):
        self.n += 1
        t = ctx.enter_context(self.nc.sbuf_tensor(f"{name}_{self.n}", shape, dt))
        self.place[t.name] = self.nc.sbuf_base - 4 * int(np.prod(shape[1:]))
        return t

    def lo(self, t):
        self.n += 1
        return self.nc.alloc_sbuf_tensor_at(f"lo_{self.n}", list(t.shape), FR, offset=self.place[t.name])

    def ps(self, ctx, name, shape, dt=F32):
        self.n += 1
        return ctx.enter_context(self.nc.psum_tensor(f"{name}_{self.n}", shape, dt))

    def const(self, name):
        at, k = CONST[name]
        return self.consts[:, at:at + k]

    def vec(self, name, i=0, k=None):
        at, n = VECS[name]
        return self.vecs[:, at + i:at + i + (n if k is None else k)]

    def row(self, name):
        at, k = ROWS[name]
        return self.rows[:, at:at + k]

    @contextmanager
    def block(self):
        mine, self.fresh = self.fresh, []
        for spent in self.spent:
            self.nc.gpsimd.sem_clear(spent)
        with self.nc.Block() as block:
            yield block
        for spent in self.spent:
            self.nc.release_semaphore(spent)
        self.spent = mine


def at(i, k=1):
    return bass.ds(i, k)


def products(nc, out, left, right, start, stop):
    nc.tensor.matmul(out, left[0], right[0], start=start, stop=False)
    nc.tensor.matmul(out, left[0], right[1], start=False, stop=False)
    return nc.tensor.matmul(out, left[1], right[0], start=False, stop=stop)


def lo_of(engine, lo, value, hi):
    return engine.tensor_tensor(lo, value, hi.bitcast(F32), ALU.subtract)


def load_all(K, consts, vecs, rows):
    nc = K.nc
    loaded, siluc = K.sem("loaded"), K.sem("siluc")
    with K.block() as block:
        @block.sync
        def _(sp):
            sp.dma_start(K.consts[:], consts).then_inc(loaded, 16)
            sp.dma_start(K.vecs[:], vecs).then_inc(loaded, 16)
            sp.dma_start(K.rows[:], rows).then_inc(loaded, 16)
            sp.wait_ge(loaded, 48)

        @block.scalar
        def _(act):
            act.wait_ge(loaded, 48)
            nc.scalar.activation(K.cond[:], K.vec("c", 0, 4 * KD), ACT.Silu).then_inc(siluc, 1)
            act.wait_ge(siluc, 1)


def ada(K, w, bias, pair, also):
    nc = K.nc
    G = 512
    n_groups = 6 * D // G
    U = 3
    wv = w.rearrange("(c p) n -> p c n", p=P)
    ident = K.const("ident")
    with ExitStack() as ctx:
        wt = [K.sb(ctx, f"ada_w{u}", [P, KD, G]) for u in range(U)]
        wh = [K.sb(ctx, f"ada_w_hi{u}", [P, KD, G], FR) for u in range(U)]
        wl = [K.lo(t) for t in wt]
        cond = K.sb(ctx, "ada_cond", [P, KD, 2])
        both = K.sb(ctx, "ada_both", [P, KD, 4], FR)
        row = K.sb(ctx, "ada_row", [4, 6 * D])
        acc = K.ps(ctx, "ada_acc", [P, U, G])
        turned = K.ps(ctx, "ada_turned", [P, 6 * KD, 4])
        w_full, w_hi, w_split, acc_full, acc_free = (
            [K.sem("ada_" + n) for _ in range(U)] for n in ("w_full", "w_hi", "w_split", "acc_full", "acc_free"))
        laid, columns, also_loaded = K.sem("ada_laid"), K.sem("ada_columns"), K.sem("ada_also")
        block = ctx.enter_context(K.block())

        @block.sync
        def _(sp):
            with sp.Fori(0, n_groups // U) as it:
                for u in range(U):
                    sp.wait_ge(acc_full[u], it + 1)
                    sp.dma_start(wt[u][:], wv[:, :, at((it * U + u) * G, G)]).then_inc(w_full[u], 16)

        @block.tensor
        def _(pe):
            for u in range(U):
                pe.sem_inc(acc_full[u], 1)
            pe.wait_ge(laid, 1)
            with pe.Fori(0, n_groups // U) as it:
                for u in range(U):
                    pe.wait_ge(w_split[u], it + 1)
                    pe.wait_ge(acc_free[u], it + 1)
                    for c in range(KD):
                        nc.tensor.matmul(acc[0:4, u, :], both[:, c, :], wh[u][:, c, :], start=(c == 0), stop=False)
                        last = nc.tensor.matmul(acc[0:4, u, :], both[:, c, :], wl[u][:, c, :], start=False, stop=(c == KD - 1))
                    last.then_inc(acc_full[u], 1)
            for u in range(U):
                pe.wait_ge(acc_free[u], n_groups // U + 1)
            for n in range(6 * KD):
                last = nc.tensor.transpose(turned[:, n, :], row[:, n * P:(n + 1) * P], ident[0:4, 0:4])
            last.then_inc(columns, 1)

        @block.scalar
        def _(act):
            if also:
                act.dma_start(also[0], also[1].rearrange("(c p) t -> p c t", p=P)).then_inc(also_loaded, 16)
            for u in range(U):
                act.sem_inc(acc_free[u], 1)

            def hi_weights(it, u):
                act.wait_ge(w_full[u], it * 16 + 16)
                nc.scalar.copy(wh[u][:], wt[u][:]).then_inc(w_hi[u], 1)

            def round_of(it, more):
                for u in range(U):
                    if u + 1 < U:
                        hi_weights(it, u + 1)
                    elif more:
                        hi_weights(it + 1, 0)
                    act.wait_ge(acc_full[u], it + 2)
                    nc.scalar.copy(row[:, at((it * U + u) * G, G)], acc[0:4, u, :]).then_inc(acc_free[u], 1)

            hi_weights(0, 0)
            with act.Fori(0, n_groups // U - 1) as it:
                round_of(it, True)
            round_of(n_groups // U - 1, False)
            if also:
                act.wait_ge(also_loaded, 16)

        @block.vector
        def _(dve):
            nc.vector.tensor_copy(cond[:].rearrange("p c s -> p s c"),
                                  K.cond[:].rearrange("p (b s c) -> p b s c", b=2, s=2)[:, pair])
            dve.drain()
            nc.vector.tensor_copy(both[:, :, 0:2], cond[:])
            dve.drain()
            nc.vector.tensor_tensor(both[:, :, 2:4], cond[:], both[:, :, 0:2].bitcast(F32), ALU.subtract).then_inc(laid, 1)
            with dve.Fori(0, n_groups // U) as it:
                for u in range(U):
                    dve.wait_ge(w_hi[u], it + 1)
                    lo_of(nc.vector, wl[u][:], wt[u][:], wh[u][:]).then_inc(w_split[u], 1)
            dve.wait_ge(columns, 1)
            for s in range(2):
                nc.vector.tensor_tensor(K.mod[:, s, :], turned[:].rearrange("p n s -> p s n")[:, s], K.vec(bias), ALU.add)
            dve.drain()
            for s in range(2):
                nc.vector.tensor_tensor(K.mod[:, s, :], K.mod[:, s, :], turned[:].rearrange("p n s -> p s n")[:, 2 + s], ALU.add)
            dve.drain()


def norm(K, src, dst, weight, scale_at, shift_at, mod=True):
    nc = K.nc
    T = TX
    parts = ((0, 0, TX),)
    ones = K.const("ones")
    with ExitStack() as ctx:
        rstd = K.sb(ctx, "rstd", [P, T])
        gain = K.sb(ctx, "gain", [P, 2, KD])
        squares = K.sb(ctx, "squares", [P, KD, T]) if dst is src else dst
        ss = K.ps(ctx, "ss", [P, 1024])
        sq, summed, inv, root, scaled, gained, done = (
            K.sem("norm_" + n) for n in ("sq", "summed", "inv", "root", "scaled", "gained", "done"))
        block = ctx.enter_context(K.block())

        @block.scalar
        def _(act):
            for c in range(KD):
                nc.scalar.activation(squares[:, c, 0:T], src[:, c, 0:T], ACT.Square).then_inc(sq, 1)
            act.wait_ge(inv, 1)
            nc.scalar.activation(rstd[:], rstd[:], ACT.Sqrt).then_inc(root, 1)
            act.wait_ge(gained, 1)
            for c in range(KD):
                act.wait_ge(scaled, c + 1)
                for s, a, b in parts:
                    bias = K.mod[:, s, shift_at + c:shift_at + c + 1] if mod else 0.0
                    last = nc.scalar.activation(dst[:, c, a:b], dst[:, c, a:b], ACT.Identity,
                                                bias=bias, scale=gain[:, s, c:c + 1])
                last.then_inc(done, 1)
            act.wait_ge(done, KD)

        @block.tensor
        def _(pe):
            for c in range(KD):
                pe.wait_ge(sq, c + 1)
                for s, a, b in parts:
                    last = nc.tensor.matmul(ss[:, a:b], ones, squares[:, c, a:b], start=(c == 0), stop=(c == KD - 1))
            last.then_inc(summed, 1)

        @block.vector
        def _(dve):
            for s, a, b in parts:
                if mod:
                    nc.vector.scalar_tensor_tensor(gain[:, s, :], K.mod[:, s, scale_at:scale_at + KD], 1.0,
                                                   K.vec(weight), ALU.add, ALU.mult)
                else:
                    nc.vector.tensor_copy(gain[:, s, :], K.vec(weight))
            dve.drain()
            dve.sem_inc(gained, 1)
            dve.wait_ge(summed, 1)
            nc.vector.tensor_scalar(rstd[:], ss[:, 0:T], 1.0 / D, EPS, ALU.mult, ALU.add)
            dve.drain()
            nc.vector.reciprocal(rstd[:], rstd[:]).then_inc(inv, 1)
            dve.wait_ge(root, 1)
            for c in range(KD):
                nc.vector.tensor_tensor(dst[:, c, 0:T], src[:, c, 0:T], rstd[:], ALU.mult).then_inc(scaled, 1)


class Normed:

    def __init__(self, K, ctx, weight, scale_at, shift_at, ctx_tokens, by_column=False):
        self.K, self.weight, self.scale_at, self.shift_at, self.by_column = K, weight, scale_at, shift_at, by_column
        self.T = TT if ctx_tokens else TX
        self.spans = ((0, 0, TX), (1, TX, TT)) if ctx_tokens else ((0, 0, TX),)
        self.h = K.sb(ctx, "normed", [P, KD, self.T])
        self.hi = K.sb(ctx, "normed_hi", [P, KD, self.T], FR)
        self.lo = K.lo(self.h)
        self.parts = (self.hi, self.lo)
        self.rstd = K.sb(ctx, "rstd", [P, self.T])
        self.gain = K.sb(ctx, "gain", [P, 2, KD])
        self.squared, self.summed, self.inv, self.root, self.gained, self.scaled, self.shifted, self.hi_ready, self.ready = (
            K.sem("normed_" + n) for n in ("squared", "summed", "inv", "root", "gained", "scaled", "shifted", "hi", "ready"))

    def squares(self, act):
        for c in range(KD):
            self.K.nc.scalar.activation(self.h[:, c, :], self.K.x[:, c, 0:self.T], ACT.Square).then_inc(self.squared, 1)

    def scalar(self, act):
        nc = self.K.nc
        act.wait_ge(self.inv, 1)
        nc.scalar.activation(self.rstd[:], self.rstd[:], ACT.Sqrt).then_inc(self.root, 1)
        act.wait_ge(self.gained, 1)
        for c in range(KD):
            act.wait_ge(self.scaled, c + 1)
            for s, a, b in self.spans:
                last = nc.scalar.activation(self.h[:, c, a:b], self.h[:, c, a:b], ACT.Identity,
                                            bias=self.K.mod[:, s, self.shift_at + c:self.shift_at + c + 1],
                                            scale=self.gain[:, s, c:c + 1])
            last.then_inc(self.shifted, 1)

    def tensor(self, pe, sums):
        for c in range(KD):
            pe.wait_ge(self.squared, c + 1)
            for _, a, b in self.spans:
                last = self.K.nc.tensor.matmul(sums[:, a:b], self.K.const("ones"), self.h[:, c, a:b],
                                               start=(c == 0), stop=(c == KD - 1))
        last.then_inc(self.summed, 1)

    def gains(self, dve):
        for s, _, _ in self.spans:
            last = self.K.nc.vector.scalar_tensor_tensor(
                self.gain[:, s, :], self.K.mod[:, s, self.scale_at:self.scale_at + KD], 1.0, self.K.vec(self.weight),
                ALU.add, ALU.mult)
        dve.drain()
        dve.sem_inc(self.gained, 1)

    def scale(self, c):
        tt, x, h, rstd = self.K.nc.vector.tensor_tensor, self.K.x, self.h, self.rstd
        if not self.by_column:
            return tt(h[:, c, :], x[:, c, 0:self.T], rstd[:], ALU.mult)
        columns = lambda a: a.rearrange("p (r c) -> p c r", r=GRID_H)
        tt(h[:, c, 0:TX].rearrange("p (c r) -> p c r", r=GRID_H), columns(x[:, c, 0:TX]), columns(rstd[:, 0:TX]), ALU.mult)
        return tt(h[:, c, TX:self.T], x[:, c, TX:self.T], rstd[:, TX:self.T], ALU.mult)

    def vector(self, dve, sums):
        nc = self.K.nc
        dve.wait_ge(self.summed, 1)
        nc.vector.tensor_scalar(self.rstd[:], sums[:, 0:self.T], 1.0 / D, EPS, ALU.mult, ALU.add)
        dve.drain()
        nc.vector.reciprocal(self.rstd[:], self.rstd[:]).then_inc(self.inv, 1)
        dve.wait_ge(self.root, 1)
        for c in range(2):
            self.scale(c).then_inc(self.scaled, 1)
        for c in range(KD):
            if c + 2 < KD:
                self.scale(c + 2).then_inc(self.scaled, 1)
            dve.wait_ge(self.shifted, c + 1)
            nc.vector.tensor_copy(self.hi[:, c, :], self.h[:, c, :]).then_inc(self.hi_ready, 1)
            dve.wait_ge(self.hi_ready, c + 1)
            lo_of(nc.vector, self.lo[:, c, :], self.h[:, c, :], self.hi[:, c, :]).then_inc(self.ready, 1)


def features(K, h, w, col0, n_chunks, tok, evac, first=None):
    nc = K.nc
    wv = w.rearrange("(c p) n -> p c n", p=P)
    parts = ((0, TX), (TX, TT)) if tok == TT else ((0, tok),)
    with ExitStack() as ctx:
        wt = [K.sb(ctx, f"feat_w{u}", [P, KD, P]) for u in range(2)]
        wh = [K.sb(ctx, f"feat_w_hi{u}", [P, KD, P], FR) for u in range(2)]
        wl = [K.lo(t) for t in wt]
        acc = K.ps(ctx, "feat_acc", [P, 2, 1024])
        sums = K.ps(ctx, "feat_norm", [P, 1024])
        w_full, w_hi, w_split, acc_full, acc_free = (
            [K.sem("feat_" + n) for _ in range(2)] for n in ("w_full", "w_hi", "w_split", "acc_full", "acc_free"))
        block = ctx.enter_context(K.block())

        @block.sync
        def _(sp):
            with sp.Fori(0, n_chunks // 2) as it:
                for u in range(2):
                    sp.wait_ge(acc_full[u], it + 1)
                    sp.dma_start(wt[u][:], wv[:, :, at((it * 2 + u) * P + col0, P)]).then_inc(w_full[u], 16)

        @block.vector
        def _(dve):
            def split(it):
                for u in range(2):
                    dve.wait_ge(w_full[u], it * 16 + 16)
                    nc.vector.tensor_copy(wh[u][:], wt[u][:]).then_inc(w_hi[u], 1)
                    dve.wait_ge(w_hi[u], it + 1)
                    lo_of(nc.vector, wl[u][:], wt[u][:], wh[u][:]).then_inc(w_split[u], 1)

            if first:
                first.gains(dve)
            split(0)
            if first:
                first.vector(dve, sums)
            with dve.Fori(0, n_chunks // 2 - 1) as it:
                split(it + 1)

        @block.tensor
        def _(pe):
            for u in range(2):
                pe.sem_inc(acc_full[u], 1)
            if first:
                first.tensor(pe, sums)
            with pe.Fori(0, n_chunks // 2) as it:
                for u in range(2):
                    pe.wait_ge(w_split[u], it + 1)
                    pe.wait_ge(acc_free[u], it + 1)
                    for c in range(KD):
                        if first and u == 0:
                            pe.wait_ge(first.ready, c + 1)
                        for a, b in parts:
                            last = products(nc, acc[:, u, a:b], (wh[u][:, c, :], wl[u][:, c, :]),
                                            [t[:, c, a:b] for t in h], c == 0, c == KD - 1)
                    last.then_inc(acc_full[u], 1)

        @block.scalar
        def _(act):
            for u in range(2):
                act.sem_inc(acc_free[u], 1)
            if first:
                first.squares(act)
                first.scalar(act)
            with act.Fori(0, n_chunks // 2) as it:
                for u in range(2):
                    act.wait_ge(acc_full[u], it + 2)
                    evac(it * 2 + u, acc[:, u:u + 1, 0:tok]).then_inc(acc_free[u], 1)


def token_rows(K, h, w, col0, n_cols, tiles, dst):
    nc = K.nc
    G = 256
    wv = w.rearrange("(c p) n -> p c n", p=P)
    with ExitStack() as ctx:
        wt = [K.sb(ctx, f"tok_w{u}", [P, KD, G]) for u in range(2)]
        wh = [K.sb(ctx, f"tok_w_hi{u}", [P, KD, G], FR) for u in range(2)]
        wl = [K.lo(t) for t in wt]
        acc = K.ps(ctx, "tok_acc", [P, tiles, 512])
        w_full, w_hi, w_split = ([K.sem("tok_" + n) for _ in range(2)] for n in ("w_full", "w_hi", "w_split"))
        acc_full, acc_free = ([K.sem("tok_" + n) for _ in range(tiles)] for n in ("acc_full", "acc_free"))
        block = ctx.enter_context(K.block())

        @block.sync
        def _(sp):
            with sp.Fori(0, n_cols // G // 2) as it:
                for u in range(2):
                    sp.wait_ge(acc_full[tiles - 1], it * 2 + u + 1)
                    sp.dma_start(wt[u][:], wv[:, :, at((it * 2 + u) * G + col0, G)]).then_inc(w_full[u], 16)

        @block.vector
        def _(dve):
            with dve.Fori(0, n_cols // G // 2) as it:
                for u in range(2):
                    dve.wait_ge(w_full[u], it * 16 + 16)
                    nc.vector.tensor_copy(wh[u][:], wt[u][:]).then_inc(w_hi[u], 1)
                    dve.wait_ge(w_hi[u], it + 1)
                    lo_of(nc.vector, wl[u][:], wt[u][:], wh[u][:]).then_inc(w_split[u], 1)

        @block.tensor
        def _(pe):
            pe.sem_inc(acc_full[tiles - 1], 2)
            with pe.Fori(0, n_cols // G // 2) as it:
                for u in range(2):
                    pe.wait_ge(w_split[u], it + 1)
                    for t in range(tiles):
                        pe.wait_ge(acc_free[t], it * 2 + u + 1)
                        for c in range(KD):
                            last = products(nc, acc[:, t, 0:G], [a[:, c, t * P:(t + 1) * P] for a in h],
                                            (wh[u][:, c, :], wl[u][:, c, :]), c == 0, c == KD - 1)
                        last.then_inc(acc_full[t], 1)

        @block.scalar
        def _(act):
            for t in range(tiles):
                act.sem_inc(acc_free[t], 1)
            with act.Fori(0, n_cols // G // 2) as it:
                for u in range(2):
                    for t in range(tiles):
                        act.wait_ge(acc_full[t], it * 2 + u + (1 if t < tiles - 1 else 3))
                        nc.scalar.copy(dst[:, t, at((it * 2 + u) * G, G)], acc[:, t, 0:G]).then_inc(acc_free[t], 1)


def rope(K, qk, n_chunks):
    nc = K.nc
    with ExitStack() as ctx:
        turned = [K.sb(ctx, f"turned{u}", [P, 1, TX]) for u in range(2)]
        acc = K.ps(ctx, "rope_acc", [P, 2, TX])
        acc_full = [K.sem("rope_full") for _ in range(2)]
        acc_free = [K.sem("rope_free") for _ in range(2)]
        sin = K.const("sin").unsqueeze(1)
        cos = K.const("cos").unsqueeze(1)
        block = ctx.enter_context(K.block())

        @block.tensor
        def _(pe):
            with pe.Fori(0, n_chunks // 2) as it:
                for u in range(2):
                    pe.wait_ge(acc_free[u], it + 1)
                    nc.tensor.matmul(acc[:, u, :], K.const("rot"), qk[:, at(it * 2 + u), 0:TX],
                                     start=True, stop=True).then_inc(acc_full[u], 1)

        @block.vector
        def _(dve):
            for u in range(2):
                dve.sem_inc(acc_free[u], 1)
            with dve.Fori(0, n_chunks // 2) as it:
                for u in range(2):
                    part = qk[:, at(it * 2 + u), 0:TX]
                    dve.wait_ge(acc_full[u], it + 1)
                    nc.vector.tensor_tensor(turned[u][:], acc[:, u:u + 1, :], sin, ALU.mult)
                    nc.vector.tensor_tensor(part, part, cos, ALU.mult)
                    dve.drain()
                    nc.vector.tensor_tensor(part, part, turned[u][:], ALU.add).then_inc(acc_free[u], 1)


def residual(K, src, w, gate_at, tok):
    nc = K.nc
    wv = w.rearrange("(c p) n -> p c n", p=P)
    parts = ((0, 0, TX), (1, TX, TT)) if tok == TT else ((0, 0, tok),)
    with ExitStack() as ctx:
        hi = K.sb(ctx, "res_hi", [P, KD, tok], FR)
        lo = K.lo(src)
        wt = [K.sb(ctx, f"res_w{u}", [P, KD, P]) for u in range(2)]
        wh = [K.sb(ctx, f"res_w_hi{u}", [P, KD, P], FR) for u in range(2)]
        wl = [K.lo(t) for t in wt]
        acc = K.ps(ctx, "res_acc", [P, 2, 1024])
        w_full, w_hi, w_split, acc_full, acc_free = (
            [K.sem("res_" + n) for _ in range(2)] for n in ("w_full", "w_hi", "w_split", "acc_full", "acc_free"))
        hi_ready, even, odd = (K.sem("res_src_" + n) for n in ("hi", "even", "odd"))
        block = ctx.enter_context(K.block())

        @block.sync
        def _(sp):
            with sp.Fori(0, KD // 2) as it:
                for u in range(2):
                    sp.wait_ge(acc_full[u], it + 1)
                    sp.dma_start(wt[u][:], wv[:, :, at((it * 2 + u) * P, P)]).then_inc(w_full[u], 16)

        @block.scalar
        def _(act):
            with act.Fori(0, KD // 2) as it:
                for u in range(2):
                    act.wait_ge(w_full[u], it * 16 + 16)
                    nc.scalar.copy(wh[u][:], wt[u][:]).then_inc(w_hi[u], 1)

        @block.gpsimd
        def _(pool):
            for c in range(1, KD, 2):
                pool.wait_ge(hi_ready, c + 1)
                lo_of(nc.gpsimd, lo[:, c, 0:tok], src[:, c, 0:tok], hi[:, c, :]).then_inc(odd, 1)
            with pool.Fori(0, KD // 2) as it:
                for u in range(2):
                    pool.wait_ge(w_hi[u], it + 1)
                    lo_of(nc.gpsimd, wl[u][:], wt[u][:], wh[u][:]).then_inc(w_split[u], 1)

        @block.tensor
        def _(pe):
            for u in range(2):
                pe.sem_inc(acc_full[u], 1)
            with pe.Fori(0, KD // 2) as it:
                for u in range(2):
                    pe.wait_ge(w_split[u], it + 1)
                    pe.wait_ge(acc_free[u], it + 1)
                    for c in range(KD):
                        if u == 0:
                            pe.wait_ge(odd if c % 2 else even, c // 2 + 1)
                        for _, a, b in parts:
                            last = products(nc, acc[:, u, a:b], (wh[u][:, c, :], wl[u][:, c, :]),
                                            (hi[:, c, a:b], lo[:, c, a:b]), c == 0, c == KD - 1)
                    last.then_inc(acc_full[u], 1)

        @block.vector
        def _(dve):
            for u in range(2):
                dve.sem_inc(acc_free[u], 1)
            for c in range(KD):
                nc.vector.tensor_copy(hi[:, c, :], src[:, c, 0:tok]).then_inc(hi_ready, 1)
                if c % 2 == 0:
                    dve.wait_ge(hi_ready, c + 1)
                    lo_of(nc.vector, lo[:, c, 0:tok], src[:, c, 0:tok], hi[:, c, :]).then_inc(even, 1)
            with dve.Fori(0, KD // 2) as it:
                for u in range(2):
                    n = it * 2 + u
                    dve.wait_ge(acc_full[u], it + 2)
                    for s, a, b in parts:
                        last = nc.vector.scalar_tensor_tensor(
                            K.x[:, at(n), a:b], acc[:, u:u + 1, a:b], K.mod[:, s, at(n + gate_at)],
                            K.x[:, at(n), a:b], ALU.mult, ALU.add)
                    last.then_inc(acc_free[u], 1)


def ffn(K, first, w_up, w_down, counts, taps, bias, gate_at, tok):
    nc = K.nc
    uv = w_up.rearrange("(c p) (s n) -> p c s n", p=P, s=2)
    dv = w_down.rearrange("(c p) n -> p c n", p=P)
    parts = ((0, 0, TX), (1, TX, TT)) if tok == TT else ((0, 0, tok),)
    tap0, b0 = VECS[taps][0], VECS[bias][0]
    most = max(counts)
    DOWN = KD // 2
    h = first.parts
    pieces, n0 = [], 0
    for p, count in enumerate(counts):
        pieces.append((p, n0, count, n0 // 2 + p * DOWN))
        n0 += count
    with ExitStack() as ctx:
        wt = [K.sb(ctx, f"up_w{u}", [P, KD, 2, P]) for u in range(2)]
        wh = [K.sb(ctx, f"up_w_hi{u}", [P, KD, 2, P], FR) for u in range(2)]
        wl = [K.lo(t) for t in wt]
        dt = [K.sb(ctx, f"down_w{u}", [P, most, P]) for u in range(2)]
        dh = [K.sb(ctx, f"down_w_hi{u}", [P, most, P], FR) for u in range(2)]
        dl = [K.lo(t) for t in dt]
        conv = K.sb(ctx, "conv", [P, 2, 2, tok])
        gated = K.sb(ctx, "gated", [P, most, tok])
        ghi = K.sb(ctx, "gated_hi", [P, most, tok], FR)
        glo = K.lo(gated)
        acc = K.ps(ctx, "ffn_acc", [P, 2, 2, 1024])
        sums = acc[:, 1, 1, :]
        up_full, up_hi, up_split, down_full, down_hi, down_split, acc_full, acc_free, mid, tapped, silu, out = (
            [K.sem("ffn_" + n) for _ in range(2)]
            for n in ("up_full", "up_hi", "up_split", "down_full", "down_hi", "down_split", "acc_full", "acc_free", "mid",
                      "tapped", "silu", "out"))
        gated_ready = K.sem("ffn_gated")
        block = ctx.enter_context(K.block())

        @block.sync
        def _(sp):
            def load_up(n0, it, u):
                for s in range(2):
                    sp.dma_start(wt[u][:, :, s, :], uv[:, :, s, at((it * 2 + u + n0) * P, P)]).then_inc(up_full[u], 16)

            def load_down(n0, count, it, u):
                sp.dma_start(dt[u][:, 0:count, :], dv[:, n0:n0 + count, at((it * 2 + u) * P, P)]).then_inc(down_full[u], 16)

            for u in range(2):
                load_up(0, 0, u)
            for p, n0, count, v0 in pieces:
                for u in range(2):
                    if p > 0:
                        sp.wait_ge(acc_full[u], v0)
                    load_down(n0, count, 0, u)
                with sp.Fori(0, count // 2 - 1) as it:
                    for u in range(2):
                        sp.wait_ge(acc_full[u], it + (v0 + 1))
                        load_up(n0, it + 1, u)
                if p + 1 < len(pieces):
                    for u in range(2):
                        sp.wait_ge(acc_full[u], v0 + count // 2)
                        load_up(n0 + count, 0, u)
                with sp.Fori(0, DOWN - 1) as it:
                    for u in range(2):
                        sp.wait_ge(acc_full[u], it + (v0 + count // 2 + 1))
                        load_down(n0, count, it + 1, u)

        @block.gpsimd
        def _(pool):
            for p, n0, count, v0 in pieces:
                with pool.Fori(0, count // 2) as it:
                    for u in range(2):
                        pool.wait_ge(up_hi[u], it + (n0 // 2 + 1))
                        lo_of(nc.gpsimd, wl[u][:], wt[u][:], wh[u][:]).then_inc(up_split[u], 1)
                with pool.Fori(0, DOWN) as it:
                    for u in range(2):
                        pool.wait_ge(down_hi[u], it + (p * DOWN + 1))
                        lo_of(nc.gpsimd, dl[u][:, 0:count, :], dt[u][:, 0:count, :], dh[u][:, 0:count, :]).then_inc(down_split[u], 1)

        @block.tensor
        def _(pe):
            first.tensor(pe, sums)
            for p, n0, count, v0 in pieces:
                with pe.Fori(0, count // 2) as it:
                    for u in range(2):
                        pe.wait_ge(up_split[u], it + (n0 // 2 + 1))
                        pe.wait_ge(acc_free[u], it + (v0 + 1))
                        for s in range(2):
                            for c in range(KD):
                                if (p, u, s) == (0, 0, 0):
                                    pe.wait_ge(first.ready, c + 1)
                                for _, a, b in parts:
                                    last = products(nc, acc[:, u, s, a:b], (wh[u][:, c, s, :], wl[u][:, c, s, :]),
                                                    [t[:, c, a:b] for t in h], c == 0, c == KD - 1)
                        last.then_inc(acc_full[u], 1)
                with pe.Fori(0, DOWN) as it:
                    for u in range(2):
                        pe.wait_ge(down_split[u], it + (p * DOWN + 1))
                        pe.wait_ge(acc_free[u], it + (v0 + count // 2 + 1))
                        for c in range(count):
                            if u == 0:
                                pe.wait_ge(gated_ready, n0 + c + 1)
                            for _, a, b in parts:
                                last = products(nc, acc[:, u, 0, a:b], (dh[u][:, c, :], dl[u][:, c, :]),
                                                (ghi[:, c, a:b], glo[:, c, a:b]), c == 0, c == count - 1)
                        last.then_inc(acc_full[u], 1)

        @block.scalar
        def _(act):
            def hi_up(v, u):
                act.wait_ge(up_full[u], v * 32 + 32)
                nc.scalar.copy(wh[u][:], wt[u][:]).then_inc(up_hi[u], 1)

            def hi_down(count, v, u):
                act.wait_ge(down_full[u], v * 16 + 16)
                nc.scalar.copy(dh[u][:, 0:count, :], dt[u][:, 0:count, :]).then_inc(down_hi[u], 1)

            def pair(n0, v0, it, more):
                for u in range(2):
                    n = it * 2 + u
                    if u == 0 or more:
                        hi_up(it + (n0 // 2 + u), 1 - u)
                    act.wait_ge(acc_full[u], it + (v0 + 1))
                    act.wait_ge(out[u], it + (n0 // 2 + 1))
                    for s in range(2):
                        last = nc.scalar.activation(conv[:, u, s, :], acc[:, u, s, 0:tok], ACT.Identity,
                                                    bias=K.vecs[:, at(n + (b0 + n0 + s * NF))],
                                                    scale=K.vecs[:, at(n + (tap0 + n0 + 2 * NF + s * NF))])
                    last.then_inc(mid[u], 1)
                    act.wait_ge(tapped[u], it + (n0 // 2 + 1))
                    nc.scalar.activation(conv[:, u, 1, :], conv[:, u, 1, :], ACT.Silu).then_inc(silu[u], 1)

            first.squares(act)
            for p, n0, count, v0 in pieces:
                hi_up(n0 // 2, 0)
                if p == 0:
                    first.scalar(act)
                with act.Fori(0, count // 2 - 1) as it:
                    pair(n0, v0, it, True)
                for u in range(2):
                    hi_down(count, p * DOWN, u)
                pair(n0, v0, count // 2 - 1, False)
                with act.Fori(0, DOWN - 1) as it:
                    for u in range(2):
                        hi_down(count, it + (p * DOWN + 1), u)

        @block.vector
        def _(dve):
            for u in range(2):
                dve.sem_inc(acc_free[u], 1)
                dve.sem_inc(out[u], 1)
            first.gains(dve)
            first.vector(dve, sums)
            for p, n0, count, v0 in pieces:
                with dve.Fori(0, count // 2) as it:
                    for u in range(2):
                        n = it * 2 + u
                        dve.wait_ge(mid[u], it + (n0 // 2 + 1))
                        for s in range(2):
                            for _, a, b in parts:
                                nc.vector.scalar_tensor_tensor(
                                    conv[:, u, s, a + 1:b], acc[:, u, s, a:b - 1], K.vecs[:, at(n + (tap0 + n0 + s * NF))],
                                    conv[:, u, s, a + 1:b], ALU.mult, ALU.add)
                        dve.drain()
                        for s in range(2):
                            for _, a, b in parts:
                                last = nc.vector.scalar_tensor_tensor(
                                    conv[:, u, s, a:b - 1], acc[:, u, s, a + 1:b],
                                    K.vecs[:, at(n + (tap0 + n0 + 4 * NF + s * NF))],
                                    conv[:, u, s, a:b - 1], ALU.mult, ALU.add)
                        last.then_inc(tapped[u], 1)
                        dve.drain()
                        dve.sem_inc(acc_free[u], 1)
                        dve.wait_ge(silu[u], it + (n0 // 2 + 1))
                        nc.vector.tensor_tensor(gated[:, at(n), 0:tok], conv[:, u, 0:1, :], conv[:, u, 1:2, :],
                                                ALU.mult).then_inc(out[u], 1)
                        dve.wait_ge(out[u], it + (n0 // 2 + 2))
                        nc.vector.tensor_copy(ghi[:, at(n), 0:tok], gated[:, at(n), 0:tok])
                        dve.drain()
                        lo_of(nc.vector, glo[:, at(n), 0:tok], gated[:, at(n), 0:tok], ghi[:, at(n), 0:tok]).then_inc(gated_ready, 1)
                with dve.Fori(0, DOWN) as it:
                    for u in range(2):
                        n = it * 2 + u
                        dve.wait_ge(acc_full[u], it + (v0 + count // 2 + 1))
                        for s, a, b in parts:
                            last = nc.vector.scalar_tensor_tensor(
                                K.x[:, at(n), a:b], acc[:, u, 0:1, a:b], K.mod[:, s, at(n + gate_at)],
                                K.x[:, at(n), a:b], ALU.mult, ALU.add)
                        last.then_inc(acc_free[u], 1)
                dve.drain()


def head_norm(K, src, chunks, tok, dst, a, eps, gain):
    nc = K.nc
    parts = ((0, TX), (TX, TT)) if tok == TT else ((0, tok),)
    pick, ident = K.const("pick"), K.const("ident")
    with ExitStack() as ctx:
        sq = K.sb(ctx, "hn_sq", [P, 2, tok])
        rstd = K.sb(ctx, "hn_rstd", [chunks, tok])
        ss = K.ps(ctx, "hn_ss", [P, 1024])
        spread = K.ps(ctx, "hn_spread", [P, 2, 1024])
        sq_full, summed, inv, root, spread_full, done = (
            K.sem("hn_" + n) for n in ("sq", "summed", "inv", "root", "spread", "done"))
        block = ctx.enter_context(K.block())

        @block.scalar
        def _(act):
            for n in range(chunks):
                if n >= 2:
                    act.wait_ge(summed, n - 1)
                nc.scalar.activation(sq[:, n % 2, :], src[:, n, 0:tok], ACT.Square).then_inc(sq_full, 1)
            act.wait_ge(inv, 1)
            nc.scalar.activation(rstd[:], rstd[:], ACT.Sqrt).then_inc(root, 1)

        @block.tensor
        def _(pe):
            for n in range(chunks):
                pe.wait_ge(sq_full, n + 1)
                for p, q in parts:
                    last = nc.tensor.matmul(ss[0:chunks, p:q], pick[:, KD - 1 - n:KD - 1 - n + chunks], sq[:, n % 2, p:q],
                                            start=(n == 0), stop=(n == chunks - 1))
                last.then_inc(summed, 1)
            pe.wait_ge(root, 1)
            for n in range(chunks):
                if n >= 2:
                    pe.wait_ge(done, n - 1)
                for p, q in parts:
                    last = nc.tensor.matmul(spread[:, n % 2, p:q], ident[0:chunks, n:n + 1].broadcast_to([chunks, P]), rstd[:, p:q],
                                            start=True, stop=True)
                last.then_inc(spread_full, 1)

        @block.vector
        def _(dve):
            dve.wait_ge(summed, chunks)
            nc.vector.tensor_scalar(rstd[:], ss[0:chunks, 0:tok], a, eps, ALU.mult, ALU.add)
            dve.drain()
            nc.vector.reciprocal(rstd[:], rstd[:]).then_inc(inv, 1)
            for n in range(chunks):
                dve.wait_ge(spread_full, n + 1)
                nc.vector.scalar_tensor_tensor(dst[:, n, 0:tok], src[:, n, 0:tok], gain, spread[:, n % 2, 0:tok],
                                               ALU.mult, ALU.mult).then_inc(done, 1)
            dve.drain()


def attention(K, q, k, v, o, diff, bias_rows):
    nc = K.nc
    scale = HD ** -0.5
    NQ = NT if diff else NTX
    NA = 1 if diff else 2
    TQ = NQ * P
    ident = K.const("ident")
    with ExitStack() as ctx:
        qs = [K.sb(ctx, f"att_q{u}", [P, 1, TQ]) for u in range(2)]
        ks = [K.sb(ctx, f"att_k{u}", [P, 1, TT]) for u in range(2)]
        vs = [K.sb(ctx, f"att_v{u}", [P, NT, P]) for u in range(2)]
        prob = K.sb(ctx, "prob", [P, 2, 2, TT])
        pT = K.sb(ctx, "pT", [P, NA, NT, TX])
        if diff:
            pTc = K.sb(ctx, "pTc", [P, NTC, TC])
        mx = K.sb(ctx, "mx", [P, 2, 2, 2])
        nm = K.sb(ctx, "nm", [P, 2, 2])
        rs = K.sb(ctx, "rs", [P, 2, 2, 2])
        rr = K.sb(ctx, "rr", [P, 2, 2])
        lam = K.sb(ctx, "lam", [P, 1])
        S = K.ps(ctx, "scores", [P, 2, 3 * 512])
        tp = K.ps(ctx, "turned", [P, 2 * 512])
        if not diff:
            sb_ = K.sb(ctx, "biased", [P, 2, 2, TX])
            bias = [K.sb(ctx, f"bias{u}", [P, 2, NSLOT, GRID_W]) for u in range(2)]
            bias_full = [K.sem("bias_full") for _ in range(2)]
        staged = [K.sem("att_staged") for _ in range(2)]
        first_half = K.sem("att_first_half")
        s_ready, m_ready, e_done, a_ready, t_ready, t_out, pv, lam_ready = (
            K.sem("att_" + n) for n in ("scores", "max", "exp", "probs", "turned", "turned_out", "pv", "lam"))
        block = ctx.enter_context(K.block())

        @block.gpsimd
        def _(pool):
            with pool.Fori(0, 4) as it:
                for u in range(2):
                    hh = it * 2 + u
                    pool.wait_ge(pv, hh + 1)
                    nc.gpsimd.tensor_copy(qs[u][:], q[:, at(hh), :])
                    nc.gpsimd.tensor_copy(ks[u][:], k[:, at(hh), :])
                    nc.gpsimd.tensor_copy(vs[u][:], v[:, :, at(hh * P, P)])
                    pool.drain()
                    pool.sem_inc(staged[u], 1)

        if not diff:
            @block.sync
            def _(sp):
                with sp.Fori(0, 4) as it:
                    for u in range(2):
                        hh = it * 2 + u
                        sp.wait_ge(m_ready, hh * NQ + NQ)
                        for j in range(2):
                            head = (hh * 2 + j)
                            sp.dma_start(bias[u][0:64, j], bias_rows[at(head), :, 1:1 + NSLOT, :].rearrange(
                                "h c s k -> c (h s) k")).then_inc(bias_full[u], 16)
                            sp.dma_start(bias[u][64:128, j], bias_rows[at(head), :, 0:NSLOT, :].rearrange(
                                "h c s k -> c (h s) k")).then_inc(bias_full[u], 16)

        @block.tensor
        def _(pe):
            pe.sem_inc(pv, 2)
            pe.sem_inc(t_ready, 2 * NA)

            def scores(u, g, qt):
                b = qt % 2
                pe.wait_ge(e_done, g + 1)
                for j in range(2):
                    half = slice(64 * j, 64 * j + 64)
                    q_tile = qs[u][half, 0, qt * P:(qt + 1) * P]
                    image = S[:, b, j * TX:(j + 1) * TX]
                    context = S[:, b, 2 * TX + j * TC:2 * TX + (j + 1) * TC]
                    if j == 1 and qt < NTX:
                        nc.tensor.matmul(image, q_tile, ks[u][half, 0, 0:TX], start=True, stop=True)
                    if j == 1:
                        pe.wait_ge(first_half, g + 1)
                    nc.tensor.matmul(context, q_tile, ks[u][half, 0, TX:TT], start=True, stop=True).then_inc(
                        s_ready if j else first_half, 1)
                    if j == 0 and qt < NTX:
                        nc.tensor.matmul(image, q_tile, ks[u][half, 0, 0:TX], start=True, stop=True)

            def turn(hh, qt):
                b = qt % 2
                g = hh * NQ + qt
                pe.wait_ge(a_ready, g + 1)
                for j in range(NA):
                    pe.wait_ge(t_out, hh * (NQ * NA + 1) + (qt * NA + j + 1))
                    for kt in range(NT):
                        if qt < NTX or kt >= NTX:
                            last = nc.tensor.transpose(tp[:, kt * P:(kt + 1) * P], prob[:, b, j, kt * P:(kt + 1) * P], ident)
                    last.then_inc(t_ready, 1)

            def ahead(it, u, qt, more):
                if qt < NQ:
                    scores(u, (it * 2 + u) * NQ + qt, qt)
                elif u == 0 or more:
                    if qt == NQ:
                        pe.wait_ge(staged[1 - u], it + u + 1)
                    scores(1 - u, (it * 2 + u + 1) * NQ + qt - NQ, qt - NQ)

            def pairs(it, more):
                for u in range(2):
                    hh = it * 2 + u
                    for qt in range(NQ):
                        ahead(it, u, qt + 2, more)
                        turn(hh, qt)
                    pe.wait_ge(t_out, hh * (NQ * NA + 1) + (NQ * NA + 1))
                    for j in range(NA):
                        rows = slice(0, P) if diff else slice(64 * j, 64 * j + 64)
                        for kt in range(NT):
                            last = nc.tensor.matmul(tp[rows, 0:TX], vs[u][:, kt, rows], pT[:, j, kt, :],
                                                    start=(kt == 0), stop=(kt == NT - 1))
                    if diff:
                        for kt in range(NTC):
                            last = nc.tensor.matmul(tp[:, TX:TT], vs[u][:, NTX + kt, :], pTc[:, kt, :],
                                                    start=(kt == 0), stop=(kt == NTC - 1))
                    last.then_inc(pv, 1)

            pe.wait_ge(staged[0], 1)
            for qt in range(2):
                scores(0, qt, qt)
            with pe.Fori(0, 3) as it:
                pairs(it, True)
            pairs(3, False)

        @block.vector
        def _(dve):
            dve.sem_inc(m_ready, 2 * NQ)
            if diff:
                lv = K.row("lam").rearrange("p (a b d) -> p a b d", a=2, b=2)
                prod = prob[:, 0, 0, 0:2 * HD].rearrange("p (a d) -> p a d", a=2)
                nc.vector.tensor_tensor(prod, lv[:, :, 0], lv[:, :, 1], ALU.mult)
                dve.drain()
                nc.vector.tensor_reduce(mx[:, 0, 0, :], prod, AX_X, ALU.add)
                dve.drain()
                dve.sem_inc(lam_ready, 1)
                dve.wait_ge(lam_ready, 2)
                nc.vector.scalar_tensor_tensor(lam[:], nm[:, 0, 0:1], LAM_INIT, nm[:, 0, 1:2], ALU.add, ALU.subtract)
                dve.drain()
                dve.sem_inc(lam_ready, 1)

            def maxima(u, g, qt):
                b = qt % 2
                dve.wait_ge(s_ready, g + 1)
                if diff:
                    if qt < NTX:
                        nc.vector.tensor_reduce(mx[:, b, 0, :], S[:, b, 0:2 * TX].rearrange("p (j k) -> p j k", j=2),
                                                AX_X, ALU.max)
                else:
                    at_row = KH - 1 - 2 * qt
                    for j in range(2):
                        nc.vector.scalar_tensor_tensor(
                            sb_[:, b, j, :], S[:, b, j * TX:(j + 1) * TX], scale,
                            bias[u][:, j, at_row - 1:at_row - 1 + GRID_H, :].rearrange("p s k -> p (s k)"),
                            ALU.mult, ALU.add)
                    dve.drain()
                    nc.vector.tensor_reduce(mx[:, b, 0, :], sb_[:, b], AX_X, ALU.max)
                nc.vector.tensor_reduce(mx[:, b, 1, :], S[:, b, 2 * TX:3 * TX].rearrange("p (j k) -> p j k", j=2),
                                        AX_X, ALU.max)
                dve.drain()
                if qt >= NTX:
                    nc.vector.tensor_scalar(nm[:, b, :], mx[:, b, 1, :], -scale, None, ALU.mult).then_inc(m_ready, 1)
                    return
                if diff:
                    nc.vector.tensor_tensor(mx[:, b, 0, :], mx[:, b, 0, :], mx[:, b, 1, :], ALU.max)
                    dve.drain()
                    nc.vector.tensor_scalar(nm[:, b, :], mx[:, b, 0, :], -scale, None, ALU.mult).then_inc(m_ready, 1)
                else:
                    nc.vector.scalar_tensor_tensor(mx[:, b, 0, :], mx[:, b, 1, :], scale, mx[:, b, 0, :],
                                                   ALU.mult, ALU.max)
                    dve.drain()
                    nc.vector.tensor_scalar(nm[:, b, :], mx[:, b, 0, :], -1.0, None, ALU.mult).then_inc(m_ready, 1)

            def weigh(g, qt):
                b = qt % 2
                lo = 0 if qt < NTX else TX
                dve.wait_ge(e_done, g + 3)
                if qt < NTX:
                    nc.vector.tensor_tensor(rr[:, b, :], rs[:, b, 0, :], rs[:, b, 1, :], ALU.add)
                    dve.drain()
                    nc.vector.reciprocal(rr[:, b, :], rr[:, b, :])
                else:
                    nc.vector.reciprocal(rr[:, b, :], rs[:, b, 1, :])
                dve.drain()
                if diff:
                    nc.vector.tensor_scalar(prob[:, b, 1, lo:], prob[:, b, 1, lo:], rr[:, b, 1:2], lam[:], ALU.mult, ALU.mult)
                    dve.drain()
                    nc.vector.scalar_tensor_tensor(prob[:, b, 0, lo:], prob[:, b, 0, lo:], rr[:, b, 0:1],
                                                   prob[:, b, 1, lo:], ALU.mult, ALU.subtract).then_inc(a_ready, 1)
                else:
                    for j in range(2):
                        last = nc.vector.tensor_scalar(prob[:, b, j, :], prob[:, b, j, :], rr[:, b, j:j + 1], None, ALU.mult)
                    last.then_inc(a_ready, 1)

            def first_maxima(it, u):
                if not diff:
                    dve.wait_ge(bias_full[u], it * 64 + 64)
                    for j in range(2):
                        nc.vector.tensor_tensor(bias[u][:, j], bias[u][:, j], K.const("window").unsqueeze(1).broadcast_to(
                            [P, NSLOT, GRID_W]), ALU.add)
                    dve.drain()
                maxima(u, (it * 2 + u) * NQ, 0)

            def pairs(it, more):
                for u in range(2):
                    g0 = (it * 2 + u) * NQ
                    for qt in range(NQ):
                        if qt + 1 < NQ:
                            maxima(u, g0 + qt + 1, qt + 1)
                        elif u == 0 or more:
                            first_maxima(it + u, 1 - u)
                        weigh(g0 + qt, qt)

            first_maxima(0, 0)
            with dve.Fori(0, 3) as it:
                pairs(it, True)
            pairs(3, False)

        @block.scalar
        def _(act):
            act.sem_inc(e_done, 2)
            act.sem_inc(t_out, 1)
            if diff:
                act.wait_ge(lam_ready, 1)
                nc.scalar.activation(nm[:, 0, :], mx[:, 0, 0, :], ACT.Exp)
                act.drain()
                act.sem_inc(lam_ready, 1)
                act.wait_ge(lam_ready, 3)

            def exps(g, qt):
                b = qt % 2
                act.wait_ge(m_ready, g + 1 + 2 * NQ)
                act.wait_ge(t_ready, g * NA + NA)
                for j in range(2):
                    if qt < NTX:
                        src = S[:, b, j * TX:(j + 1) * TX] if diff else sb_[:, b, j, :]
                        nc.scalar.activation(prob[:, b, j, 0:TX], src, ACT.Exp, bias=nm[:, b, j:j + 1],
                                             scale=scale if diff else 1.0, accum_out=rs[:, b, 0, j:j + 1])
                    nc.scalar.activation(prob[:, b, j, TX:TT], S[:, b, 2 * TX + j * TC:2 * TX + (j + 1) * TC], ACT.Exp,
                                         bias=nm[:, b, j:j + 1], scale=scale, accum_out=rs[:, b, 1, j:j + 1])
                act.drain()
                act.sem_inc(e_done, 1)

            def take(hh, g, qt):
                for j in range(NA):
                    act.wait_ge(t_ready, g * NA + j + 1 + 2 * NA)
                    if qt == 0 and j == 0:
                        act.wait_ge(pv, hh + 2)
                    if qt < NTX:
                        last = nc.scalar.copy(pT[:, j, :, qt * P:(qt + 1) * P],
                                              tp[:, 0:TT].rearrange("p (k q) -> p k q", k=NT))
                    else:
                        last = nc.scalar.copy(pTc[:, :, (qt - NTX) * P:(qt - NTX + 1) * P],
                                              tp[:, TX:TT].rearrange("p (k q) -> p k q", k=NTC))
                    last.then_inc(t_out, 1)

            def pairs(it, more):
                for u in range(2):
                    hh = it * 2 + u
                    g0 = hh * NQ
                    for qt in range(NQ):
                        if qt + 1 < NQ or u == 0 or more:
                            exps(g0 + qt + 1, (qt + 1) % NQ)
                        take(hh, g0 + qt, qt)
                    act.wait_ge(pv, hh + 3)
                    nc.scalar.copy(o[:, at(hh), 0:TQ], tp[:, 0:TQ].unsqueeze(1)).then_inc(t_out, 1)

            exps(0, 0)
            with act.Fori(0, 3) as it:
                pairs(it, True)
            pairs(3, False)


def first_block(K, io):
    nc = K.nc
    for i in range(2):
        kind = "a" if i == 0 else "b"
        tok = TT if i == 0 else TX
        ada(K, io["ada_w"][i], f"ada_b{i}", 0, (K.x[:], io["xT"]) if i == 0 else None)
        with ExitStack() as ctx:
            q = K.sb(ctx, "q", [P, KD, tok])
            k = K.sb(ctx, "k", [P, KD, TT])
            v = K.sb(ctx, "v", [P, NT, D])
            w = io[kind + "_wqkv"][0]
            with ExitStack() as proj:
                h = Normed(K, proj, f"norm_mix{i}", 8, 0, True)
                features(K, h.parts, w, 0, KD, tok, lambda n, sums: nc.scalar.copy(q[:, at(n), :], sums), first=h)
                features(K, h.parts, w, D, KD, TT, lambda n, sums: nc.scalar.copy(k[:, at(n), :], sums))
                token_rows(K, h.parts, w, 2 * D, D, NT, v)
            o = K.sb(ctx, "o", [P, KD, TT])
            if i == 0:
                rope(K, q, KD)
                rope(K, k, KD)
            attention(K, q, k, v, o, i == 0, io["bias_rows"])
            if i == 0:
                head_norm(K, o, KD, tok, o, 1.0 / P, EPS, K.subln[:])
            residual(K, o, io[kind + "_wo"][0], 16, tok)
        with ExitStack() as ctx:
            h = Normed(K, ctx, f"norm_ffn{i}", 32, 24, i == 0)
            ffn(K, h, io["ffn_up"][i], io["ffn_down"][i], ((8, 8, 6), (12, 10))[i],
                f"conv{i}", f"conv_b{i}", 40, tok)
    norm(K, K.x, K.x, "norm_out", 0, 0, mod=False)


def dn_inputs(K, first, w, dst):
    nc = K.nc
    wv = w.rearrange("(c p) n -> p c n", p=P)
    parts = ((0, TX), (TX, TT))
    tap0 = VECS["dn_conv"][0]
    n_chunks = DNQKV // P
    h = first.parts
    with ExitStack() as ctx:
        wt = [K.sb(ctx, f"dni_w{u}", [P, KD, P]) for u in range(2)]
        wh = [K.sb(ctx, f"dni_w_hi{u}", [P, KD, P], FR) for u in range(2)]
        wl = [K.lo(t) for t in wt]
        conv = K.sb(ctx, "dni_conv", [P, 2, TT])
        acc = K.ps(ctx, "dni_acc", [P, 2, 1024])
        sums = K.ps(ctx, "dni_norm", [P, 1024])
        w_full = [K.sem("dni_w_full") for _ in range(2)]
        acc_full = [K.sem("dni_acc_full") for _ in range(2)]
        mid = [K.sem("dni_mid") for _ in range(2)]
        acc_free = [K.sem("dni_acc_free") for _ in range(2)]
        out = [K.sem("dni_out") for _ in range(2)]
        w_hi, w_split = ([K.sem("dni_" + n) for _ in range(2)] for n in ("w_hi", "w_split"))
        block = ctx.enter_context(K.block())

        @block.sync
        def _(sp):
            with sp.Fori(0, n_chunks // 2) as it:
                for u in range(2):
                    sp.wait_ge(acc_full[u], it + 1)
                    sp.dma_start(wt[u][:], wv[:, :, at((it * 2 + u) * P, P)]).then_inc(w_full[u], 16)

        @block.gpsimd
        def _(pool):
            with pool.Fori(0, n_chunks // 2) as it:
                for u in range(2):
                    pool.wait_ge(w_hi[u], it + 1)
                    lo_of(nc.gpsimd, wl[u][:], wt[u][:], wh[u][:]).then_inc(w_split[u], 1)

        @block.tensor
        def _(pe):
            for u in range(2):
                pe.sem_inc(acc_full[u], 1)
            first.tensor(pe, sums)
            with pe.Fori(0, n_chunks // 2) as it:
                for u in range(2):
                    pe.wait_ge(w_split[u], it + 1)
                    pe.wait_ge(acc_free[u], it + 1)
                    for c in range(KD):
                        if u == 0:
                            pe.wait_ge(first.ready, c + 1)
                        for a, b in parts:
                            last = products(nc, acc[:, u, a:b], (wh[u][:, c, :], wl[u][:, c, :]),
                                            [t[:, c, a:b] for t in h], c == 0, c == KD - 1)
                    last.then_inc(acc_full[u], 1)

        @block.scalar
        def _(act):
            for u in range(2):
                act.sem_inc(out[u], 1)

            def hi_weights(it, u):
                act.wait_ge(w_full[u], it * 16 + 16)
                nc.scalar.copy(wh[u][:], wt[u][:]).then_inc(w_hi[u], 1)

            def pair(it, more):
                for u in range(2):
                    n = it * 2 + u
                    if u == 0 or more:
                        hi_weights(it + u, 1 - u)
                    act.wait_ge(acc_full[u], it + 2)
                    act.wait_ge(out[u], it + 1)
                    nc.scalar.activation(conv[:, u, :], acc[:, u, 0:TT], ACT.Identity,
                                         scale=K.vecs[:, at(n + (tap0 + n_chunks))]).then_inc(mid[u], 1)
                    act.wait_ge(acc_free[u], it + 2)
                    nc.scalar.activation(dst[:, at(n), :], conv[:, u:u + 1, :], ACT.Silu).then_inc(out[u], 1)

            first.squares(act)
            hi_weights(0, 0)
            first.scalar(act)
            with act.Fori(0, n_chunks // 2 - 1) as it:
                pair(it, True)
            pair(n_chunks // 2 - 1, False)

        @block.vector
        def _(dve):
            for u in range(2):
                dve.sem_inc(acc_free[u], 1)
            first.gains(dve)
            first.vector(dve, sums)
            with dve.Fori(0, n_chunks // 2) as it:
                for u in range(2):
                    n = it * 2 + u
                    dve.wait_ge(mid[u], it + 1)
                    for a, b in parts:
                        nc.vector.scalar_tensor_tensor(conv[:, u, a + 1:b], acc[:, u, a:b - 1], K.vecs[:, at(n + tap0)],
                                                       conv[:, u, a + 1:b], ALU.mult, ALU.add)
                    dve.drain()
                    for a, b in parts:
                        last = nc.vector.scalar_tensor_tensor(
                            conv[:, u, a:b - 1], acc[:, u, a + 1:b], K.vecs[:, at(n + (tap0 + 2 * n_chunks))],
                            conv[:, u, a:b - 1], ALU.mult, ALU.add)
                    last.then_inc(acc_free[u], 1)


def dn_gates(K, h, w, beta, g):
    nc = K.nc
    with ExitStack() as ctx:
        wt = K.sb(ctx, "ba_w", [P, KD, 16])
        wh = K.sb(ctx, "ba_w_hi", [P, KD, 16], FR)
        wl = K.lo(wt)
        y, e, l = (K.sb(ctx, "ba_" + n, [P, NT, 8]) for n in "yel")
        rate = K.sb(ctx, "rate", [P, 8])
        acc = K.ps(ctx, "ba_acc", [P, NT, 16])
        w_full, w_split, summed, biased, exped, done = (
            K.sem("ba_" + n) for n in ("w", "split", "summed", "biased", "exped", "done"))
        block = ctx.enter_context(K.block())

        @block.sync
        def _(sp):
            sp.dma_start(wt[:], w[:, C_BA:C_BA + 16].rearrange("(c p) n -> p c n", p=P)).then_inc(w_full, 16)

        @block.tensor
        def _(pe):
            pe.wait_ge(w_split, 1)
            for t in range(NT):
                for c in range(KD):
                    last = products(nc, acc[:, t, :], [a[:, c, t * P:(t + 1) * P] for a in h], (wh[:, c, :], wl[:, c, :]),
                                    c == 0, c == KD - 1)
            last.then_inc(summed, 1)

        @block.vector
        def _(dve):
            dve.wait_ge(w_full, 16)
            nc.vector.tensor_copy(wh[:], wt[:])
            dve.drain()
            lo_of(nc.vector, wl[:], wt[:], wh[:]).then_inc(w_split, 1)
            dve.wait_ge(summed, 1)
            nc.vector.tensor_copy(beta[:], acc[:, :, 0:8])
            nc.vector.tensor_tensor(y[:], acc[:, :, 8:16], K.row("dt_bias").unsqueeze(1).broadcast_to([P, NT, 8]), ALU.add)
            dve.drain()
            nc.vector.scalar_tensor_tensor(e[:], y[:], -1.0, y[:], ALU.mult, ALU.min).then_inc(biased, 1)
            dve.wait_ge(exped, 1)
            nc.vector.scalar_tensor_tensor(l[:], y[:], 0.0, l[:], ALU.max, ALU.add)
            dve.drain()
            nc.vector.scalar_tensor_tensor(g[:], l[:], -1.0, rate[:].unsqueeze(1).broadcast_to([P, NT, 8]),
                                           ALU.mult, ALU.mult)
            dve.drain()

        @block.scalar
        def _(act):
            act.wait_ge(biased, 1)
            nc.scalar.activation(e[:], e[:], ACT.Exp)
            nc.scalar.activation(rate[:], K.row("a_log"), ACT.Exp)
            act.drain()
            nc.scalar.activation(l[:], e[:], ACT.Ln, bias=1.0)
            act.drain()
            act.sem_inc(exped, 1)
            nc.scalar.activation(beta[:], beta[:], ACT.Sigmoid).then_inc(done, 1)
            act.wait_ge(done, 1)


def steps_of(d):
    c = list(range(NTX, NT)) + list(range(NTX)) if d == 0 else list(range(NT - 1, NTX - 1, -1)) + list(range(NTX - 1, -1, -1))
    return c


def last_of(d):
    return P - 1 if d == 0 else 0


def deltanet(K, qkv, beta, g, o):
    nc = K.nc
    NS = 2 * NT
    UNITS = LEVELS * 3
    ident = K.const("ident")
    incl = K.const("incl").rearrange("p (d i) -> p d i", d=2)
    level = K.const("level").rearrange("p (d n i) -> p d n i", d=2, n=LEVELS)

    def last_column(t, d):
        return t[:, d * NT:(d + 1) * NT, last_of(d)]

    with ExitStack() as ctx:
        qs = K.sb(ctx, "dn_q", [P, NTX, P])
        ks, vs, kt, vt = (K.sb(ctx, "dn_" + n, [P, NT, P]) for n in ("k", "v", "kt", "vt"))
        gh, bh, gcol, ecol, edl, bk = (K.sb(ctx, "dn_" + n, [P, NS]) for n in ("gh", "bh", "gcol", "ecol", "edl", "bk"))
        gx, bx, dt, egc, AT, T, U, Pm, Kb = (
            K.sb(ctx, "dn_" + n, [P, NS, P]) for n in ("gx", "bx", "dt", "egc", "AT", "T", "U", "Pm", "Kb"))
        Vb, Kd, wT = gx, bx, Pm
        AL = K.sb(ctx, "dn_AL", [P, 2, NS, P])
        qe, att = (K.sb(ctx, "dn_" + n, [P, 2, NTX, P]) for n in ("qe", "att"))
        S = K.sb(ctx, "dn_S", [P, 2, 2, P])
        vn = K.sb(ctx, "dn_vn", [P, 2, 2, P])
        B = K.ps(ctx, "dn_banks", [P, 8, 512])
        three = B[:, 0:3, :].rearrange("p b n -> p (b n)").rearrange("p (s i) -> p s i", s=NS)
        gram = B[:, 4:6, :].rearrange("p b n -> p (b n)")[:, 0:NT * P].rearrange("p (c i) -> p c i", c=NT)
        vturn = B[:, 6:8, :].rearrange("p b n -> p (b n)")[:, 0:NT * P].rearrange("p (c i) -> p c i", c=NT)
        qk = B[:, 6, :].rearrange("p (c i) -> p c i", c=NTX)
        staged, gc_ready, dt_ready, exps, tm_ready, tm_out, gram_ready, beta_ready, a_built = (
            K.sem("dn_" + n) for n in ("staged", "gc", "dt", "exps", "turned", "turned_out", "gram", "beta", "a_built"))
        al_ready, p_ready, p_out, xy_ready, t_done, kv_ready, w_ready, w_out, head_done = (
            K.sem("dn_" + n) for n in ("al", "p", "p_out", "xy", "t_done", "kv", "w", "w_out", "head_done"))
        vn_ready, vn_out, ds_ready, s_done, o_ready, o_out = (
            [K.sem(f"dn_{n}{d}") for d in range(2)] for n in ("vn", "vn_out", "ds", "s_done", "o", "o_out"))
        block = ctx.enter_context(K.block())

        @block.gpsimd
        def _(pool):
            with pool.Fori(0, HEADS) as it:
                pool.wait_ge(head_done, it + 1)
                for d in range(2):
                    nc.gpsimd.tensor_copy(gh[:, d * NT:(d + 1) * NT].unsqueeze(2), g[:, :, at(it + d * HEADS)])
                    nc.gpsimd.tensor_copy(bh[:, d * NT:(d + 1) * NT].unsqueeze(2), beta[:, :, at(it + d * HEADS)])
                pool.drain()
                pool.sem_inc(staged, 1)
                pool.wait_ge(a_built, it + 1)
                for n in range(LEVELS):
                    for q in range(3):
                        if n >= 2:
                            pool.wait_ge(t_done, it * UNITS + (n - 2) * 3 + q + 1)
                        for lo, hi, d in ((4 * q, min(4 * q + 4, NT), 0), (max(4 * q, NT), 4 * q + 4, 1)):
                            if lo < hi:
                                nc.gpsimd.tensor_tensor(
                                    AL[:, n % 2, lo:hi, :], AT[:, lo:hi, :],
                                    level[:, d, n, :].unsqueeze(1).broadcast_to([P, hi - lo, P]), ALU.mult)
                        pool.drain()
                        pool.sem_inc(al_ready, 1)
                    if n == 1:
                        pool.wait_ge(exps, it + 1)
                        pool.wait_ge(tm_out, it + 1)
                        nc.gpsimd.tensor_tensor(bk[:], bh[:], ecol[:], ALU.mult)
                        for d in range(2):
                            own = slice(d * NT, (d + 1) * NT)
                            nc.gpsimd.tensor_tensor(Vb[:, own, :], vt[:], bh[:, own].unsqueeze(2).broadcast_to([P, NT, P]), ALU.mult)
                            nc.gpsimd.tensor_tensor(Kd[:, own, :], kt[:], edl[:, own].unsqueeze(2).broadcast_to([P, NT, P]), ALU.mult)
                            nc.gpsimd.tensor_tensor(qe[:, d], qs[:], egc[:, d * NT:d * NT + NTX, :], ALU.mult)
                        pool.drain()
                        for d in range(2):
                            own = slice(d * NT, (d + 1) * NT)
                            nc.gpsimd.tensor_tensor(Kb[:, own, :], kt[:], bk[:, own].unsqueeze(2).broadcast_to([P, NT, P]), ALU.mult)
                        pool.drain()
                        pool.sem_inc(kv_ready, 1)

        @block.tensor
        def _(pe):
            pe.sem_inc(head_done, 1)
            with pe.Fori(0, HEADS) as it:
                pe.wait_ge(staged, it * 3 + 3)
                for d in range(2):
                    pe.wait_ge(o_out[d], it * NTX + 1)
                    pe.wait_ge(vn_out[d], it * NT + 1)
                    pe.wait_ge(s_done[d], it * (NT - 1) + 1)
                for s in range(NS):
                    nc.tensor.matmul(three[:, s, :], gx[:, s, :], incl[:, s // NT, :], start=True, stop=True)
                for d in range(2):
                    last = nc.tensor.matmul(B[:, 3, d * NT:(d + 1) * NT], incl[:, d, :], gh[:, d * NT:(d + 1) * NT],
                                            start=True, stop=True)
                last.then_inc(gc_ready, 1)
                for c in range(NT):
                    nc.tensor.transpose(gram[:, c, :], ks[:, c, :], ident)
                for c in range(NT):
                    last = nc.tensor.transpose(vturn[:, c, :], vs[:, c, :], ident)
                last.then_inc(tm_ready, 1)
                pe.wait_ge(tm_out, it + 1)
                for c in range(NT):
                    nc.tensor.matmul(gram[:, c, :], ks[:, c, :], ks[:, c, :], start=True, stop=True)
                for c in range(NTX):
                    last = nc.tensor.matmul(qk[:, c, :], ks[:, c, :], qs[:, c, :], start=True, stop=True)
                last.then_inc(gram_ready, 1)
                pe.wait_ge(exps, it + 1)
                for s in range(NS):
                    last = nc.tensor.matmul(three[:, s, :], bx[:, s, :], ident, start=True, stop=True)
                last.then_inc(beta_ready, 1)
                pe.wait_ge(a_built, it + 1)

                def first_product(n):
                    lev, q = divmod(n, 3)
                    pe.wait_ge(al_ready, it * UNITS + n + 1)
                    if 2 <= n < 5:
                        pe.wait_ge(t_done, it * UNITS + n - 1)
                    elif n >= 5:
                        pe.wait_ge(t_done, it * UNITS + n - 2)
                    if n >= 5:
                        pe.wait_ge(p_out, it * (UNITS - 3) + n - 4)
                    for s in range(4 * q, 4 * q + 4):
                        rhs = ident if lev == 0 else T[:, s, :]
                        last = nc.tensor.matmul(B[:, n % 2, (s % 4) * P:(s % 4 + 1) * P], AL[:, lev % 2, s, :], rhs,
                                                start=True, stop=True)
                    last.then_inc(p_ready, 1)

                def second_products(n):
                    lev, q = divmod(n, 3)
                    if lev == 0:
                        return
                    pe.wait_ge(p_out, it * (UNITS - 3) + n - 2)
                    if n >= 5:
                        pe.wait_ge(t_done, it * UNITS + n - 1)
                    for s in range(4 * q, 4 * q + 4):
                        cols = slice((s % 4) * P, (s % 4 + 1) * P)
                        if lev < LEVELS - 1:
                            nc.tensor.matmul(B[:, 2 + n % 2, cols], U[:, s, :], Pm[:, s, :], start=True, stop=True)
                        last = nc.tensor.matmul(B[:, 4 + n % 2, cols], Pm[:, s, :], U[:, s, :], start=True, stop=True)
                    last.then_inc(xy_ready, 1)

                for n in range(UNITS + 1):
                    if n < UNITS:
                        first_product(n)
                    if n >= 1:
                        second_products(n - 1)
                pe.wait_ge(t_done, it * UNITS + UNITS)
                pe.wait_ge(kv_ready, it + 1)
                for s in range(NS):
                    last = nc.tensor.matmul(three[:, s, :], Kb[:, s, :], U[:, s, :], start=True, stop=True)
                last.then_inc(w_ready, 1)
                pe.wait_ge(w_out, it + 1)
                for st in range(NT):
                    for d in range(2):
                        c = steps_of(d)[st]
                        s = d * NT + c
                        pe.wait_ge(vn_out[d], it * NT + st + 1)
                        last = nc.tensor.matmul(B[:, 3 + d, 0:P], U[:, s, :], Vb[:, s, :], start=True, stop=(st == 0))
                        if st > 0:
                            pe.wait_ge(s_done[d], it * (NT - 1) + st + 1)
                            last = nc.tensor.matmul(B[:, 3 + d, 0:P], wT[:, s, :], S[:, d, st % 2, :], start=False, stop=True)
                        last.then_inc(vn_ready[d], 1)
                    for d in range(2):
                        c = steps_of(d)[st]
                        s = d * NT + c
                        pe.wait_ge(vn_out[d], it * NT + st + 2)
                        if st < NT - 1:
                            nc.tensor.matmul(B[:, 5 + d, 0:P], Kd[:, s, :], vn[:, d, st % 2, :],
                                             start=True, stop=True).then_inc(ds_ready[d], 1)
                        if c < NTX:
                            k = st - NTC
                            pe.wait_ge(o_out[d], it * NTX + k + 1)
                            nc.tensor.matmul(B[:, d, 0:P], S[:, d, st % 2, :], qe[:, d, c, :], start=True, stop=False)
                            last = nc.tensor.matmul(B[:, d, 0:P], vn[:, d, st % 2, :], att[:, d, c, :],
                                                    start=False, stop=True)
                            last.then_inc(o_ready[d], 1)
                nc.tensor.matmul(B[:, 7, 0:P], ident, ident, start=True, stop=True).then_inc(head_done, 1)

        @block.scalar
        def _(act):
            for d in range(2):
                act.sem_inc(vn_out[d], 1)
            with act.Fori(0, HEADS) as it:
                act.wait_ge(head_done, it + 1)
                nc.scalar.copy(vs[:], qkv[:, at(it + 2 * HEADS), :].rearrange("p o (c i) -> p (o c) i", i=P))
                nc.scalar.copy(qs[:], qkv[:, at(it), 0:TX].rearrange("p o (c i) -> p (o c) i", i=P))
                for d in range(2):
                    nc.scalar.copy(bx[:, d * NT:(d + 1) * NT, :], beta[:, :, at(it + d * HEADS)].broadcast_to([P, NT, P]))
                act.drain()
                act.sem_inc(staged, 1)
                act.wait_ge(tm_ready, it + 1)
                nc.scalar.copy(kt[:], gram)
                nc.scalar.copy(vt[:], vturn)
                act.drain()
                act.sem_inc(tm_out, 1)
                act.wait_ge(dt_ready, it + 1)
                nc.scalar.activation(egc[:], three, ACT.Exp)
                nc.scalar.activation(dt[:], dt[:], ACT.Exp)
                nc.scalar.activation(ecol[:], gcol[:], ACT.Exp)
                nc.scalar.activation(edl[:], edl[:], ACT.Exp)
                act.drain()
                act.sem_inc(exps, 1)
                for n in range(3, UNITS):
                    q = n % 3
                    act.wait_ge(p_ready, it * UNITS + n + 1)
                    nc.scalar.copy(Pm[:, 4 * q:4 * q + 4, :], B[:, n % 2, :].rearrange("p (s i) -> p s i", s=4)).then_inc(p_out, 1)
                act.wait_ge(w_ready, it + 1)
                nc.scalar.mul(wT[:], three, -1.0).then_inc(w_out, 1)
                for st in range(NT):
                    for d in range(2):
                        act.wait_ge(vn_ready[d], it * NT + st + 1)
                        nc.scalar.copy(vn[:, d, st % 2, :], B[:, 3 + d, 0:P]).then_inc(vn_out[d], 1)

        @block.vector
        def _(dve):
            for d in range(2):
                dve.sem_inc(s_done[d], 1)
                dve.sem_inc(o_out[d], 1)
            with dve.Fori(0, HEADS) as it:
                dve.wait_ge(head_done, it + 1)
                nc.vector.tensor_copy(ks[:], qkv[:, at(it + HEADS), :].rearrange("p o (c i) -> p (o c) i", i=P))
                for d in range(2):
                    nc.vector.tensor_copy(gx[:, d * NT:(d + 1) * NT, :], g[:, :, at(it + d * HEADS)].broadcast_to([P, NT, P]))
                dve.drain()
                dve.sem_inc(staged, 1)
                dve.wait_ge(gc_ready, it + 1)
                nc.vector.tensor_copy(gcol[:], B[:, 3, 0:NS])
                dve.drain()
                for s in range(NS):
                    nc.vector.tensor_scalar(dt[:, s, :], three[:, s, :], gcol[:, s:s + 1], 0.0, ALU.subtract, ALU.min)
                for d in range(2):
                    nc.vector.tensor_tensor(edl[:, d * NT:(d + 1) * NT], last_column(three, d), gcol[:, d * NT:(d + 1) * NT], ALU.subtract)
                dve.drain()
                dve.sem_inc(dt_ready, 1)
                dve.wait_ge(exps, it + 1)
                dve.wait_ge(gram_ready, it + 1)
                for d in range(2):
                    own = slice(d * NT, (d + 1) * NT)
                    image = slice(d * NT, d * NT + NTX)
                    nc.vector.tensor_tensor(AT[:, own, :], dt[:, own, :], gram, ALU.mult)
                    nc.vector.tensor_tensor(att[:, d], dt[:, image, :], qk, ALU.mult)
                dve.drain()
                for d in range(2):
                    nc.vector.tensor_tensor(att[:, d], att[:, d], incl[:, d, :].unsqueeze(1).broadcast_to([P, NTX, P]), ALU.mult)
                dve.wait_ge(beta_ready, it + 1)
                nc.vector.tensor_tensor(AT[:], AT[:], three, ALU.mult)
                dve.drain()
                dve.sem_inc(a_built, 1)
                for n in range(UNITS):
                    lev, q = divmod(n, 3)
                    own = slice(4 * q, 4 * q + 4)
                    four = lambda b: B[:, b, :].rearrange("p (s i) -> p s i", s=4)
                    wide = ident.unsqueeze(1).broadcast_to([P, 4, P])
                    if lev == 0:
                        dve.wait_ge(p_ready, it * UNITS + n + 1)
                        nc.vector.tensor_tensor(T[:, own, :], wide, four(n % 2), ALU.subtract)
                        nc.vector.tensor_tensor(U[:, own, :], wide, AL[:, 0, own, :], ALU.subtract)
                    else:
                        dve.wait_ge(xy_ready, it * (UNITS - 3) + n - 2)
                        if lev < LEVELS - 1:
                            nc.vector.tensor_tensor(T[:, own, :], T[:, own, :], four(2 + n % 2), ALU.subtract)
                        nc.vector.tensor_tensor(U[:, own, :], U[:, own, :], four(4 + n % 2), ALU.subtract)
                    dve.drain()
                    dve.sem_inc(t_done, 1)
                for st in range(NT):
                    if st == NTC + NTX // 2:
                        dve.drain()
                    for d in range(2):
                        c = steps_of(d)[st]
                        s = d * NT + c
                        if st < NT - 1:
                            dve.wait_ge(ds_ready[d], it * (NT - 1) + st + 1)
                            if st == 0:
                                nc.vector.tensor_copy(S[:, d, 1, :], B[:, 5 + d, 0:P]).then_inc(s_done[d], 1)
                            else:
                                nc.vector.scalar_tensor_tensor(
                                    S[:, d, 1 - st % 2, :], S[:, d, st % 2, :], egc[:, s, last_of(d):last_of(d) + 1],
                                    B[:, 5 + d, 0:P], ALU.mult, ALU.add).then_inc(s_done[d], 1)
                        if c < NTX:
                            k = st - NTC
                            dve.wait_ge(o_ready[d], it * NTX + k + 1)
                            part = o[:, at(it), c * P:(c + 1) * P]
                            if st < NTC + NTX // 2:
                                nc.vector.tensor_copy(part, B[:, d:d + 1, 0:P]).then_inc(o_out[d], 1)
                            else:
                                nc.vector.tensor_tensor(part, part, B[:, d:d + 1, 0:P], ALU.add).then_inc(o_out[d], 1)


def hg_gates(K, z, k):
    nc = K.nc
    W = 2 * HEADS * P
    both = lambda t: t[:].unsqueeze(1).broadcast_to([P, 2, HEADS * P])
    halves = lambda t: t.rearrange("p (d n) -> p d n", d=2)
    unit = float(2.0 ** LN_SHIFT)
    with ExitStack() as ctx:
        lb, oml = K.sb(ctx, "lb", [P, HEADS * P]), K.sb(ctx, "oml", [P, HEADS * P])
        low = K.sb(ctx, "low", [P, NT, W])
        zeroed, ones, bound, sig, shifted, logs = (K.sem("hgg_" + n) for n in ("zeroed", "ones", "bound", "sig", "shifted", "logs"))
        block = ctx.enter_context(K.block())

        @block.scalar
        def _(act):
            act.wait_ge(zeroed, 1)
            nc.scalar.activation(lb[:], lb[:], ACT.Exp).then_inc(ones, 1)
            for t in range(NT):
                nc.scalar.activation(k[:, t, :], z[:, t, 0:W], ACT.Sigmoid, scale=-1.0)
                act.drain()
                nc.scalar.activation(z[:, t, 0:W], z[:, t, 0:W], ACT.Sigmoid)
                act.drain()
                act.sem_inc(sig, 1)
            for t in range(NT):
                act.wait_ge(shifted, t + 1)
                nc.scalar.activation(z[:, t, 0:W], z[:, t, 0:W], ACT.Ln).then_inc(logs, 1)

        @block.vector
        def _(dve):
            nc.vector.tensor_tensor(lb[:], K.row("lb"), K.row("lb"), ALU.subtract).then_inc(zeroed, 1)
            dve.wait_ge(ones, 1)
            nc.vector.reciprocal(oml[:], lb[:])
            dve.drain()
            nc.vector.tensor_tensor(lb[:], lb[:], oml[:], ALU.mult)
            dve.drain()
            nc.vector.tensor_tensor(lb[:], lb[:], lb[:], ALU.subtract)
            dve.drain()
            nc.vector.tensor_scalar(oml[:], lb[:], -1.0, 1.0, ALU.mult, ALU.add)
            dve.drain()
            dve.sem_inc(bound, 1)
            for t in range(NT):
                f = z[:, t, 0:W]
                dve.wait_ge(sig, t + 1)
                nc.vector.tensor_tensor(halves(f), halves(f), both(oml), ALU.mult)
                dve.drain()
                nc.vector.tensor_tensor(halves(f), halves(f), both(lb), ALU.add)
                dve.drain()
                nc.vector.tensor_scalar(f, f, F_TINY, None, ALU.max)
                dve.drain()
                nc.vector.tensor_scalar(low[:, t, :], f, 2.0 ** -40, unit, ALU.is_lt, ALU.mult)
                dve.drain()
                nc.vector.scalar_tensor_tensor(f, low[:, t, :], 1.0, f, ALU.add, ALU.mult).then_inc(shifted, 1)
            for t in range(NT):
                dve.wait_ge(logs, t + 1)
                nc.vector.scalar_tensor_tensor(z[:, t, 0:W], low[:, t, :], -LN_SHIFT * float(np.log(2.0)) / unit,
                                               z[:, t, 0:W], ALU.mult, ALU.add)
            dve.drain()

        @block.gpsimd
        def _(pool):
            pool.wait_ge(bound, 1)
            for t in range(NT):
                pool.wait_ge(sig, t + 1)
                nc.gpsimd.tensor_tensor(halves(k[:, t, :]), halves(k[:, t, :]), both(oml), ALU.mult)
            pool.drain()


def hgrn(K, q, fi, kk, o):
    nc = K.nc
    NS = 2 * NT
    UNITS = 2 * LEVELS
    ident = K.const("ident")
    incl = K.const("incl").rearrange("p (d i) -> p d i", d=2)
    strict = K.const("strict").rearrange("p (d i) -> p d i", d=2)
    level = K.const("level").bitcast(U32).rearrange("p (d n i) -> p d n i", d=2, n=LEVELS)
    with ExitStack() as ctx:
        qs = K.sb(ctx, "hg_q", [P, NTX, P])
        lf, ks, ekd, gc = (K.sb(ctx, "hg_" + n, [P, NS, P]) for n in ("lf", "k", "ekd", "gc"))
        kd = lf
        vs = K.sb(ctx, "hg_v", [P, NT, P])
        kT, egc, qe, att = (K.sb(ctx, "hg_" + n, [P, 2, NTX, P]) for n in ("kT", "egc", "qe", "att"))
        egl = K.sb(ctx, "hg_egl", [P, NS])
        S = ekd[:].rearrange("p (d t) i -> p d t i", d=2)
        E, ql = (K.sb(ctx, "hg_" + n, [P, 2, TX]) for n in ("E", "ql"))
        kl = ks[:, 0:2 * NTX, :].rearrange("p (u c) i -> p u (c i)", u=2)
        B = K.ps(ctx, "hg_banks", [P, 8, 512])
        span = lambda lo, n: B[:, lo:lo + n, :].rearrange("p b n -> p (b n)").rearrange("p (s i) -> p s i", i=P)
        staged, sums, taken, weighed, ds_ready, states, o_ready, o_out, head_done = (
            K.sem("hg_" + n) for n in ("staged", "sums", "taken", "weighed", "ds", "states", "o", "o_out", "head_done"))
        diff, e_ready, q_ready, k_ready, a_ready, seen, a_out = (
            K.sem("hg_" + n) for n in ("diff", "e", "ql", "kl", "att", "seen", "att_out"))
        block = ctx.enter_context(K.block())

        @block.gpsimd
        def _(pool):
            with pool.Fori(0, HEADS) as it:
                pool.wait_ge(taken, it + 1)
                nc.gpsimd.tensor_tensor(kd[:], ks[:], ekd[:], ALU.mult)
                for d in range(2):
                    nc.gpsimd.tensor_tensor(qe[:, d], qs[:], egc[:, d], ALU.mult)
                pool.drain()
                pool.sem_inc(weighed, 1)
                for n in range(UNITS):
                    pool.wait_ge(e_ready, it * UNITS + n + 1)
                    if n >= 2:
                        pool.wait_ge(a_ready, it * (UNITS + 2) + n + 1)
                    nc.gpsimd.tensor_tensor(kl[:, n % 2, :], kT[:, n % 2].rearrange("p c i -> p (c i)"), E[:, n % 2, :],
                                            ALU.mult).then_inc(k_ready, 1)

        @block.tensor
        def _(pe):
            pe.sem_inc(head_done, 1)
            with pe.Fori(0, HEADS) as it:
                pe.wait_ge(staged, it * 2 + 2)
                pe.wait_ge(o_out, it + 1)
                for s in range(NS):
                    nc.tensor.matmul(span(0, 3)[:, s, :], lf[:, s, :], incl[:, s // NT, :], start=True, stop=True)
                for d in range(2):
                    for lo, hi in ((0, 4), (4, 6)) if d == 0 else ((6, 8), (8, 12)):
                        nc.tensor.matmul(span(3, 3)[:, lo:hi, :], strict[:, 1 - d, :], lf[:, lo:hi, :], start=True, stop=True)
                for d in range(2):
                    for c in range(NTX):
                        last = nc.tensor.transpose(span(6, 2)[:, d * NTX + c, :], ks[:, d * NT + c, :], ident)
                last.then_inc(sums, 1)
                pe.wait_ge(taken, it + 1)
                for d in range(2):
                    for c in range(NTX):
                        last = nc.tensor.matmul(B[:, 6 + d, c * P:(c + 1) * P], kT[:, d, c, :], qs[:, c, :], start=True, stop=True)
                    last.then_inc(a_ready, 1)
                pe.wait_ge(weighed, it + 1)
                for s in range(NS):
                    last = nc.tensor.matmul(span(0, 3)[:, s, :], kd[:, s, :], vs[:, s % NT, :], start=True, stop=True)
                last.then_inc(ds_ready, 1)
                for n in range(UNITS):
                    pe.wait_ge(q_ready, it * UNITS + n + 1)
                    pe.wait_ge(k_ready, it * UNITS + n + 1)
                    pe.wait_ge(a_out, it * (UNITS + 2) + n + 1)
                    for c in range(NTX):
                        cols = slice(c * P, (c + 1) * P)
                        last = nc.tensor.matmul(B[:, 6 + n % 2, cols], kl[:, n % 2, cols], ql[:, n % 2, cols], start=True, stop=True)
                    last.then_inc(a_ready, 1)
                pe.wait_ge(a_out, it * (UNITS + 2) + UNITS + 2)
                pe.wait_ge(states, it + 1)
                for c in range(NTX):
                    for d in range(2):
                        nc.tensor.matmul(B[:, 5, c * P:(c + 1) * P], vs[:, c, :], att[:, d, c, :], start=(d == 0), stop=False)
                        last = nc.tensor.matmul(B[:, 5, c * P:(c + 1) * P], S[:, d, steps_of(d).index(c), :], qe[:, d, c, :],
                                                start=False, stop=(d == 1))
                last.then_inc(o_ready, 1)
                nc.tensor.matmul(B[:, 4, 0:P], ident, ident, start=True, stop=True).then_inc(head_done, 1)

        @block.scalar
        def _(act):
            act.sem_inc(o_out, 1)
            with act.Fori(0, HEADS) as it:
                act.wait_ge(head_done, it + 1)
                nc.scalar.copy(vs[:], fi[:, :, at((it + 2 * HEADS) * P, P)])
                nc.scalar.copy(qs[:], q[:, at(it), :].rearrange("p o (c i) -> p (o c) i", i=P))
                act.drain()
                act.sem_inc(staged, 1)
                act.wait_ge(sums, it + 1)
                nc.scalar.copy(gc[:], span(0, 3))
                nc.scalar.copy(kT[:].rearrange("p d c i -> p (d c) i"), span(6, 2))
                act.drain()
                nc.scalar.activation(ekd[:], span(3, 3), ACT.Exp)
                for d in range(2):
                    nc.scalar.activation(egc[:, d], gc[:, d * NT:d * NT + NTX, :], ACT.Exp)
                    nc.scalar.activation(egl[:, d * NT:(d + 1) * NT], gc[:, d * NT:(d + 1) * NT, last_of(d)], ACT.Exp)
                act.drain()
                act.sem_inc(taken, 1)
                for n in range(UNITS):
                    act.wait_ge(diff, it * UNITS + n + 1)
                    nc.scalar.activation(E[:, n % 2, :], E[:, n % 2, :], ACT.Abs)
                    act.drain()
                    nc.scalar.activation(E[:, n % 2, :], E[:, n % 2, :], ACT.Exp, scale=-1.0).then_inc(e_ready, 1)
                act.wait_ge(o_ready, it + 1)
                nc.scalar.copy(o[:, at(it), :].rearrange("p o (r c) -> p (o c) r", r=GRID_H),
                               B[:, 5, :].rearrange("p (c r) -> p c r", r=GRID_H)).then_inc(o_out, 1)

        @block.vector
        def _(dve):
            def keep(it, n):
                lev, d = divmod(n, 2)
                dve.wait_ge(a_ready, it * (UNITS + 2) + n + 3)
                dve.sem_inc(seen, 1)
                nc.vector.copy_predicated(att[:, d], level[:, d, lev, :].unsqueeze(1).broadcast_to([P, NTX, P]),
                                          B[:, 6 + d, :].rearrange("p (c i) -> p c i", i=P)).then_inc(a_out, 1)

            with dve.Fori(0, HEADS) as it:
                dve.wait_ge(head_done, it + 1)
                for d in range(2):
                    own = slice(d * NT, (d + 1) * NT)
                    nc.vector.tensor_copy(lf[:, own, :], fi[:, :, at((it + d * HEADS) * P, P)])
                    nc.vector.tensor_copy(ks[:, own, :], kk[:, :, at((it + d * HEADS) * P, P)])
                dve.drain()
                dve.sem_inc(staged, 1)
                dve.wait_ge(taken, it + 1)

                def distances(n):
                    lev, d = divmod(n, 2)
                    s = 1 << lev
                    if n >= 2:
                        dve.wait_ge(k_ready, it * UNITS + n - 1)
                        dve.wait_ge(q_ready, it * UNITS + n - 1)
                    x = gc[:, d * NT:d * NT + NTX, :].rearrange("p c i -> p (c i)").rearrange("p (b t) -> p b t", t=2 * s)
                    ref = x[:, :, s - 1:s] if d == 0 else x[:, :, s:s + 1]
                    nc.vector.tensor_tensor(E[:, n % 2, :].rearrange("p (b t) -> p b t", t=2 * s), x,
                                            ref.broadcast_to([P, TX // (2 * s), 2 * s]), ALU.subtract).then_inc(diff, 1)

                distances(0)
                for d in range(2):
                    dve.wait_ge(a_ready, it * (UNITS + 2) + d + 1)
                    nc.vector.tensor_tensor(att[:, d], B[:, 6 + d, :].rearrange("p (c i) -> p c i", i=P),
                                            ident.unsqueeze(1).broadcast_to([P, NTX, P]), ALU.mult).then_inc(a_out, 1)
                for n in range(UNITS):
                    d = n % 2
                    if n + 1 < UNITS:
                        distances(n + 1)
                    dve.wait_ge(e_ready, it * UNITS + n + 1)
                    if n >= 2:
                        dve.wait_ge(a_ready, it * (UNITS + 2) + n + 1)
                    nc.vector.tensor_tensor(ql[:, d, :], qs[:].rearrange("p c i -> p (c i)"), E[:, d, :], ALU.mult).then_inc(q_ready, 1)
                    if n == 1:
                        dve.wait_ge(ds_ready, it + 1)
                        for dd in range(2):
                            nc.vector.tensor_copy(S[:, dd, 1, :], span(0, 3)[:, dd * NT + steps_of(dd)[0], :])
                            nc.vector.memset(S[:, dd, 0, :], 0.0)
                        dve.drain()
                        for st in range(1, NT - 1):
                            for dd in range(2):
                                i = dd * NT + steps_of(dd)[st]
                                nc.vector.scalar_tensor_tensor(S[:, dd, st + 1, :], S[:, dd, st, :], egl[:, i:i + 1],
                                                               span(0, 3)[:, i, :], ALU.mult, ALU.add)
                            dve.drain()
                        dve.sem_inc(states, 1)
                    if n >= 1:
                        keep(it, n - 1)
                keep(it, UNITS - 1)


def times(K, a, b, hi, lo):
    nc = K.nc
    with ExitStack() as ctx:
        ready, hi_ready = K.sem("times_ready"), K.sem("times_hi")
        block = ctx.enter_context(K.block())

        @block.vector
        def _(dve):
            for c in range(HEADS):
                nc.vector.tensor_tensor(a[:, c, :], a[:, c, :], b[:, c, :], ALU.mult).then_inc(ready, 1)
            for c in range(0, HEADS, 2):
                dve.wait_ge(hi_ready, c + 1)
                lo_of(nc.vector, lo[:, c, :], a[:, c, :], hi[:, c, :])
            dve.drain()

        @block.scalar
        def _(act):
            for c in range(HEADS):
                act.wait_ge(ready, c + 1)
                nc.scalar.copy(hi[:, c, :], a[:, c, :]).then_inc(hi_ready, 1)

        @block.gpsimd
        def _(pool):
            for c in range(1, HEADS, 2):
                pool.wait_ge(hi_ready, c + 1)
                lo_of(nc.gpsimd, lo[:, c, :], a[:, c, :], hi[:, c, :])
            pool.drain()


def merge(K, h, w_in, dn, w_dn, hg, w_hg, m):
    nc = K.nc
    gv = w_in[:, C_GATE:C_GATE + 2 * D].rearrange("(c p) (s n) -> p c s n", p=P, s=2)
    bv = [w.rearrange("(c p) n -> p c n", p=P) for w in (w_dn, w_hg)]
    src = (dn, hg)
    with ExitStack() as ctx:
        wg = [K.sb(ctx, f"gate_w{u}", [P, KD, 2, P]) for u in range(2)]
        wb = [K.sb(ctx, f"branch_w{u}", [P, 2, HEADS, P]) for u in range(2)]
        wgh = [K.sb(ctx, f"gate_w_hi{u}", [P, KD, 2, P], FR) for u in range(2)]
        wbh = [K.sb(ctx, f"branch_w_hi{u}", [P, 2, HEADS, P], FR) for u in range(2)]
        wgl, wbl = ([K.lo(t) for t in w] for w in (wg, wb))
        sig = K.sb(ctx, "gate_sig", [P, 2, 2, TX])
        acc = K.ps(ctx, "merge_acc", [P, 2, 4, TX])
        w_full, w_hi, w_split, acc_full, sig_full, out = (
            [K.sem("mrg_" + n) for _ in range(2)] for n in ("w_full", "w_hi", "w_split", "acc_full", "sig_full", "out"))
        block = ctx.enter_context(K.block())

        @block.sync
        def _(sp):
            with sp.Fori(0, KD // 2) as it:
                for u in range(2):
                    cols = at((it * 2 + u) * P, P)
                    sp.wait_ge(acc_full[u], it + 1)
                    for s in range(2):
                        sp.dma_start(wg[u][:, :, s, :], gv[:, :, s, cols]).then_inc(w_full[u], 16)
                        sp.dma_start(wb[u][:, s], bv[s][:, :, cols]).then_inc(w_full[u], 16)

        @block.gpsimd
        def _(pool):
            with pool.Fori(0, KD // 2) as it:
                for u in range(2):
                    pool.wait_ge(w_hi[u], it + 1)
                    lo_of(nc.gpsimd, wgl[u][:], wg[u][:], wgh[u][:])
                    lo_of(nc.gpsimd, wbl[u][:], wb[u][:], wbh[u][:])
                    pool.drain()
                    pool.sem_inc(w_split[u], 1)

        @block.tensor
        def _(pe):
            for u in range(2):
                pe.sem_inc(acc_full[u], 1)
            with pe.Fori(0, KD // 2) as it:
                for u in range(2):
                    pe.wait_ge(w_split[u], it + 1)
                    pe.wait_ge(out[u], it + 1)
                    for s in range(2):
                        for c in range(KD):
                            products(nc, acc[:, u, s, :], (wgh[u][:, c, s, :], wgl[u][:, c, s, :]),
                                     [t[:, c, 0:TX] for t in h], c == 0, c == KD - 1)
                        for c in range(HEADS):
                            last = products(nc, acc[:, u, 2 + s, :], (wbh[u][:, s, c, :], wbl[u][:, s, c, :]),
                                            [t[:, c, :] for t in src[s]], c == 0, c == HEADS - 1)
                    last.then_inc(acc_full[u], 1)

        @block.scalar
        def _(act):
            def hi_weights(it, u):
                act.wait_ge(w_full[u], it * 64 + 64)
                nc.scalar.copy(wgh[u][:], wg[u][:])
                nc.scalar.copy(wbh[u][:], wb[u][:])
                act.drain()
                act.sem_inc(w_hi[u], 1)

            def pair(it, more):
                for u in range(2):
                    if u == 0 or more:
                        hi_weights(it + u, 1 - u)
                    act.wait_ge(acc_full[u], it + 2)
                    act.wait_ge(out[u], it + 1)
                    nc.scalar.activation(sig[:, u], acc[:, u, 0:2, :], ACT.Sigmoid).then_inc(sig_full[u], 1)

            hi_weights(0, 0)
            with act.Fori(0, KD // 2 - 1) as it:
                pair(it, True)
            pair(KD // 2 - 1, False)

        @block.vector
        def _(dve):
            for u in range(2):
                dve.sem_inc(out[u], 1)
            with dve.Fori(0, KD // 2) as it:
                for u in range(2):
                    dve.wait_ge(sig_full[u], it + 1)
                    nc.vector.tensor_tensor(sig[:, u], sig[:, u], acc[:, u, 2:4, :], ALU.mult)
                    dve.drain()
                    nc.vector.tensor_tensor(m[:, at(it * 2 + u), :], sig[:, u, 0:1, :], sig[:, u, 1:2, :], ALU.add).then_inc(out[u], 1)


def route(K, h, w_router, h_rows, table, gate, dest, slots, blocks):
    nc = K.nc
    NB = NE
    with ExitStack() as ctx:
        wr = K.sb(ctx, "router_w", [P, KD, NG + NE])
        rows = K.sb(ctx, "h_rows", [P, 2, D])
        L = K.sb(ctx, "logits", [P, NTX, NG + NE])
        g1, g2, eg, oh = (K.sb(ctx, "grp_" + n, [P, NTX, NG]) for n in ("a", "b", "e", "oh"))
        gm, gs = K.sb(ctx, "grp_max", [P, NTX]), K.sb(ctx, "grp_sum", [P, NTX])
        pick = K.sb(ctx, "pick", [P, NTX, EPG, NG])
        p, e1 = K.sb(ctx, "exp_p", [P, NTX, EPG]), K.sb(ctx, "exp_val", [P, NTX, EPG])
        chosen = K.sb(ctx, "chosen", [P, TOPK, NTX, EPG])
        top = K.sb(ctx, "top", [P, TOPK, NTX])
        m0, m1 = K.sb(ctx, "max_a", [P, NTX]), K.sb(ctx, "max_b", [P, NTX])
        M = K.sb(ctx, "assigned", [P, TOPK, NTX, NE])
        Ms = K.sb(ctx, "assigned_any", [P, NTX, NE])
        cnt, nb, ca, cb, start = (K.sb(ctx, "cnt_" + n, [P, NE]) for n in ("n", "blocks", "a", "b", "start"))
        where = K.sb(ctx, "where", [P, NTX, NE])
        picked = K.sb(ctx, "picked", [P, TOPK, NTX, NE])
        destf = K.sb(ctx, "destf", [P, TOPK, NTX])
        be = K.sb(ctx, "block_expert", [P, 1])
        pairs = K.sb(ctx, "pairs", [1, 1], I32)
        zero = K.sb(ctx, "zero", [NBLK, P])
        tab = K.sb(ctx, "tab", [NBLK, P])
        lp = K.ps(ctx, "route_logits", [P, NTX, NG + NE])
        cp = K.ps(ctx, "route_counts", [P, NTX + 1, NE])
        bp = K.ps(ctx, "route_blocks", [P, P])
        tp = K.ps(ctx, "route_turned", [P, 2, D])
        names = ("w", "logits", "shifted", "exps", "shifted2", "exps2", "assigned", "counts", "be", "bp", "dest",
                 "zeroed", "cleared", "scattered", "tab", "tab_turned", "turned", "rows", "stored0", "stored1", "done")
        (w_full, logits, shifted, exps, shifted2, exps2, assigned, counts, be_ready, bp_ready, dest_ready,
         zeroed, cleared, scattered, tab_full, tab_turned, turned, rows_out, stored0, stored1, done) = (
            K.sem("rt_" + n) for n in names)
        stored = (stored0, stored1)
        block = ctx.enter_context(K.block())

        @block.sync
        def _(sp):
            sp.dma_start(wr[:], w_router.rearrange("(c p) n -> p c n", p=P)).then_inc(w_full, 16)
            sp.wait_ge(zeroed, 1)
            sp.dma_start(table.rearrange("(b p) o -> b (p o)", p=P), zero[:]).then_inc(cleared, 16)
            for t in range(NTX):
                sp.wait_ge(rows_out, t + 1)
                sp.dma_start(h_rows[t * P:(t + 1) * P, :], rows[:, t % 2, :]).then_inc(stored[t % 2], 16)
            sp.wait_ge(scattered, 16 * TOPK * NTX)
            sp.dma_start(tab[:], table.rearrange("(b p) o -> b (p o)", p=P)).then_inc(tab_full, 16)
            for u in range(2):
                sp.wait_ge(stored[u], 16 * NTX // 2)

        @block.gpsimd
        def _(pool):
            nc.gpsimd.memset(zero[:], 0.0)
            pool.drain()
            pool.sem_inc(zeroed, 1)
            pool.wait_ge(cleared, 16)
            pool.wait_ge(dest_ready, 1)
            for k in range(TOPK):
                for t in range(NTX):
                    nc.gpsimd.indirect_dma_start(
                        out=table, out_offset=bass.IndirectOffsetOnAxis(ap=dest[:, k, t:t + 1], axis=0),
                        in_=K.const("tokid")[:, t:t + 1], in_offset=None).then_inc(scattered, 16)

        @block.tensor
        def _(pe):
            ident = K.const("ident")
            ones = K.const("ones")
            before = K.const("strict")[:, 0:P]
            pe.wait_ge(w_full, 16)
            for t in range(NTX):
                for c in range(KD):
                    last = nc.tensor.matmul(lp[:, t, :], h[:, c, t * P:(t + 1) * P], wr[:, c, :], start=(c == 0), stop=(c == KD - 1))
            last.then_inc(logits, 1)
            for t in range(NTX):
                if t >= 2:
                    pe.wait_ge(rows_out, t - 1)
                for c in range(KD):
                    last = nc.tensor.transpose(tp[:, t % 2, c * P:(c + 1) * P], h[:, c, t * P:(t + 1) * P], ident)
                last.then_inc(turned, 1)
            pe.wait_ge(assigned, 1)
            for t in range(NTX):
                for b in range(t):
                    nc.tensor.matmul(cp[:, t, :], ones, Ms[:, b, :], start=(b == 0), stop=False)
                nc.tensor.matmul(cp[:, t, :], before, Ms[:, t, :], start=(t == 0), stop=True)
            for t in range(NTX):
                last = nc.tensor.matmul(cp[:, NTX, :], ones, Ms[:, t, :], start=(t == 0), stop=(t == NTX - 1))
            last.then_inc(counts, 1)
            pe.wait_ge(be_ready, 1)
            nc.tensor.matmul(bp[0:1, :], be[:], ident, start=True, stop=True).then_inc(bp_ready, 1)
            pe.wait_ge(tab_full, 16)
            pe.wait_ge(done, 1)
            nc.tensor.transpose(bp[:, 0:NBLK], tab[:], ident[0:NBLK, 0:NBLK]).then_inc(tab_turned, 1)

        @block.scalar
        def _(act):
            act.wait_ge(shifted, 1)
            nc.scalar.activation(eg[:], g1[:], ACT.Exp).then_inc(exps, 1)
            for t in range(NTX):
                act.wait_ge(turned, t + 1)
                if t >= 2:
                    act.wait_ge(stored[t % 2], 16)
                nc.scalar.copy(rows[:, t % 2, :], tp[:, t % 2, :]).then_inc(rows_out, 1)
            act.wait_ge(shifted2, 1)
            nc.scalar.activation(p[:], p[:], ACT.Exp).then_inc(exps2, 1)

        @block.vector
        def _(dve):
            tt, ts, rd = nc.vector.tensor_tensor, nc.vector.tensor_scalar, nc.vector.tensor_reduce
            over_g = lambda a: a[:].unsqueeze(2).broadcast_to([P, NTX, NG])
            over_e = lambda a: a[:].unsqueeze(2).broadcast_to([P, NTX, EPG])
            rank_g = K.const("group_rank").unsqueeze(1).broadcast_to([P, NTX, NG])
            rank_e = K.const("expert_rank").unsqueeze(1).broadcast_to([P, NTX, EPG])
            dve.wait_ge(logits, 1)
            tt(L[:], lp[:], K.row("b_router").unsqueeze(1).broadcast_to([P, NTX, NG + NE]), ALU.add)
            dve.drain()
            rd(gm[:], L[:, :, 0:NG], AX_X, ALU.max)
            dve.drain()
            tt(g1[:], L[:, :, 0:NG], over_g(gm), ALU.subtract).then_inc(shifted, 1)
            tt(g2[:], L[:, :, 0:NG], over_g(gm), ALU.is_equal)
            dve.drain()
            tt(g2[:], g2[:], rank_g, ALU.mult)
            dve.drain()
            rd(gm[:], g2[:], AX_X, ALU.max)
            dve.drain()
            tt(oh[:], g2[:], over_g(gm), ALU.is_equal)
            dve.drain()
            tt(pick[:], L[:, :, NG:].rearrange("p t (g j) -> p t j g", g=NG),
               oh[:].unsqueeze(2).broadcast_to([P, NTX, EPG, NG]), ALU.mult)
            dve.drain()
            rd(p[:], pick[:], AX_X, ALU.add)
            dve.drain()
            rd(m0[:], p[:], AX_X, ALU.max)
            dve.drain()
            tt(p[:], p[:], over_e(m0), ALU.subtract).then_inc(shifted2, 1)
            dve.wait_ge(exps, 1)
            rd(gs[:], eg[:], AX_X, ALU.add)
            dve.drain()
            nc.vector.reciprocal(gs[:], gs[:])
            dve.wait_ge(exps2, 1)
            rd(m0[:], p[:], AX_X, ALU.add)
            dve.drain()
            nc.vector.reciprocal(m0[:], m0[:])
            dve.drain()
            tt(p[:], p[:], over_e(m0), ALU.mult)
            dve.drain()
            for k in range(TOPK):
                rd(top[:, k, :], p[:], AX_X, ALU.max)
                dve.drain()
                tt(e1[:], p[:], top[:, k, :].unsqueeze(2).broadcast_to([P, NTX, EPG]), ALU.is_equal)
                dve.drain()
                tt(e1[:], e1[:], rank_e, ALU.mult)
                dve.drain()
                rd(m1[:], e1[:], AX_X, ALU.max)
                dve.drain()
                tt(chosen[:, k], e1[:], over_e(m1), ALU.is_equal)
                dve.drain()
                if k + 1 < TOPK:
                    nc.vector.scalar_tensor_tensor(p[:], chosen[:, k], -2.0, p[:], ALU.mult, ALU.add)
                    dve.drain()
            tt(m0[:], top[:, 0, :], top[:, 1, :], ALU.add)
            dve.drain()
            nc.vector.reciprocal(m0[:], m0[:])
            for k in range(TOPK):
                tt(gate[:, k, :], top[:, k, :], gs[:], ALU.mult)
                for t in range(NTX):
                    tt(M[:, k, t, :].rearrange("p (g j) -> p g j", g=NG),
                       oh[:, t, :].unsqueeze(2).broadcast_to([P, NG, EPG]),
                       chosen[:, k, t, :].unsqueeze(1).broadcast_to([P, NG, EPG]), ALU.mult)
            dve.drain()
            for k in range(TOPK):
                tt(gate[:, k, :], gate[:, k, :], m0[:], ALU.mult)
            tt(Ms[:], M[:, 0], M[:, 1], ALU.add)
            dve.drain()
            dve.sem_inc(assigned, 1)
            dve.wait_ge(counts, 1)
            nc.vector.tensor_copy(cnt[:], cp[:, NTX, :])
            dve.drain()
            ts(nb[:], cnt[:], 0.0, None, ALU.is_gt)
            for m in range(1, TX // MB):
                dve.drain()
                nc.vector.scalar_tensor_tensor(nb[:], cnt[:], float(MB * m), nb[:], ALU.is_gt, ALU.add)
            dve.drain()
            src, step, i = nb, 1, 0
            while step < NE:
                dst = (ca, cb)[i % 2]
                tt(dst[:, step:], src[:, step:], src[:, 0:NE - step], ALU.add)
                nc.vector.tensor_copy(dst[:, 0:step], src[:, 0:step])
                dve.drain()
                src, step, i = dst, 2 * step, i + 1
            spare = (ca, cb)[i % 2]
            tt(start[:], src[:], nb[:], ALU.subtract)
            ts(spare[:], src[:], K.const("blk"), None, ALU.is_le)
            nc.vector.tensor_copy(pairs[:], src[0:1, NE - 1:NE])
            dve.drain()
            rd(be[:], spare[:], AX_X, ALU.add)
            ts(start[:], start[:], float(MB), None, ALU.mult)
            dve.drain()
            ts(be[:], be[:], float(NE - 1), None, ALU.min).then_inc(be_ready, 1)
            tt(where[:], cp[:, 0:NTX, :], start[:].unsqueeze(1).broadcast_to([P, NTX, NE]), ALU.add)
            dve.drain()
            for k in range(TOPK):
                tt(picked[:, k], M[:, k], where[:], ALU.mult)
            dve.drain()
            for k in range(TOPK):
                rd(destf[:, k, :], picked[:, k], AX_X, ALU.add)
            dve.drain()
            nc.vector.tensor_copy(dest[:], destf[:])
            dve.drain()
            dve.sem_inc(dest_ready, 1)
            dve.wait_ge(bp_ready, 1)
            nc.vector.tensor_copy(blocks[0:1, 0:NBLK], bp[0:1, 0:NBLK])
            ts(pairs[:], pairs[:], 1, None, ALU.add)
            dve.drain()
            ts(blocks[0:1, NBLK:NBLK + 1], pairs[:], 1, None, ALU.arith_shift_right)
            dve.drain()
            dve.sem_inc(done, 1)
            dve.wait_ge(tab_turned, 1)
            nc.vector.tensor_copy(slots[:], bp[:, 0:NBLK])
            dve.drain()


def experts(K, w_gate, w_up, w_down, h_rows, y_rows, slots, blocks):
    nc = K.nc
    ident = K.const("ident")
    ORDER = (("gate", 0), ("up", 0), ("gate", 1), ("up", 1), ("down", 0), ("down", 1))
    HALVES = 2 * len(ORDER)
    RING = 4
    half_cols = KD * DE // 2

    def done_count(it, name, u):
        return it * HALVES + (HALVES + 2 * ORDER.index((name, u)) + 2)

    with ExitStack() as ctx:
        wt = {k: K.sb(ctx, f"exp_{k[0]}{k[1]}", [P, KD * DE]) for k in ORDER}
        wl = {k: K.lo(wt[k]) for k in ORDER}
        wh = [K.sb(ctx, f"exp_hi{r}", [P, half_cols], FR) for r in range(RING)]
        idx = K.sb(ctx, "exp_idx", [P, 1], U32)
        xr = K.sb(ctx, "exp_x", [P, D])
        xh, xl = ([K.sb(ctx, f"exp_x{n}{u}", [P, KD * P], FR) for u in range(2)] for n in ("hi", "lo"))
        hid = [K.sb(ctx, f"exp_hid{u}", [P, DE]) for u in range(2)]
        hh, hl = (K.sb(ctx, f"exp_hid_{n}", [P, DE], FR) for n in ("hi", "lo"))
        y = K.sb(ctx, "exp_y", [P, D])
        tp = K.ps(ctx, "exp_turned", [P, D])
        gp = K.ps(ctx, "exp_gate_acc", [P, 2, DE])
        up = K.ps(ctx, "exp_up_acc", [P, 2, DE])
        yp = K.ps(ctx, "exp_down_acc", [P, D])
        full = {k: K.sem(f"ex_{k[0]}_full{k[1]}") for k in ORDER}
        half_hi, half_split, half_done = (K.sem("ex_half_" + n) for n in ("hi", "split", "done"))
        x_full, turned, x_hi, x_split, silu, hid_ready, seen, hid_turned, h_hi, h_split, y_out, y_stored = (
            K.sem("ex_" + n) for n in ("x", "turned", "x_hi", "x_split", "silu", "hid", "seen", "hid_turned", "h_hi",
                                       "h_split", "y_out", "y_stored"))
        block = ctx.enter_context(K.block())

        def pairs_of(engine):
            return engine.value_load(blocks[0:1, NBLK:NBLK + 1], min_val=1, max_val=NPAIR)

        def half(t, i):
            return t[:, i * half_cols:(i + 1) * half_cols]

        @block.sync
        def _(sp):
            n_pairs = pairs_of(sp)
            with sp.Fori(0, NPAIR) as it:
                with sp.If(it < n_pairs):
                    e = [sp.value_load(blocks[0:1, at(it * 2 + u)], min_val=0, max_val=NE - 1) for u in range(2)]
                    for k in ORDER:
                        w = {"gate": w_gate, "up": w_up, "down": w_down}[k[0]]
                        sp.wait_ge(half_done, it * HALVES + (2 * ORDER.index(k) + 2))
                        sp.dma_start(wt[k][:].rearrange("p (c n) -> p c n", n=w.shape[2]),
                                     w[at(e[k[1]])].rearrange("e (c p) n -> p (e c) n", p=P)).then_inc(full[k], 16)

        @block.gpsimd
        def _(pool):
            n_pairs = pairs_of(pool)
            with pool.Fori(0, NPAIR) as it:
                with pool.If(it < n_pairs):
                    for u in range(2):
                        pool.wait_ge(turned, it * 2 + u + 1)
                        nc.gpsimd.tensor_copy(idx[:], slots[:, at(it * 2 + u)])
                        pool.drain()
                        nc.gpsimd.indirect_dma_start(out=xr[:], out_offset=None, in_=h_rows,
                                                     in_offset=bass.IndirectOffsetOnAxis(ap=idx[:], axis=0)).then_inc(x_full, 16)

        @block.tensor
        def _(pe):
            pe.sem_inc(turned, 1)
            pe.sem_inc(half_done, HALVES)
            n_pairs = pairs_of(pe)

            def turn(it, u):
                b = it * 2 + u
                pe.wait_ge(x_full, b * 16 + 16)
                pe.wait_ge(x_split, b + 1)
                for c in range(KD):
                    last = nc.tensor.transpose(tp[:, c * P:(c + 1) * P], xr[:, c * P:(c + 1) * P], ident)
                last.then_inc(turned, 1)

            def up_product(it, name, u, acc):
                for i in range(2):
                    j = 2 * ORDER.index((name, u)) + i
                    pe.wait_ge(half_split, it * HALVES + (j + 1))
                    for c in range(KD // 2):
                        cols, rows = slice(c * DE, (c + 1) * DE), slice((i * KD // 2 + c) * P, (i * KD // 2 + c + 1) * P)
                        last = products(nc, acc[:, u, :], (xh[u][:, rows], xl[u][:, rows]),
                                        (wh[j % RING][:, cols], half(wl[name, u], i)[:, cols]),
                                        i == 0 and c == 0, i == 1 and c == KD // 2 - 1)
                    last.then_inc(half_done, 1)

            def turn_hidden(it, u):
                pe.wait_ge(hid_ready, it * 2 + u + 1)
                pe.sem_inc(seen, 1)
                for c in range(KE):
                    last = nc.tensor.transpose(gp[:, u, c * P:(c + 1) * P], hid[u][:, c * P:(c + 1) * P], ident)
                last.then_inc(hid_turned, 1)

            def down_product(it, u):
                pe.wait_ge(h_split, it * 2 + u + 1)
                pe.wait_ge(y_out, it * 2 + u + 1)
                for i in range(2):
                    j = 2 * ORDER.index(("down", u)) + i
                    pe.wait_ge(half_split, it * HALVES + (j + 1))
                    for c in range(KE // 2):
                        rows = slice((i * KE // 2 + c) * P, (i * KE // 2 + c + 1) * P)
                        for n in range(2):
                            cols = slice(c * D + n * 512, c * D + (n + 1) * 512)
                            last = products(nc, yp[:, n * 512:(n + 1) * 512], (hh[:, rows], hl[:, rows]),
                                            (wh[j % RING][:, cols], half(wl["down", u], i)[:, cols]),
                                            i == 0 and c == 0, i == 1 and c == KE // 2 - 1)
                    last.then_inc(half_done, 1)

            turn(0, 0)
            with pe.Fori(0, NPAIR) as it:
                with pe.If(it < n_pairs):
                    pe.wait_ge(x_split, it * 2 + 2)
                    up_product(it, "gate", 0, gp)
                    turn(it, 1)
                    up_product(it, "up", 0, up)
                    pe.wait_ge(x_split, it * 2 + 3)
                    up_product(it, "gate", 1, gp)
                    turn_hidden(it, 0)
                    up_product(it, "up", 1, up)
                    down_product(it, 0)
                    turn_hidden(it, 1)
                    with pe.If(it + 1 < n_pairs):
                        turn(it + 1, 0)
                    down_product(it, 1)

        @block.scalar
        def _(act):
            act.sem_inc(y_out, 1)
            act.sem_inc(y_stored, 16)
            n_pairs = pairs_of(act)

            def hi_weights(it, *halves):
                for j in halves:
                    k = ORDER[j // 2]
                    if j % 2 == 0:
                        act.wait_ge(full[k], it * 16 + 16)
                    act.wait_ge(half_done, it * HALVES + (HALVES + j - RING + 1))
                    nc.scalar.copy(wh[j % RING][:], half(wt[k], j % 2)).then_inc(half_hi, 1)

            def hi_tokens(it, u):
                act.wait_ge(turned, it * 2 + u + 2)
                nc.scalar.copy(xh[u][:], tp[:]).then_inc(x_hi, 1)

            def gate(it, u):
                act.wait_ge(half_done, done_count(it, "gate", u))
                nc.scalar.activation(hid[u][:], gp[:, u, :], ACT.Silu).then_inc(silu, 1)

            def hi_hidden(it, u):
                act.wait_ge(hid_turned, it * 2 + u + 1)
                nc.scalar.copy(hh[:], gp[:, u, :]).then_inc(h_hi, 1)

            def output(it, u):
                b = it * 2 + u
                act.wait_ge(half_done, done_count(it, "down", u))
                act.wait_ge(y_stored, b * 16 + 16)
                nc.scalar.copy(y[:], yp[:]).then_inc(y_out, 1)
                act.wait_ge(y_out, b + 2)
                act.dma_start(y_rows[at(b * MB, MB), :], y[:]).then_inc(y_stored, 16)

            def begin(it):
                hi_weights(it, 0, 1)
                hi_tokens(it, 0)

            begin(0)
            with act.Fori(0, NPAIR) as it:
                with act.If(it < n_pairs):
                    hi_weights(it, 2, 3, 4, 5)
                    gate(it, 0)
                    hi_tokens(it, 1)
                    hi_weights(it, 6, 7)
                    hi_hidden(it, 0)
                    gate(it, 1)
                    hi_weights(it, 8, 9, 10, 11)
                    hi_hidden(it, 1)
                    output(it, 0)
                    with act.If(it + 1 < n_pairs):
                        begin(it + 1)
                    output(it, 1)
                with act.Else():
                    for u in range(2):
                        act.dma_start(y_rows[at((it * 2 + u) * MB, MB), :], y[:]).then_inc(y_stored, 16)
            act.wait_ge(y_stored, 16 * (NBLK + 1))

        @block.vector
        def _(dve):
            dve.sem_inc(x_split, 1)
            n_pairs = pairs_of(dve)

            def lo_weights(it, *halves):
                for j in halves:
                    k, i = ORDER[j // 2], j % 2
                    dve.wait_ge(half_hi, it * HALVES + (j + 1))
                    lo_of(nc.vector, half(wl[k], i), half(wt[k], i), wh[j % RING][:]).then_inc(half_split, 1)

            def lo_tokens(it, u):
                dve.wait_ge(x_hi, it * 2 + u + 1)
                lo_of(nc.vector, xl[u][:], tp[:], xh[u][:]).then_inc(x_split, 1)

            def hidden(it, u):
                b = it * 2 + u
                dve.wait_ge(silu, b + 1)
                dve.wait_ge(half_done, done_count(it, "up", u))
                nc.vector.tensor_tensor(hid[u][:], hid[u][:], up[:, u, :], ALU.mult).then_inc(hid_ready, 1)

            def lo_hidden(it, u):
                dve.wait_ge(h_hi, it * 2 + u + 1)
                lo_of(nc.vector, hl[:], gp[:, u, :], hh[:]).then_inc(h_split, 1)

            def begin(it):
                lo_weights(it, 0, 1)
                lo_tokens(it, 0)

            begin(0)
            with dve.Fori(0, NPAIR) as it:
                with dve.If(it < n_pairs):
                    lo_weights(it, 2, 3, 4, 5)
                    lo_tokens(it, 1)
                    hidden(it, 0)
                    lo_weights(it, 6, 7)
                    lo_hidden(it, 0)
                    lo_weights(it, 8, 9)
                    hidden(it, 1)
                    lo_weights(it, 10, 11)
                    lo_hidden(it, 1)
                    with dve.If(it + 1 < n_pairs):
                        begin(it + 1)


def combine(K, gate, dest, y_rows):
    nc = K.nc
    ident = K.const("ident")
    with ExitStack() as ctx:
        rows = K.sb(ctx, "cmb_rows", [P, TOPK, NTX, D])
        f = K.sb(ctx, "cmb_f", [P, NTX, D])
        tp = K.ps(ctx, "cmb_turned", [P, 2, 2, TX])
        got = [K.sem(f"cmb_got{t}") for t in range(NTX)]
        summed, turned, out = (K.sem("cmb_" + n) for n in ("summed", "turned", "out"))
        block = ctx.enter_context(K.block())

        @block.gpsimd
        def _(pool):
            for t in range(NTX):
                for k in range(TOPK):
                    nc.gpsimd.indirect_dma_start(out=rows[:, k, t, :], out_offset=None, in_=y_rows,
                                                 in_offset=bass.IndirectOffsetOnAxis(ap=dest[:, k, t:t + 1], axis=0)).then_inc(got[t], 16)

        @block.vector
        def _(dve):
            for t in range(NTX):
                dve.wait_ge(got[t], 16 * TOPK)
                nc.vector.tensor_scalar(f[:, t, :], rows[:, 0, t, :], gate[:, 0, t:t + 1], None, ALU.mult)
                dve.drain()
                nc.vector.scalar_tensor_tensor(f[:, t, :], rows[:, 1, t, :], gate[:, 1, t:t + 1], f[:, t, :],
                                               ALU.mult, ALU.add).then_inc(summed, 1)
            for n in range(KD):
                dve.wait_ge(turned, n + 1)
                nc.vector.scalar_tensor_tensor(K.x[:, n, 0:TX], tp[:, n % 2, 0, :], K.mod[:, 0, 40 + n:41 + n],
                                               K.x[:, n, 0:TX], ALU.mult, ALU.add).then_inc(out, 1)
            dve.drain()

        @block.tensor
        def _(pe):
            pe.wait_ge(summed, NTX)
            for n in range(KD):
                if n >= 2:
                    pe.wait_ge(out, n - 1)
                for t in range(NTX):
                    last = nc.tensor.transpose(tp[:, n % 2, 0, t * P:(t + 1) * P], f[:, t, n * P:(n + 1) * P], ident)
                last.then_inc(turned, 1)


def second_block(K, io):
    nc = K.nc
    w_in = io["w_in_2"][0]
    ada(K, io["w_ada_2"][0], "ada_b2", 1, (K.x[:, :, TX:TT], io["ctx2T"]))
    normed = lambda ctx, *how: Normed(K, ctx, "norm_mix2", 8, 0, *how)

    with ExitStack() as ctx:
        odn = K.sb(ctx, "odn", [P, HEADS, TX])
        with ExitStack() as dn:
            qkv = K.sb(dn, "dn_qkv", [P, 3 * HEADS, TT])
            beta, g = (K.sb(dn, n, [P, NT, 8]) for n in ("dn_beta", "dn_g"))
            with ExitStack() as proj:
                h = normed(proj, True)
                dn_inputs(K, h, w_in, qkv)
                dn_gates(K, h.parts, w_in, beta, g)
            head_norm(K, qkv[:, 0:HEADS, :], HEADS, TX, qkv[:, 0:HEADS, :], 1.0, EPS, P ** -0.5)
            head_norm(K, qkv[:, HEADS:2 * HEADS, :], HEADS, TT, qkv[:, HEADS:2 * HEADS, :], 1.0, EPS, 1.0)
            deltanet(K, qkv, beta, g, odn)
        ohg = K.sb(ctx, "ohg", [P, HEADS, TX])
        with ExitStack() as hg:
            fi = K.sb(hg, "hg_fi", [P, NT, 3 * HEADS * P])
            q = K.sb(hg, "hg_qs", [P, HEADS, TX])
            with ExitStack() as proj:
                h = normed(proj, True, True)
                features(K, h.parts, w_in, C_HQ, HEADS, TX,
                         lambda n, sums: nc.scalar.activation(q[:, at(n), :], sums, ACT.Silu), first=h)
                token_rows(K, h.parts, w_in, C_HF, 3 * HEADS * P, NT, fi)
            kk = K.sb(hg, "hg_kk", [P, NT, 2 * HEADS * P])
            hg_gates(K, fi, kk)
            hgrn(K, q, fi, kk, ohg)
        h = normed(ctx, False)
        parts = []
        for col, o, gain in ((C_Z_DN, odn, "dn_norm"), (C_Z_HG, ohg, "hg_norm")):
            hi = K.sb(ctx, "branch_hi", [P, HEADS, TX], FR)
            with ExitStack() as gating:
                z = K.sb(gating, "z", [P, HEADS, TX])
                features(K, h.parts, w_in, col, HEADS, TX,
                         lambda n, sums: nc.scalar.activation(z[:, at(n), :], sums, ACT.Silu), first=None if parts else h)
                head_norm(K, o, HEADS, TX, o, 1.0 / P, EPS, K.vec(gain))
                lo = K.lo(o)
                times(K, o, z, hi, lo)
            parts.append((hi, lo))
        m = K.sb(ctx, "merged", [P, KD, TX])
        merge(K, h.parts, w_in, parts[0], io["w_br_dn_2"][0], parts[1], io["w_br_hg_2"][0], m)
        residual(K, m, io["w_out_2"][0], 16, TX)
    h_rows = nc.dram_tensor("h_rows", (TX, D), F32, kind="Internal").ap()
    table = nc.dram_tensor("slot_table", (NBLK * MB, 1), F32, kind="Internal").ap()
    y_rows = nc.dram_tensor("y_rows", (NBLK * MB, D), F32, kind="Internal").ap()
    with ExitStack() as ctx:
        gate = K.sb(ctx, "gate", [P, TOPK, NTX])
        dest = K.sb(ctx, "dest", [P, TOPK, NTX], U32)
        slots = K.sb(ctx, "slots", [P, NBLK], U32)
        blocks = K.sb(ctx, "blocks", [1, NBLK + 1], I32)
        with ExitStack() as rt:
            h = K.sb(rt, "ffn_h", [P, KD, TX])
            norm(K, K.x, h, "norm_ffn2", 32, 24)
            route(K, h, io["w_router"], h_rows, table, gate, dest, slots, blocks)
        experts(K, io["w_exp_gate_2"][0], io["w_exp_up_2"][0], io["w_exp_down_2"][0], h_rows, y_rows, slots, blocks)
        combine(K, gate, dest, y_rows)
    norm(K, K.x, K.x, "g_final", 0, 0, mod=False)


def store(K, out):
    nc = K.nc
    stored = K.sem("stored")
    with K.block() as block:
        @block.sync
        def _(sp):
            sp.dma_start(out.rearrange("(c p) t -> p c t", p=P), K.x[:, :, 0:TX]).then_inc(stored, 16)
            sp.wait_ge(stored, 16)


def program(nc, io, out):
    with ExitStack() as whole:
        K = Core(nc)
        K.x = K.sb(whole, "x", [P, KD, TT])
        K.consts = K.sb(whole, "consts", [P, N_CONST])
        K.vecs = K.sb(whole, "vecs", [P, N_VEC])
        K.rows = K.sb(whole, "rows", [P, N_ROW])
        K.cond = K.sb(whole, "cond", [P, 4 * KD])
        K.mod = K.sb(whole, "mod", [P, 2, 48])
        K.subln = K.sb(whole, "subln", [P, 1])
        load_all(K, io["consts"], io["vecs"], io["rows"])
        scaled_subln(K)
        first_block(K, io)
        second_block(K, io)
        store(K, out)


def scaled_subln(K):
    nc = K.nc
    with K.block() as block:
        @block.vector
        def _(dve):
            nc.vector.tensor_scalar(K.subln[:], K.vec("subln"), 1.0 - LAM_INIT, None, ALU.mult)
            dve.drain()


def layout(inputs):
    f = {k: np.asarray(v) for k, v in inputs.items()}
    rows = lambda a: np.ascontiguousarray(a).reshape(-1, P)
    taps = lambda a: rows(a)
    vec = {
        "c": f["c"], "c_ctx": f["c_ctx"], "c2": f["c_2"], "c_ctx2": f["c_ctx_2"],
        "ada_b0": f["ada_b"][0], "ada_b1": f["ada_b"][1], "ada_b2": f["b_ada_2"],
        "norm_mix0": f["norm_mix"][0], "norm_mix1": f["norm_mix"][1], "norm_mix2": f["g_mix_2"],
        "norm_ffn0": f["norm_ffn"][0], "norm_ffn1": f["norm_ffn"][1], "norm_ffn2": f["g_ffn_2"],
        "norm_out": f["norm_out"], "g_final": f["g_final_2"],
        "conv0": f["ffn_conv"][0], "conv1": f["ffn_conv"][1],
        "conv_b0": f["ffn_conv_b"][0], "conv_b1": f["ffn_conv_b"][1], "dn_conv": f["dn_conv_2"],
        "subln": f["a_subln"], "dn_norm": f["dn_norm_g_2"], "hg_norm": f["hg_norm_g_2"],
    }
    line = {
        "lam": f["a_lambda"], "a_log": f["dn_a_log_2"], "dt_bias": f["dn_dt_bias_2"],
        "b_router": np.concatenate([f["b_router_grp_2"], f["b_router_exp_2"]], 1), "lb": f["hg_lb_logits_2"],
    }
    c = np.arange(GRID_W)
    dx = c[None, :] - c[:, None] + KW - 1
    inside = (dx >= 0) & (dx < 2 * KW - 1)
    wide = np.concatenate([f["b_rpb"][0], np.zeros((D // HD, 2 * KH - 1, 1), np.float32)], 2)
    bias = wide[:, :, np.where(inside, dx, 2 * KW - 1)]
    out = {k: f[k] for k in ("ada_w", "ffn_up", "ffn_down", "a_wqkv", "a_wo", "b_wqkv", "b_wo",
                             "w_ada_2", "w_in_2", "w_br_dn_2", "w_br_hg_2", "w_out_2",
                             "w_exp_gate_2", "w_exp_up_2", "w_exp_down_2")}
    out["xT"] = np.concatenate([f["x"][0].T, f["ctx"][0].T], 1)
    out["ctx2T"] = f["ctx_2"][0].T
    out["vecs"] = np.concatenate([rows(vec[n]) for n in VECS], 0).T
    out["rows"] = np.tile(np.concatenate([line[n].reshape(-1) for n in ROWS])[None], (P, 1))
    out["bias_rows"] = bias.transpose(0, 2, 1, 3)
    out["w_router"] = np.concatenate([f["w_router_grp_2"][0], f["w_router_exp_2"][0]], 1)
    out["consts"] = constants()
    return {k: np.ascontiguousarray(a) for k, a in out.items()}


def kernel(**inputs):
    import concourse.bacc as bacc
    from concourse.bass_utils import run_bass_kernel_spmd

    nc = bacc.Bacc("TRN2", target_bir_lowering=False, num_devices=1)
    arrays = layout(inputs)
    io = {k: nc.dram_tensor(f"in_{k}", a.shape, mybir.dt.from_np(a.dtype), kind="ExternalInput").ap()
          for k, a in arrays.items()}
    out = nc.dram_tensor("out_x", (D, TX), F32, kind="ExternalOutput").ap()
    program(nc, io, out)
    r = run_bass_kernel_spmd(nc, [{f"in_{k}": a for k, a in arrays.items()}], core_ids=[0])
    return np.ascontiguousarray(r.results[0]["out_x"].T)[None]
```
